# Optimizing a Trainium2 kernel written in Bass

```python
import jax, jax.numpy as jnp
from jax import lax
import numpy as np

D_MODEL = 1024
BATCH = 1
SEQ = 1024
DEPTH = 1

D_MIX = D_MODEL
D_RWKV = D_MIX // 2
D_CONV = D_MIX - D_RWKV
HEAD_DIM = 64
N_RWKV_HEADS = D_RWKV // HEAD_DIM
N_CONV_GROUPS = D_CONV // HEAD_DIM
W_LORA = 32
A_LORA = 32
V_LORA = 32
G_LORA = 96
CONV_WIDTH = 31
FFN_CONV_WIDTH = 3
D_FF = 2816
GLU_COLS = 2 * D_CONV
RWKV_COLS = 3 * D_RWKV + W_LORA + A_LORA + G_LORA
COLS_FIRST = GLU_COLS + RWKV_COLS
COLS_REST = COLS_FIRST + V_LORA
RMS_EPS = 1e-6
LN_EPS = 1e-5
GN_EPS = 64e-5


def _rms_norm(x, g):
    xf = x.astype(jnp.float32)
    y = xf * lax.rsqrt(jnp.mean(xf * xf, axis=-1, keepdims=True) + RMS_EPS)
    return (y * g.astype(jnp.float32)).astype(x.dtype)

def _layer_norm(x, g, b):
    xf = x.astype(jnp.float32)
    mu = jnp.mean(xf, axis=-1, keepdims=True)
    var = jnp.mean(jnp.square(xf - mu), axis=-1, keepdims=True)
    y = (xf - mu) * lax.rsqrt(var + LN_EPS)
    return (y * g.astype(jnp.float32) + b.astype(jnp.float32)).astype(x.dtype)

def _token_shift(p):
    return jnp.pad(p, ((0, 0), (1, 0), (0, 0)))[:, :-1]

def _causal_dwconv(x, w, b):
    K = w.shape[0]
    y = lax.conv_general_dilated(
        x, w[:, None, :].astype(x.dtype), window_strides=(1,), padding=((K - 1, 0),),
        dimension_numbers=("NWC", "WIO", "NWC"), feature_group_count=x.shape[-1])
    return y + b.astype(x.dtype)

def _wkv7(r, decay, k, v, a_vec, b_vec):
    B, T, H, N = r.shape

    def step(S, inp):
        r_t, w_t, k_t, v_t, a_t, b_t = inp
        sa = jnp.einsum("bhvk,bhk->bhv", S, a_t)
        S = S * w_t[:, :, None, :] + sa[..., None] * b_t[:, :, None, :] + v_t[..., None] * k_t[:, :, None, :]
        y = jnp.einsum("bhvk,bhk->bhv", S, r_t)
        return S, y

    xs = tuple(jnp.moveaxis(t.astype(jnp.float32), 1, 0) for t in (r, decay, k, v, a_vec, b_vec))
    S0 = jnp.zeros((B, H, N, N), jnp.float32)
    _, ys = lax.scan(step, S0, xs)
    return jnp.moveaxis(ys, 0, 1)

def _head_group_norm(y, g, b):
    B, T, H, N = y.shape
    mu = jnp.mean(y, axis=-1, keepdims=True)
    var = jnp.mean(jnp.square(y - mu), axis=-1, keepdims=True)
    y = ((y - mu) * lax.rsqrt(var + GN_EPS)).reshape(B, T, H * N)
    return y * g.astype(jnp.float32) + b.astype(jnp.float32)

def _hybrid_mixer(h, w_in, mu, vres_v0, vres_up, v_first, decay_w0, decay_up, iclr_a0, iclr_up,
                  gate_up, k_k, k_a, r_k, lnx_g, lnx_b, cconv_w, cconv_b, cln_g, cln_b, w_out):
    B, T, _ = h.shape
    H, N = N_RWKV_HEADS, HEAD_DIM
    p = h @ w_in.astype(h.dtype)
    u = p[..., :GLU_COLS]
    q = p[..., GLU_COLS:]
    q = q + (_token_shift(q) - q) * mu.astype(h.dtype)
    o1, o2, o3 = D_RWKV, 2 * D_RWKV, 3 * D_RWKV
    o4, o5, o6 = o3 + W_LORA, o3 + W_LORA + A_LORA, RWKV_COLS
    r, k, v = q[..., :o1], q[..., o1:o2], q[..., o2:o3]
    wd, ad, gd = q[..., o3:o4], q[..., o4:o5], q[..., o5:o6]

    wf = (decay_w0 + jnp.tanh(wd) @ decay_up).astype(jnp.float32)
    decay = jnp.exp(-jnp.exp(-jax.nn.softplus(-wf) - 0.5))
    if v_first is None:
        v_first = v
    else:
        vd = q[..., o6:]
        v = v + (v_first - v) * jax.nn.sigmoid(vres_v0 + vd @ vres_up)
    a = jax.nn.sigmoid(iclr_a0 + ad @ iclr_up)
    g = jax.nn.sigmoid(gd) @ gate_up
    kk = (k * k_k).reshape(B, T, H, N).astype(jnp.float32)
    kk = kk * lax.rsqrt(jnp.maximum(jnp.sum(kk * kk, axis=-1, keepdims=True), 1e-24))
    k = k * (1 + (a - 1) * k_a)
    r_h = r.reshape(B, T, H, N)
    k_h = k.reshape(B, T, H, N)
    v_h = v.reshape(B, T, H, N)
    a_h = a.reshape(B, T, H, N).astype(jnp.float32)
    y = _wkv7(r_h, decay.reshape(B, T, H, N), k_h, v_h, -kk, kk * a_h)
    y = _head_group_norm(y, lnx_g, lnx_b).astype(h.dtype)
    bonus = jnp.sum(r_h * k_h * r_k.astype(h.dtype), axis=-1, keepdims=True) * v_h
    rwkv_out = (y + bonus.reshape(B, T, D_RWKV)) * g

    c = u[..., :D_CONV] * jax.nn.sigmoid(u[..., D_CONV:])
    c = _causal_dwconv(c, cconv_w, cconv_b)
    c = jax.nn.silu(_layer_norm(c, cln_g, cln_b))

    mix = jnp.concatenate([rwkv_out, c], axis=-1) @ w_out.astype(h.dtype)
    return mix, v_first

def _conv_ffn(h, ffn_up, ffn_conv_w, ffn_conv_b, ffn_down):
    hid = h @ ffn_up.astype(h.dtype)
    hid = _causal_dwconv(hid, ffn_conv_w, ffn_conv_b)
    gate, up = hid[..., :D_FF], hid[..., D_FF:]
    return (jax.nn.gelu(gate, approximate=True) * up) @ ffn_down.astype(h.dtype)

def first_inputs(seed: int = 0) -> dict:
    key = jax.random.key(seed)
    ks = iter(jax.random.split(key, 40))
    f32 = jnp.float32

    def nrm(shape, scale):
        return jax.random.normal(next(ks), shape, f32) * scale

    def unif(shape, lo, hi):
        return jax.random.uniform(next(ks), shape, f32, lo, hi)

    L, Lr = DEPTH, DEPTH - 1
    return {
        "x": nrm((BATCH, SEQ, D_MODEL), 1.0),
        "w_in_first": nrm((D_MODEL, COLS_FIRST), D_MODEL ** -0.5),
        "mu_first": unif((RWKV_COLS,), 0.0, 1.0),
        "w_in_rest": nrm((Lr, D_MODEL, COLS_REST), D_MODEL ** -0.5),
        "mu_rest": unif((Lr, RWKV_COLS + V_LORA), 0.0, 1.0),
        "vres_v0": nrm((Lr, D_RWKV), 0.5),
        "vres_up": nrm((Lr, V_LORA, D_RWKV), 0.1),
        "decay_w0": unif((L, D_RWKV), -6.0, 1.0),
        "decay_up": nrm((L, W_LORA, D_RWKV), 0.1),
        "iclr_a0": nrm((L, D_RWKV), 0.5),
        "iclr_up": nrm((L, A_LORA, D_RWKV), 0.1),
        "gate_up": nrm((L, G_LORA, D_RWKV), G_LORA ** -0.5),
        "k_k": 0.85 + nrm((L, D_RWKV), 0.05),
        "k_a": 1.0 + nrm((L, D_RWKV), 0.05),
        "r_k": nrm((L, N_RWKV_HEADS, HEAD_DIM), 0.1),
        "lnx_g": 1.0 + nrm((L, D_RWKV), 0.05),
        "lnx_b": nrm((L, D_RWKV), 0.01),
        "cconv_w": nrm((L, CONV_WIDTH, D_CONV), CONV_WIDTH ** -0.5),
        "cconv_b": nrm((L, D_CONV), 0.01),
        "cln_g": 1.0 + nrm((L, D_CONV), 0.05),
        "cln_b": nrm((L, D_CONV), 0.01),
        "w_out": nrm((L, D_MIX, D_MODEL), D_MIX ** -0.5),
        "norm_pre_mix": 1.0 + nrm((L, D_MODEL), 0.05),
        "norm_post_mix": 1.0 + nrm((L, D_MODEL), 0.05),
        "norm_pre_ffn": 1.0 + nrm((L, D_MODEL), 0.05),
        "norm_post_ffn": 1.0 + nrm((L, D_MODEL), 0.05),
        "ffn_up": nrm((L, D_MODEL, 2 * D_FF), D_MODEL ** -0.5),
        "ffn_conv_w": nrm((L, FFN_CONV_WIDTH, 2 * D_FF), FFN_CONV_WIDTH ** -0.5),
        "ffn_conv_b": nrm((L, 2 * D_FF), 0.01),
        "ffn_down": nrm((L, D_FF, D_MODEL), D_FF ** -0.5),
    }

def first_block(x, w_in_first, mu_first, w_in_rest, mu_rest, vres_v0, vres_up, decay_w0, decay_up,
              iclr_a0, iclr_up, gate_up, k_k, k_a, r_k, lnx_g, lnx_b, cconv_w, cconv_b, cln_g, cln_b,
              w_out, norm_pre_mix, norm_post_mix, norm_pre_ffn, norm_post_ffn, ffn_up, ffn_conv_w,
              ffn_conv_b, ffn_down):
    v_first = None
    for i in range(DEPTH):
        if i == 0:
            w_in_i, mu_i, v0_i, vup_i = w_in_first, mu_first, None, None
        else:
            w_in_i, mu_i, v0_i, vup_i = w_in_rest[i - 1], mu_rest[i - 1], vres_v0[i - 1], vres_up[i - 1]
        h = _rms_norm(x, norm_pre_mix[i])
        mix, v_first = _hybrid_mixer(
            h, w_in_i, mu_i, v0_i, vup_i, v_first, decay_w0[i], decay_up[i], iclr_a0[i], iclr_up[i],
            gate_up[i], k_k[i], k_a[i], r_k[i], lnx_g[i], lnx_b[i], cconv_w[i], cconv_b[i],
            cln_g[i], cln_b[i], w_out[i])
        x = x + _rms_norm(mix, norm_post_mix[i])
        h = _rms_norm(x, norm_pre_ffn[i])
        f = _conv_ffn(h, ffn_up[i], ffn_conv_w[i], ffn_conv_b[i], ffn_down[i])
        x = x + _rms_norm(f, norm_post_ffn[i])
    return x


CHUNK = 64
N_META = 16
PAD = CHUNK - N_META
A_KDIM = 128
A_HEADS = D_MODEL // A_KDIM
A_FDIM = A_HEADS * A_KDIM
A_WIDTH = D_MODEL // 2
A_VDIM = A_WIDTH // A_HEADS
POOL_WINDOWS = (2, 4, 8, 16)
B_GROUPS = 4
B_WIDTH = D_MODEL // 2
B_GDIM = B_WIDTH // B_GROUPS
N_BRANCH = 2
SPLITS = (A_FDIM, 2 * A_FDIM, 2 * A_FDIM + A_WIDTH, 2 * A_FDIM + 2 * A_WIDTH,
          2 * A_FDIM + 2 * A_WIDTH + B_WIDTH, 2 * A_FDIM + 2 * A_WIDTH + B_WIDTH + D_MODEL)
IN_COLS = 2 * A_FDIM + 2 * A_WIDTH + B_WIDTH + N_BRANCH * D_MODEL
D_FF_2 = ((8 * D_MODEL // 3 + 127) // 128) * 128
CONV_W = 3
EPS = 1e-6


def rmsnorm(x, g):
    xf = x.astype(jnp.float32)
    y = xf * lax.rsqrt(jnp.mean(xf * xf, axis=-1, keepdims=True) + EPS)
    return (y * g.astype(jnp.float32)).astype(x.dtype)

def hgrn2_mixer(q, f_logit, i, og, lb, head_g):
    dt = i.dtype
    f32 = jnp.float32
    B_, T, _ = q.shape
    n_chunks = (T + PAD) // CHUNK
    lbf = lb.astype(f32)
    f = lbf + (1.0 - lbf) * jax.nn.sigmoid(f_logit.astype(f32))
    k = 1.0 - f
    logf = jnp.log(f)
    qf = jax.nn.silu(q.astype(f32))
    vf = i.astype(f32)

    def to_chunks(t, d):
        t = jnp.pad(t, ((0, 0), (PAD, 0), (0, 0)))
        return t.reshape(B_, n_chunks, CHUNK, A_HEADS, d).transpose(1, 0, 3, 2, 4)

    qc = to_chunks(qf, A_KDIM)
    kc = to_chunks(k, A_KDIM)
    vc = to_chunks(vf, A_VDIM)
    ac = jnp.cumsum(to_chunks(logf, A_KDIM), axis=3)
    causal = jnp.tril(jnp.ones((CHUNK, CHUNK), dtype=bool))[:, :, None]

    def step(S, inp):
        q_, k_, v_, a_ = inp
        o_inter = jnp.einsum('bhtk,bhkv->bhtv', q_ * jnp.exp(a_), S)
        diff = a_[:, :, :, None, :] - a_[:, :, None, :, :]
        decay = jnp.exp(jnp.where(causal, diff, -jnp.inf))
        scores = jnp.einsum('bhtsk,bhsk->bhts', q_[:, :, :, None, :] * decay, k_)
        o = o_inter + jnp.einsum('bhts,bhsv->bhtv', scores, v_)
        a_last = a_[:, :, -1:, :]
        S = jnp.exp(a_last[:, :, 0, :])[..., None] * S + jnp.einsum(
            'bhsk,bhsv->bhkv', k_ * jnp.exp(a_last - a_), v_)
        return S, o

    S0 = jnp.zeros((B_, A_HEADS, A_KDIM, A_VDIM), f32)
    _, o = lax.scan(step, S0, (qc, kc, vc, ac))
    o = o.transpose(1, 0, 3, 2, 4).reshape(B_, n_chunks * CHUNK, A_HEADS, A_VDIM)[:, PAD:]
    o = o * lax.rsqrt(jnp.mean(o * o, axis=-1, keepdims=True) + EPS)
    o = o * head_g.astype(f32).reshape(A_HEADS, A_VDIM)
    o = o.reshape(B_, T, A_WIDTH) * jax.nn.silu(og.astype(f32))
    return o.astype(dt)

def pool_mixer(p, w_group, scale):
    dt = p.dtype
    B_, T, _ = p.shape
    pf = p.astype(jnp.float32).reshape(B_, T, B_GROUPS, B_GDIM)
    cs = jnp.cumsum(pf, axis=1)
    pos = jnp.arange(1, T + 1, dtype=jnp.float32)
    outs = []
    for gi, w in enumerate(POOL_WINDOWS):
        c = cs[:, :, gi]
        lag = jnp.pad(c[:, :-w], ((0, 0), (w, 0), (0, 0)))
        mean = (c - lag) / jnp.minimum(pos, float(w))[None, :, None]
        outs.append(mean - pf[:, :, gi])
    d = jnp.stack(outs, axis=2)
    y = jnp.einsum('btgc,gcd->btgd', d, w_group.astype(jnp.float32)).reshape(B_, T, B_WIDTH)
    return (y * scale.astype(jnp.float32)).astype(dt)

def causal_dwconv(u, w, b):
    C = u.shape[-1]
    up = jnp.pad(u, ((0, 0), (CONV_W - 1, 0), (0, 0)))
    y = lax.conv_general_dilated(up, w[:, None, :].astype(u.dtype), window_strides=(1,), padding='VALID',
                                 dimension_numbers=('NWC', 'WIO', 'NWC'), feature_group_count=C)
    return y + b

def second_inputs(seed: int = 0) -> dict:
    key = jax.random.key(seed)
    ks = jax.random.split(key, 20)
    f32 = jnp.float32
    nrm = lambda k, shape, s: jax.random.normal(k, shape, f32) * s
    L = DEPTH
    return {
        "x": nrm(ks[0], (BATCH, SEQ, D_MODEL), 1.0),
        "meta_tokens": nrm(ks[1], (N_META, D_MODEL), 1.0),
        "lb_logits": nrm(ks[2], (DEPTH + 1, A_FDIM), 1.0),
        "norm1_g": 1.0 + nrm(ks[3], (L, D_MODEL), 0.05),
        "w_in": nrm(ks[4], (L, D_MODEL, IN_COLS), D_MODEL ** -0.5),
        "b_f": nrm(ks[5], (L, A_FDIM), 0.1),
        "head_norm_g": 1.0 + nrm(ks[6], (L, A_WIDTH), 0.05),
        "w_pool": nrm(ks[7], (L, B_GROUPS, B_GDIM, B_GDIM), B_GDIM ** -0.5),
        "pool_scale": 1.0 + nrm(ks[8], (L, B_WIDTH), 0.1),
        "w_branch_a": nrm(ks[9], (L, A_WIDTH, D_MODEL), A_WIDTH ** -0.5),
        "w_branch_b": nrm(ks[10], (L, B_WIDTH, D_MODEL), B_WIDTH ** -0.5),
        "w_out": nrm(ks[11], (L, D_MODEL, D_MODEL), D_MODEL ** -0.5),
        "norm2_g": 1.0 + nrm(ks[12], (L, D_MODEL), 0.05),
        "w_up": nrm(ks[13], (L, D_MODEL, 2 * D_FF_2), D_MODEL ** -0.5),
        "conv_w": nrm(ks[14], (L, CONV_W, D_FF_2), CONV_W ** -0.5),
        "conv_b": nrm(ks[15], (L, D_FF_2), 0.01),
        "w_down": nrm(ks[16], (L, D_FF_2, D_MODEL), D_FF_2 ** -0.5),
        "final_norm_g": 1.0 + nrm(ks[17], (D_MODEL,), 0.05),
    }

def second_block(x, meta_tokens, lb_logits, norm1_g, w_in, b_f, head_norm_g, w_pool, pool_scale,
              w_branch_a, w_branch_b, w_out, norm2_g, w_up, conv_w, conv_b, w_down, final_norm_g):
    B_ = x.shape[0]
    meta = jnp.broadcast_to(meta_tokens.astype(x.dtype)[None], (B_, N_META, D_MODEL))
    h = jnp.concatenate([meta, x], axis=1)
    lb_all = jnp.cumsum(jax.nn.softmax(lb_logits.astype(jnp.float32), axis=0), axis=0)
    for l in range(DEPTH):
        z = rmsnorm(h, norm1_g[l])
        proj = z @ w_in[l]
        q, fl, iv, og, pin, ga, gb = jnp.split(proj, SPLITS, axis=-1)
        o_a = hgrn2_mixer(q, fl + b_f[l], iv, og, lb_all[l], head_norm_g[l])
        o_b = pool_mixer(pin, w_pool[l], pool_scale[l])
        mix = jax.nn.sigmoid(ga) * (o_a @ w_branch_a[l]) + jax.nn.sigmoid(gb) * (o_b @ w_branch_b[l])
        h = h + mix @ w_out[l]
        z = rmsnorm(h, norm2_g[l])
        u, v = jnp.split(z @ w_up[l], 2, axis=-1)
        u = causal_dwconv(u, conv_w[l], conv_b[l])
        h = h + (jax.nn.silu(u) * v) @ w_down[l]
    h = rmsnorm(h, final_norm_g)
    return h[:, N_META:]


def setup_inputs(seed=0):
    out = dict(first_inputs(seed))
    for name, value in second_inputs(seed + 1).items():
        if name != "x":
            out[name + "_2"] = value
    return out


def reference(
    x, w_in_first, mu_first, w_in_rest, mu_rest, vres_v0, vres_up, decay_w0, decay_up, iclr_a0,
    iclr_up, gate_up, k_k, k_a, r_k, lnx_g, lnx_b, cconv_w, cconv_b, cln_g, cln_b, w_out,
    norm_pre_mix, norm_post_mix, norm_pre_ffn, norm_post_ffn, ffn_up, ffn_conv_w, ffn_conv_b,
    ffn_down, meta_tokens_2, lb_logits_2, norm1_g_2, w_in_2, b_f_2, head_norm_g_2, w_pool_2,
    pool_scale_2, w_branch_a_2, w_branch_b_2, w_out_2, norm2_g_2, w_up_2, conv_w_2, conv_b_2,
    w_down_2, final_norm_g_2,
):
    x = first_block(
        x, w_in_first, mu_first, w_in_rest, mu_rest, vres_v0, vres_up, decay_w0, decay_up,
        iclr_a0, iclr_up, gate_up, k_k, k_a, r_k, lnx_g, lnx_b, cconv_w, cconv_b, cln_g, cln_b,
        w_out, norm_pre_mix, norm_post_mix, norm_pre_ffn, norm_post_ffn, ffn_up, ffn_conv_w,
        ffn_conv_b, ffn_down,
    )
    return second_block(
        x, meta_tokens_2, lb_logits_2, norm1_g_2, w_in_2, b_f_2, head_norm_g_2, w_pool_2,
        pool_scale_2, w_branch_a_2, w_branch_b_2, w_out_2, norm2_g_2, w_up_2, conv_w_2,
        conv_b_2, w_down_2, final_norm_g_2,
    )


_drawn_inputs = setup_inputs


def setup_inputs(seed=0):
    import zlib

    import numpy as np

    out = dict(_drawn_inputs(seed))
    spreads = {}
    factors = {'decay_up': 3.453,
     'lnx_b': 8.0,
     'cconv_b': 4.359,
     'cln_b': 8.0,
     'ffn_conv_b': 6.46,
     'meta_tokens_2': 4.113,
     'lb_logits_2': 3.359,
     'norm1_g_2': 2.817,
     'b_f_2': 8.0,
     'head_norm_g_2': 5.998,
     'conv_b_2': 64.0,
     'pool_scale_2': 2.812,
     'norm2_g_2': 8.0}
    for name, (base, spread) in spreads.items():
        noise = np.random.default_rng([zlib.crc32(name.encode()), seed]).standard_normal(out[name].shape)
        drawn = base * np.exp(spread * noise) if base else spread * noise
        out[name] = __import__('jax').numpy.asarray(drawn.astype(out[name].dtype))
    for name, factor in factors.items():
        out[name] = (out[name] * factor).astype(out[name].dtype)
    return out
```

```python
from contextlib import ExitStack

import concourse.bass as bass
from concourse import mybir
import numpy as np

ALU = mybir.AluOpType
ACT = mybir.ActivationFunctionType
AX = mybir.AxisListType
F32 = mybir.dt.float32
F32R = mybir.dt.float32r

P = 128
T = 1024
D = 1024
KD = D // P
NT = T // P
META = 16
T2 = T + META
H = 8
N = 64
C1 = 64
NC1 = T // C1
PAIRS = H // 2
DR = H * N
F1 = 2816
CONVW = 31
RMS_EPS = 1e-6

PARAMS = [("mu_first", 12), ("decay_w0", 4), ("iclr_a0", 4), ("k_k", 4), ("k_a", 4), ("r_k", 4),
          ("lnx_g", 4), ("lnx_b", 4), ("cconv_b", 4), ("cln_g", 4), ("cln_b", 4),
          ("lb_logits_2", 16), ("b_f_2", 8), ("head_norm_g_2", 4), ("pool_scale_2", 4), ("ffn_conv_b", 44),
          ("cconv_w", 124),
          ("ffn_conv_w", 132),
          ("conv_w_2", 66), ("conv_b_2", 22)]


def param_rows():
    pieces, first, row = [], {}, 0
    for name, rows in PARAMS:
        first[name] = row
        done = 0
        while done < rows:
            k = min(rows - done, P - row % P)
            pieces.append((name, done, k, row // P, row % P))
            row += k
            done += k
    return pieces, first, row


PIECES, FIRST, ROWS = param_rows()
ROW_TILES = -(-ROWS // P)


def shape_constants():
    p, out = np.arange(P), {}
    out["ident"] = np.eye(P)
    out["head_ones"] = (p[:, None] // N == p[None, :] // N).astype(float)
    out["head_sel"] = (p[:, None] // N == np.arange(2)[None, :]).astype(float)
    s, t = (p % C1)[:, None], np.arange(C1)[None, :]
    out["eye"] = (s == t).astype(float)
    out["before"] = (s < t).astype(float)
    out["upto"] = (s <= t).astype(float)
    out["levels"] = np.concatenate(
        [((s >> l) + 1 == (t >> l)) & ((s >> l) % 2 == 0) for l in range(6)], axis=1).astype(float)
    s, t = p[:, None], p[None, :]
    out["levels2"] = np.concatenate(
        [s == t] + [((s >> l) + 1 == (t >> l)) & ((s >> l) % 2 == 0) for l in range(7)], axis=1).astype(float)
    out["chunk_run"] = np.broadcast_to((np.arange(T) % C1 != 0).astype(float), (P, T))
    out["tile_run"] = np.broadcast_to((np.arange(T2) % P != 0).astype(float), (P, T2))
    windows = np.array([2, 4, 8, 16])[:, None]
    rate = windows / np.minimum(np.arange(1, 17)[None, :], windows)
    out["pool_rate"] = np.broadcast_to(rate.reshape(1, 64), (P, 64))
    at, first = 0, {}
    for name, a in out.items():
        first[name] = (at, a.shape[1])
        at += a.shape[1]
    return np.ascontiguousarray(np.concatenate(list(out.values()), axis=1).astype(np.float32)), first


CONSTS, CONST_AT = shape_constants()


class Made:

    def __init__(self, sem, names):
        self.sem, self.names, self.turn, self.next = sem, list(names), len(names), 0

    def start(self, eng):
        eng.sem_inc(self.sem, self.turn)

    def skip(self, eng, j, n):
        eng.wait_ge(self.sem, (j + 1) * self.turn + self.next)
        eng.sem_inc(self.sem, n)
        self.next = (self.next + n) % self.turn

    def by(self, instruction, name):
        assert self.names[self.next] == name, (self.names[self.next], name)
        self.next = (self.next + 1) % self.turn
        instruction.then_inc(self.sem, 1)

    def wait(self, eng, j, name, back=0):
        eng.wait_ge(self.sem, (j + 1 - back) * self.turn + self.names.index(name) + 1)


class Scope:

    used = []

    def __init__(self, nc, tag):
        self.nc, self.tag, self.ctx = nc, tag, ExitStack()

    def __enter__(self):
        return self

    def __exit__(self, *a):
        return self.ctx.__exit__(*a)

    def sb(self, name, shape, dt=F32):
        return self.ctx.enter_context(self.nc.sbuf_tensor(f"{self.tag}_{name}", shape, dt))

    def ps(self, name, shape, dt=F32):
        return self.ctx.enter_context(self.nc.psum_tensor(f"{self.tag}_{name}", shape, dt))

    def sem(self, name):
        handle = self.nc.alloc_semaphore(f"{self.tag}_{name}")
        self.used.append(handle)
        return handle

    def block(self):
        return self.ctx.enter_context(self.nc.Block())


def clear_semaphores(nc):
    nc.clear_and_free_semaphores(Scope.used)
    Scope.used = []
    nc.all_engine_barrier()


def const_of(consts, name):
    at, n = CONST_AT[name]
    return consts[:, at:at + n]


def load_parameters(nc, ins, consts, table, ident):
    with Scope(nc, "par") as s:
        rows = s.sb("rows", [P, ROW_TILES, P])
        turned = s.ps("turned", [P, ROW_TILES, P])
        landed = s.sem("landed")
        ident_landed = s.sem("ident_landed")
        turned_ready = s.sem("turned_ready")
        block = s.block()

        @block.sync
        def _(sp):
            sp.dma_start(ident[:], const_of(consts, "ident")).then_inc(ident_landed, 16)
            for name, r0, k, tile, at in PIECES:
                v = ins[name]
                letters = "abcd"[:len(v.shape)]
                flat = v.rearrange(f"{' '.join(letters)} -> ({' '.join(letters)})").rearrange("(r p) -> r p", p=P) \
                    if len(v.shape) > 1 else v[0:(v.shape[0] // P) * P].rearrange("(r p) -> r p", p=P)
                sp.dma_start(rows[at:at + k, tile, :], flat[r0:r0 + k, :]).then_inc(landed, 16)

        @block.tensor
        def _(pe):
            pe.wait_ge(ident_landed, 16)
            pe.wait_ge(landed, 16 * len(PIECES))
            for tile in range(ROW_TILES):
                k = min(P, ROWS - tile * P)
                mm = nc.tensor.transpose(turned[:, tile, 0:k], rows[0:k, tile, :], ident[0:k, 0:k])
            mm.then_inc(turned_ready, 1)

        @block.vector
        def _(dve):
            dve.wait_ge(turned_ready, 1)
            nc.vector.tensor_copy(table[:, 0:ROWS], turned[:].rearrange("p a b -> p (a b)")[:, 0:ROWS])


def norm_to_features(nc, tag, x, gain, hi, lo, ident, meta=None):
    first_col = META if meta is not None else 0
    with Scope(nc, tag) as s:
        gains = s.sb("gains", [P, D])
        squares = s.sb("squares", [P, D])
        sums = s.sb("sums", [P, NT + 1])
        stds = s.sb("stds", [P, NT + 1])
        rstds = s.sb("rstds", [P, NT + 1])
        eps = s.sb("eps", [P, 1])
        normed = s.sb("normed", [P, 2, D])
        turned = [s.ps(f"turned{i}", [P, KD, P]) for i in range(2)]
        gains_landed = s.sem("gains_landed")
        eps_ready = s.sem("eps_ready")
        sums_ready = s.sem("sums_ready")
        std_ready = s.sem("std_ready")
        rstd_ready = s.sem("rstd_ready")
        normed_ready = s.sem("normed_ready")
        turned_ready = s.sem("turned_ready")
        hi_ready = s.sem("hi_ready")
        lo_ready = s.sem("lo_ready")
        block = s.block()

        @block.sync
        def _(sp):
            sp.dma_start(gains[:], gain.broadcast_to((P, D))).then_inc(gains_landed, 16)

        @block.scalar
        def _(act):
            def statistics(n, src, p, col):
                nc.scalar.activation(squares[0:p, :], src, ACT.Square,
                                     accum_out=sums[0:p, col]).then_inc(sums_ready, 1)
                act.wait_ge(sums_ready, n + 1)
                nc.scalar.activation(stds[0:p, col], sums[0:p, col], ACT.Sqrt, scale=1.0 / D,
                                     bias=eps[0:p, :]).then_inc(std_ready, 1)

            def split(n, slot, p, cols):
                act.wait_ge(turned_ready, n + 1)
                nc.scalar.activation(hi[:, :, cols], turned[slot][:, :, 0:p], ACT.Copy).then_inc(hi_ready, 1)

            act.wait_ge(eps_ready, 1)
            with act.Fori(0, NT // 2) as i:
                for e in range(2):
                    statistics(2 * i + e, x[:, bass.ds(2 * i + e, 1), :], P, bass.ds(2 * i + e, 1))
            if meta is not None:
                statistics(NT, meta[:, :], META, slice(NT, NT + 1))
            with act.Fori(0, NT // 2) as i:
                for e in range(2):
                    split(2 * i + e, e, P, bass.ds((2 * i + e) * P + first_col, P))
            if meta is not None:
                split(NT, 0, META, slice(0, META))

        @block.vector
        def _(dve):
            def normalise(n, src, slot, p, col):
                dve.wait_ge(std_ready, n + 1)
                nc.vector.reciprocal(rstds[0:p, col], stds[0:p, col]).then_inc(rstd_ready, 1)
                dve.wait_ge(rstd_ready, n + 1)
                nc.vector.scalar_tensor_tensor(normed[0:p, slot, :], src, rstds[0:p, col], gains[0:p, :],
                                               ALU.mult, ALU.mult).then_inc(normed_ready, 1)

            def split(n, slot, p, cols):
                dve.wait_ge(hi_ready, n + 1)
                nc.vector.tensor_tensor(lo[:, :, cols], turned[slot][:, :, 0:p], hi[:, :, cols].bitcast(F32),
                                        ALU.subtract).then_inc(lo_ready, 1)

            nc.vector.memset(eps[:], RMS_EPS).then_inc(eps_ready, 1)
            dve.wait_ge(gains_landed, 16)
            normalise(0, x[:, 0, :], 0, P, slice(0, 1))
            normalise(1, x[:, 1, :], 1, P, slice(1, 2))
            with dve.Fori(0, NT // 2 - 1) as i:
                for e in range(2):
                    split(2 * i + e, e, P, bass.ds((2 * i + e) * P + first_col, P))
                    normalise(2 * i + e + 2, x[:, bass.ds(2 * i + e + 2, 1), :], e, P, bass.ds(2 * i + e + 2, 1))
            split(NT - 2, 0, P, slice((NT - 2) * P + first_col, (NT - 1) * P + first_col))
            if meta is not None:
                normalise(NT, meta[:, :], 0, META, slice(NT, NT + 1))
            split(NT - 1, 1, P, slice((NT - 1) * P + first_col, NT * P + first_col))
            if meta is not None:
                split(NT, 0, META, slice(0, META))

        @block.tensor
        def _(pe):
            def turn(n, slot, p):
                pe.wait_ge(normed_ready, n + 1)
                for f in range(KD):
                    mm = nc.tensor.transpose(turned[slot][:, f, 0:p], normed[0:p, slot, f * P:(f + 1) * P],
                                             ident[0:p, 0:p])
                mm.then_inc(turned_ready, 1)

            turn(0, 0, P)
            turn(1, 1, P)
            with pe.Fori(0, NT // 2 - 1) as i:
                for e in range(2):
                    pe.wait_ge(lo_ready, 2 * i + e + 1)
                    turn(2 * i + e + 2, e, P)
            if meta is not None:
                pe.wait_ge(lo_ready, NT - 1)
                turn(NT, 0, META)


class Stream:

    def __init__(self, s):
        self.raw = s.sb("w_raw", [P, 2, KD, P])
        self.hi = s.sb("w_hi", [P, 2, KD, P], F32R)
        self.lo = s.sb("w_lo", [P, 2, KD, P], F32R)
        self.landed = [s.sem(f"w_landed{e}") for e in range(2)]
        self.hi_ready = s.sem("w_hi_ready")
        self.lo_ready = s.sem("w_lo_ready")
        self.product_ready = s.sem("product_ready")
        self.psum_free = s.sem("psum_free")
        self.cleared = s.sem("cleared")

    def load(self, sp, n, slot, src, first=False):
        if not first:
            sp.wait_ge(self.lo_ready, n - 1)
            sp.sem_inc(self.cleared, 1)
        m = src.shape[1]
        sp.dma_start(self.raw[:, slot, :, 0:m], src.rearrange("(k p) m -> p k m", p=P)).then_inc(
            self.landed[slot], 16)

    def split_hi(self, nc, act, n, turn, slot, m=P, first=False):
        act.wait_ge(self.landed[slot], 16 * (turn + 1))
        if not first:
            act.wait_ge(self.product_ready, n - 1)
        nc.scalar.activation(self.hi[:, slot, :, 0:m], self.raw[:, slot, :, 0:m], ACT.Copy).then_inc(
            self.hi_ready, 1)

    def split_lo(self, nc, pool, n, slot, m=P):
        pool.wait_ge(self.hi_ready, n + 1)
        nc.gpsimd.tensor_tensor(self.lo[:, slot, :, 0:m], self.raw[:, slot, :, 0:m],
                                self.hi[:, slot, :, 0:m], ALU.subtract).then_inc(self.lo_ready, 1)

    def product(self, nc, pe, n, slot, m, hi, lo, outs, first=False):
        pe.wait_ge(self.lo_ready, n + 1)
        if not first:
            pe.wait_ge(self.psum_free, n - 1)
        for k in range(KD):
            for part, (w, a) in enumerate(((self.hi, hi), (self.hi, lo), (self.lo, hi))):
                for out, c0, c in outs:
                    mm = nc.tensor.matmul(out, w[:, slot, k, 0:m], a[:, k, c0:c0 + c],
                                          start=k == 0 and part == 0, stop=k == KD - 1 and part == 2)
        mm.then_inc(self.product_ready, 1)


def first_projections(nc, ins, table, col_mu, hi, lo, c, rkv, low):
    w = ins["w_in_first"]
    U = 2 * DR
    GLU = 8
    RKV = 12
    steps = GLU + RKV + 2
    with Scope(nc, "proj1") as s:
        st = Stream(s)
        out = [s.ps(f"out{e}", [P, 2, 512]) for e in range(2)]
        gate = s.sb("gate", [P, T])
        shifted = s.sb("shifted", [P, 2, 1 + T])
        keep = s.sb("keep", [P, 14])
        gate_ready = s.sem("gate_ready")
        shifted_ready = s.sem("shifted_ready")
        prepared = s.sem("prepared")
        block = s.block()
        flat = [o[:].rearrange("p a b -> p (a b)") for o in out]

        def cols(c0, n=P):
            return w[:, bass.ds(c0, n)]

        @block.sync
        def _(sp):
            st.load(sp, 0, 0, w[:, DR:DR + P], first=True)
            st.load(sp, 1, 1, w[:, 0:P], first=True)
            with sp.Fori(1, 4) as i:
                st.load(sp, 2 * i, 0, cols(i * P + DR))
                st.load(sp, 2 * i + 1, 1, cols(i * P))
            with sp.Fori(0, RKV // 2) as i:
                for e in range(2):
                    st.load(sp, 2 * i + e + GLU, e, cols((2 * i + e) * P + U))
            st.load(sp, GLU + RKV, 0, w[:, U + 3 * DR:U + 3 * DR + 64])
            st.load(sp, GLU + RKV + 1, 1, w[:, U + 3 * DR + 64:U + 3 * DR + 160])

        @block.gpsimd
        def _(pool):
            with pool.Fori(0, (steps - 2) // 2) as i:
                for e in range(2):
                    st.split_lo(nc, pool, 2 * i + e, e)
            st.split_lo(nc, pool, steps - 2, 0, 64)
            st.split_lo(nc, pool, steps - 1, 1, 96)

        @block.tensor
        def _(pe):
            def step(n, e, m=P, first=False):
                st.product(nc, pe, n, e, m, hi, lo,
                           [(out[e][0:m, h, :], 512 * h, 512) for h in range(2)], first)

            step(0, 0, first=True)
            step(1, 1, first=True)
            with pe.Fori(1, (steps - 2) // 2) as i:
                step(2 * i, 0)
                step(2 * i + 1, 1)
            step(steps - 2, 0, 64)
            step(steps - 1, 1, 96)

        @block.scalar
        def _(act):
            def shift(n, e, mu, m=P):
                act.wait_ge(st.product_ready, n + 1)
                act.wait_ge(st.psum_free, n - 1)
                nc.scalar.activation(shifted[0:m, e, 1:1 + T], flat[e][0:m, :], ACT.Copy,
                                     scale=mu).then_inc(shifted_ready, 1)

            def glu(i, peeled=False):
                act.wait_ge(st.product_ready, 2 * i + 1)
                if not peeled:
                    act.wait_ge(st.psum_free, 2 * i)
                nc.scalar.activation(gate[:], flat[0][:], ACT.Sigmoid).then_inc(gate_ready, 1)

            st.split_hi(nc, act, 0, 0, 0, first=True)
            st.split_hi(nc, act, 1, 0, 1, first=True)
            glu(0, peeled=True)
            st.split_hi(nc, act, 2, 1, 0)
            st.split_hi(nc, act, 3, 1, 1)
            with act.Fori(1, 4) as i:
                glu(i)
                st.split_hi(nc, act, 2 * i + 2, i + 1, 0)
                st.split_hi(nc, act, 2 * i + 3, i + 1, 1)
            act.wait_ge(prepared, 3)
            with act.Fori(0, RKV // 2 - 1) as i:
                for e in range(2):
                    n = 2 * i + e + GLU
                    shift(n, e, table[:, bass.ds(2 * i + e + FIRST["mu_first"], 1)])
                    st.split_hi(nc, act, n + 2, i + GLU // 2 + 1, e)
            n = GLU + RKV - 2
            for e, m in ((0, 64), (1, 96)):
                mu = FIRST["mu_first"] + RKV - 2 + e
                shift(n + e, e, table[:, mu:mu + 1])
                st.split_hi(nc, act, n + e + 2, n // 2 + 1, e, m)
            shift(n + 2, 0, col_mu[0:64, 0:1], 64)
            shift(n + 3, 1, col_mu[0:96, 1:2], 96)

        @block.vector
        def _(dve):
            def shift(n, e, dst, keep_col, m=P):
                dve.wait_ge(shifted_ready, n - GLU + 1)
                nc.vector.scalar_tensor_tensor(dst, flat[e][0:m, :], keep_col, shifted[0:m, e, 0:T],
                                               ALU.mult, ALU.add).then_inc(st.psum_free, 1)

            nc.vector.tensor_scalar(keep[:, 0:12], table[:, FIRST["mu_first"]:FIRST["mu_first"] + 12],
                                    -1.0, 1.0, ALU.mult, ALU.add).then_inc(prepared, 1)
            nc.vector.tensor_scalar(keep[:, 12:14], col_mu[:, :], -1.0, 1.0, ALU.mult,
                                    ALU.add).then_inc(prepared, 1)
            nc.vector.memset(shifted[:, :, 0:1], 0.0).then_inc(prepared, 1)
            nc.vector.memset(c[:, :, 0:CONVW - 1], 0.0)
            dve.wait_ge(prepared, 3)
            with dve.Fori(0, 4) as i:
                dve.wait_ge(gate_ready, i + 1)
                dve.wait_ge(st.product_ready, 2 * i + 2)
                nc.vector.tensor_tensor(c[:, bass.ds(i, 1), CONVW - 1:CONVW - 1 + T], flat[1][:], gate[:],
                                        ALU.mult).then_inc(st.psum_free, 2)
            with dve.Fori(0, RKV // 2) as i:
                for e in range(2):
                    shift(2 * i + e + GLU, e, rkv[:, bass.ds(2 * i + e, 1), :], keep[:, bass.ds(2 * i + e, 1)])
            shift(GLU + RKV, 0, low[0:64, 0, :], keep[0:64, 12:13], 64)
            shift(GLU + RKV + 1, 1, low[0:96, 1, :], keep[0:96, 13:14], 96)


GN_EPS = 64e-5
HALF_E = float(np.exp(-0.5))
BATCH = 8
LEVELS = 6


def recurrence1(nc, ins, consts, table, ident, c, rkv, low, conv):
    act_names = (["sg", "a", "square", "p", "pinv", "pprev", "kk_std", "v"]
                 + [f"{x}t{b}" for x in "vbk" for b in range(2)]
                 + [f"T{l}{b}" for l in range(1, LEVELS) for b in range(2)]
                 + [x for ch in range(NC1) for x in ((f"G{ch}", f"SP{ch}") if ch else (f"G{ch}",))]
                 + ["y", "y_square", "y_std"])
    taps = iter(range(1, CONVW))
    plan = {}

    def tap_names(at, n):
        plan[at] = [t for _, t in zip(range(n), taps)]
        return [f"tap{t}" for t in plan[at]]

    dve_names = ["kkr", "sg_sum", "before_sum", "kat", "kf", "bon", "tap0"] + tap_names("stats", 2)
    dve_names += ["kk_floor", "kk_inv", "kk_wide", "kk", "at", "rt", "b1", "bt", "kt"]
    for q in range(4):
        dve_names += [f"LB{q}", f"LK{q}"]
    for b in range(2):
        dve_names += [f"XT0{b}"]
    for b in range(2):
        dve_names += [f"X0{b}"]
    for l in range(1, LEVELS):
        for b in range(2):
            dve_names += tap_names(f"level{l}{b}", 2)
            dve_names += ([f"X{l}{b}"] if l < LEVELS - 1 else []) + [f"XT{l}{b}"]
    for ch in range(NC1):
        dve_names += [f"U{ch}", f"S{ch}"]
    dve_names += tap_names("tail", 8)
    dve_names += ["yc", "y_inv", "y_wide", "yn", "ynorm", "bonus", "ysum", "gated"]
    assert not list(taps)
    pe_names = ["decay", "iclr", "kk_stats", "kk_scale"]
    pe_names += ["vt0", "vt1"]
    for q in range(4):
        pe_names += [f"LB{q}", f"LK{q}"]
    pe_names += ["bt0", "bt1", "kt0", "kt1", "T00", "T01"]
    for l in range(1, LEVELS):
        for b in range(2):
            pe_names += [f"T{l}{b}"]
        for b in range(2):
            pe_names += [f"X{l}{b}"]
    for ch in range(NC1):
        pe_names += [f"G{ch}", f"U{ch}", f"S{ch}", f"Y{ch}"]
    pe_names += ["mean", "y_stats", "y_scale", "bonus", "gate"]
    pool_names = [f"LM{l}{b}" for l in range(LEVELS) for b in range(2)]

    with Scope(nc, "rec1") as s:
        masks = {}
        for name in ("head_ones", "head_sel", "before", "upto", "levels", "eye", "chunk_run"):
            masks[name] = s.sb(name, [P, CONST_AT[name][1]])
        both = s.sb("both", [P, 2, C1])
        ups = s.sb("ups", [P, 3, P])
        cols = s.sb("cols", [P, 4])
        gn_eps = s.sb("gn_eps", [P, 1])

        def wide(name):
            return s.sb(name, [P, T])

        sg, a, p, pinv, kkr, kk, kf, bon, sq, cumt = map(
            wide, ("sg", "a", "p", "pinv", "kkr", "kk", "kf", "bon", "sq", "cumt"))
        ar = s.sb("ar", [P, NC1, 2, C1])
        b_, k_, v_ = map(wide, ("b", "k", "v"))
        vt, bt, kt = (s.sb(n, [P, NC1, C1]) for n in ("vt", "bt", "kt"))
        lb, lk = (s.sb(n, [P, NC1, 2, C1]) for n in ("lb", "lk"))
        lm, tt, xx, xt = (s.sb(n, [P, 2, BATCH, C1]) for n in ("lm", "tt", "xx", "xt"))
        floor, std, inv = (s.sb(n, [P, 2 * NT]) for n in ("floor", "std", "inv"))
        gs, us = (s.sb(n, [P, N]) for n in ("gs", "us"))
        st = s.sb("st", [P, 2, N])
        sp_ = s.sb("sp", [P, N])

        big = s.ps("big", [P, 2, 512])
        big2 = s.ps("big2", [P, 2, 512])
        w = s.ps("w", [P, 4, 512])
        bigf, big2f = (t[:].rearrange("p a b -> p (a b)") for t in (big, big2))
        consts_landed = s.sem("consts_landed")
        ups_landed = s.sem("ups_landed")
        prepared = s.sem("prepared")
        low_ready = s.sem("low_ready")
        passed = s.sem("passed")
        cleared = s.sem("cleared")
        A = Made(s.sem("scalar_made"), act_names)
        V = Made(s.sem("vector_made"), dve_names)
        M = Made(s.sem("tensor_made"), pe_names)
        G = Made(s.sem("pool_made"), pool_names)
        block = s.block()
        col = lambda name, j: table[:, bass.ds(j + FIRST[name], 1)]
        heads = [slice(0, N), slice(N, P)]

        @block.sync
        def _(sp):
            for name, tile in masks.items():
                sp.dma_start(tile[:], const_of(consts, name)).then_inc(consts_landed, 16)
            with sp.Fori(0, PAIRS) as j:
                M.wait(sp, j, "gate", back=1)
                sp.sem_inc(cleared, 1)
                for n, (name, p0, k) in enumerate((("decay_up", 0, 32), ("iclr_up", 32, 32), ("gate_up", 0, 96))):
                    sp.dma_start(ups[p0:p0 + k, n, :], ins[name][0, :, bass.ds(j * P, P)]).then_inc(ups_landed, 16)

        @block.gpsimd
        def _(pool):
            G.start(pool)
            pool.wait_ge(consts_landed, 16 * len(masks))
            with pool.Fori(0, PAIRS) as j:
                for l in range(LEVELS):
                    for b in range(2):
                        if l == 0:
                            V.wait(pool, j, f"LB{2 * b + 1}")
                        else:
                            M.wait(pool, j, f"T{l - 1}{b}")
                            if l == 1:
                                V.wait(pool, j, f"XT0{b}")
                        mask = masks["levels"][:, l * C1:(l + 1) * C1].unsqueeze(1).broadcast_to((P, BATCH, C1))
                        G.by(nc.gpsimd.tensor_tensor(lm[:, b], lb[:, b * BATCH:(b + 1) * BATCH, 0, :], mask,
                                                     ALU.mult), f"LM{l}{b}")

        @block.scalar
        def _(act):
            A.start(act)
            act.wait_ge(consts_landed, 16 * len(masks))
            nc.scalar.activation(low[0:32, 0, :], low[0:32, 0, :], ACT.Tanh).then_inc(low_ready, 1)
            nc.scalar.activation(low[0:96, 1, :], low[0:96, 1, :], ACT.Sigmoid).then_inc(low_ready, 1)
            act.wait_ge(prepared, 4)
            with act.Fori(0, PAIRS) as j:
                M.wait(act, j, "decay")
                A.by(nc.scalar.activation(sg[:], bigf, ACT.Sigmoid, bias=col("decay_w0", j)), "sg")
                M.wait(act, j, "iclr")
                A.by(nc.scalar.activation(a[:], big2f, ACT.Sigmoid, bias=col("iclr_a0", j)), "a")
                V.wait(act, j, "kkr")
                A.by(nc.scalar.activation(sq[:], kkr[:], ACT.Square), "square")
                V.wait(act, j, "before_sum")
                A.by(nc.scalar.activation(p[:], cumt[:], ACT.Exp, scale=-HALF_E), "p")
                A.by(nc.scalar.activation(pinv[:], cumt[:], ACT.Exp, scale=HALF_E), "pinv")
                A.by(nc.scalar.activation(sg[:], sg[:], ACT.Exp, scale=-HALF_E), "pprev")
                V.wait(act, j, "kk_floor")
                A.by(nc.scalar.activation(std[:], floor[:], ACT.Sqrt), "kk_std")
                A.by(nc.scalar.activation(v_[:], rkv[:, bass.ds(j + 8, 1), :], ACT.Copy), "v")
                for x, dst, bank in (("v", vt, big2), ("b", bt, big), ("k", kt, big2)):
                    for b in range(2):
                        M.wait(act, j, f"{x}t{b}")
                        A.by(nc.scalar.activation(dst[:, b * BATCH:(b + 1) * BATCH, :],
                                                  bank[:, b, :].rearrange("p (c n) -> p c n", n=N), ACT.Copy), f"{x}t{b}")
                for l in range(1, LEVELS):
                    for b in range(2):
                        M.wait(act, j, f"T{l}{b}")
                        A.by(nc.scalar.activation(tt[:, b], w[:, b, :].rearrange("p (c n) -> p c n", n=C1), ACT.Copy),
                             f"T{l}{b}")
                for ch in range(NC1):
                    M.wait(act, j, f"G{ch}")
                    A.by(nc.scalar.activation(gs[:], w[:, 0, 0:N], ACT.Copy), f"G{ch}")
                    if ch:
                        V.wait(act, j, f"S{ch - 1}")
                        A.by(nc.scalar.activation(sp_[:], st[:, ch % 2, :], ACT.Copy,
                                                  scale=p[:, ch * C1 + C1 - 1:ch * C1 + C1]), f"SP{ch}")
                M.wait(act, j, f"Y{NC1 - 1}")
                A.by(nc.scalar.activation(kk[:], big2f, ACT.Copy), "y")
                V.wait(act, j, "yc")
                A.by(nc.scalar.activation(sq[:], kk[:], ACT.Square), "y_square")
                M.wait(act, j, "y_stats")
                A.by(nc.scalar.activation(std[:], w[:, 3, 0:2 * NT], ACT.Sqrt, scale=1.0 / N,
                                          bias=gn_eps[:]), "y_std")

        @block.vector
        def _(dve):
            vec = nc.vector

            def conv_taps(j, at):
                for t in plan[at]:
                    V.wait(dve, j, f"tap{t - 1}")
                    V.by(vec.scalar_tensor_tensor(conv[:, bass.ds(j, 1), :], c[:, bass.ds(j, 1), t:t + T],
                                                  table[:, bass.ds(j + (FIRST["cconv_w"] + 4 * t), 1)],
                                                  conv[:, bass.ds(j, 1), :], ALU.mult, ALU.add), f"tap{t}")

            V.start(dve)
            dve.wait_ge(consts_landed, 16 * len(masks))
            vec.memset(gn_eps[:], GN_EPS).then_inc(prepared, 1)
            vec.tensor_scalar(cols[:], table[:, FIRST["k_a"]:FIRST["k_a"] + 4], -1.0, 1.0, ALU.mult,
                              ALU.add).then_inc(prepared, 1)
            vec.tensor_copy(both[:, 0, :], masks["before"][:]).then_inc(prepared, 1)
            vec.tensor_copy(both[:, 1, :], masks["upto"][:]).then_inc(prepared, 1)
            dve.wait_ge(prepared, 4)
            with dve.Fori(0, PAIRS) as j:
                r, k, v = (rkv[:, bass.ds(j + 4 * n, 1), :] for n in range(3))
                V.by(vec.tensor_scalar(kkr[:], k, col("k_k", j), None, ALU.mult), "kkr")
                A.wait(dve, j, "sg")
                V.by(vec.tensor_tensor_scan(cumt[:], masks["chunk_run"][:], sg[:], 0.0, ALU.mult, ALU.add), "sg_sum")
                V.wait(dve, j, "sg_sum")
                V.by(vec.tensor_tensor(sg[:], cumt[:], sg[:], ALU.subtract), "before_sum")
                A.wait(dve, j, "a")
                V.by(vec.tensor_scalar(kf[:], a[:], col("k_a", j), cols[:, bass.ds(j, 1)], ALU.mult, ALU.add), "kat")
                V.wait(dve, j, "kat")
                V.by(vec.tensor_tensor(kf[:], k, kf[:], ALU.mult), "kf")
                V.wait(dve, j, "kf")
                V.by(vec.scalar_tensor_tensor(bon[:], r, col("r_k", j), kf[:], ALU.mult, ALU.mult), "bon")
                V.by(vec.tensor_scalar(conv[:, bass.ds(j, 1), :], c[:, bass.ds(j, 1), 0:T],
                                       table[:, bass.ds(j + FIRST["cconv_w"], 1)], col("cconv_b", j),
                                       ALU.mult, ALU.add), "tap0")
                conv_taps(j, "stats")
                M.wait(dve, j, "kk_stats")
                V.by(vec.tensor_scalar(floor[:], w[:, 0, 0:2 * NT], 1e-24, None, ALU.max), "kk_floor")
                A.wait(dve, j, "kk_std")
                V.by(vec.reciprocal(inv[:], std[:]), "kk_inv")
                V.wait(dve, j, "kk_inv")
                wide_inv = inv[:].unsqueeze(2).broadcast_to((P, 2 * NT, N))
                V.by(vec.tensor_copy(kk[:].rearrange("p (a n) -> p a n", n=N), wide_inv), "kk_wide")
                M.wait(dve, j, "kk_scale")
                V.by(vec.tensor_tensor(kk[:], bigf, kkr[:], ALU.mult), "kk")
                A.wait(dve, j, "pprev")
                V.wait(dve, j, "kk")
                chunks = lambda t: t.rearrange("p (c n) -> p c n", n=C1)
                V.by(vec.scalar_tensor_tensor(ar[:, :, 0, :], chunks(kk[:]), -1.0, chunks(sg[:]),
                                              ALU.mult, ALU.mult), "at")
                V.by(vec.tensor_tensor(ar[:, :, 1, :], r.rearrange("p a (c n) -> p (a c) n", n=C1), chunks(p[:]),
                                       ALU.mult), "rt")
                V.by(vec.tensor_tensor(kk[:], kk[:], a[:], ALU.mult), "b1")
                V.wait(dve, j, "b1")
                V.by(vec.tensor_tensor(b_[:], kk[:], pinv[:], ALU.mult), "bt")
                V.by(vec.tensor_tensor(k_[:], kf[:], pinv[:], ALU.mult), "kt")
                mask = both[:].unsqueeze(1).broadcast_to((P, 4, 2, C1))
                for q in range(4):
                    for name, dst, bank in (("LB", lb, q % 2), ("LK", lk, 2 + q % 2)):
                        M.wait(dve, j, f"{name}{q}")
                        V.by(vec.tensor_tensor(dst[:, 4 * q:4 * q + 4], w[:, bank, :].rearrange(
                            "p (c x n) -> p c x n", x=2, n=C1), mask, ALU.mult), f"{name}{q}")
                eye = masks["eye"][:].unsqueeze(1).broadcast_to((P, BATCH, C1))
                for b in range(2):
                    G.wait(dve, j, f"LM0{b}")
                    V.by(vec.tensor_tensor(xt[:, b], lm[:, b], eye, ALU.add), f"XT0{b}")
                bank = lambda t: t.rearrange("p (c n) -> p c n", n=C1)
                for b in range(2):
                    M.wait(dve, j, f"T0{b}")
                    V.by(vec.tensor_tensor(xx[:, b], bank(w[:, b, :]), eye, ALU.add), f"X0{b}")
                for l in range(1, LEVELS):
                    for b in range(2):
                        conv_taps(j, f"level{l}{b}")
                        M.wait(dve, j, f"X{l}{b}")
                        if l < LEVELS - 1:
                            V.by(vec.tensor_tensor(xx[:, b], bank(w[:, 2 + b, :]), xx[:, b], ALU.add), f"X{l}{b}")
                        V.by(vec.tensor_tensor(xt[:, b], bank(big[:, b, :]), xt[:, b], ALU.add), f"XT{l}{b}")
                for ch in range(NC1):
                    M.wait(dve, j, f"U{ch}")
                    V.by(vec.tensor_copy(us[:], w[:, 1, 0:N]), f"U{ch}")
                    M.wait(dve, j, f"S{ch}")
                    decay = p[:, ch * C1 + C1 - 1:ch * C1 + C1]
                    if ch:
                        A.wait(dve, j, f"SP{ch}")
                        V.by(vec.scalar_tensor_tensor(st[:, (ch + 1) % 2, :], w[:, 2, 0:N], decay, sp_[:],
                                                      ALU.mult, ALU.add), f"S{ch}")
                    else:
                        V.by(vec.tensor_scalar(st[:, 1, :], w[:, 2, 0:N], decay, None, ALU.mult), f"S{ch}")
                conv_taps(j, "tail")
                M.wait(dve, j, "mean")
                V.by(vec.scalar_tensor_tensor(kk[:], bigf, -1.0 / N, kk[:], ALU.mult, ALU.add), "yc")
                A.wait(dve, j, "y_std")
                V.by(vec.reciprocal(inv[:], std[:]), "y_inv")
                V.wait(dve, j, "y_inv")
                V.by(vec.tensor_copy(a[:].rearrange("p (a n) -> p a n", n=N), wide_inv), "y_wide")
                M.wait(dve, j, "y_scale")
                V.by(vec.tensor_tensor(kk[:], bigf, kk[:], ALU.mult), "yn")
                V.wait(dve, j, "yn")
                V.by(vec.tensor_scalar(kk[:], kk[:], col("lnx_g", j), col("lnx_b", j), ALU.mult, ALU.add), "ynorm")
                M.wait(dve, j, "bonus")
                V.by(vec.tensor_tensor(kf[:], big2f, v_[:], ALU.mult), "bonus")
                V.wait(dve, j, "bonus")
                V.by(vec.tensor_tensor(kk[:], kk[:], kf[:], ALU.add), "ysum")
                M.wait(dve, j, "gate")
                V.wait(dve, j, "ysum")
                V.by(vec.tensor_tensor(r, bigf.unsqueeze(1), kk[:].unsqueeze(1), ALU.mult), "gated")

        @block.tensor
        def _(pe):
            mm = nc.tensor.matmul

            def broad(out, lhs, rhs, p0=0, k=P):
                for h in range(2):
                    last = mm(out[:, h, :], lhs, rhs[p0:p0 + k, 512 * h:512 * h + 512], start=True, stop=True)
                return last

            def per_head(out, lhs, rhs, start=True, stop=True):
                for h in heads:
                    last = mm(out[h], lhs[h], rhs[h], start=start, stop=stop, skip_group_check=True)
                return last

            def stats():
                for i in range(NT):
                    last = mm(w[:, stats_bank, 2 * i:2 * i + 2], sq[:, i * P:(i + 1) * P], masks["head_sel"][:],
                              start=True, stop=True)
                return last

            def scales(src):
                for i in range(NT):
                    last = mm(bigf[:, i * P:(i + 1) * P], src[:, i * P:(i + 1) * P], ident[:], start=True, stop=True)
                return last

            def at(t, ch):
                return t[:, ch * C1:(ch + 1) * C1]

            def need(made, name, back=0):
                made.wait(pe, j, name, back)
                pe.sem_inc(passed, 1)

            M.start(pe)
            pe.wait_ge(consts_landed, 16 * len(masks))
            pe.wait_ge(low_ready, 2)
            with pe.Fori(0, PAIRS) as j:
                pe.wait_ge(ups_landed, 48 * (j + 1))
                need(V, "gated", back=1)
                M.by(broad(big, ups[0:32, 0, :], low[:, 0, :], 0, 32), "decay")
                M.by(broad(big2, ups[32:64, 1, :], low[:, 0, :], 32, 32), "iclr")
                need(A, "square")
                stats_bank = 0
                M.by(stats(), "kk_stats")
                need(V, "kk_wide")
                M.by(scales(kk), "kk_scale")
                need(A, "v")

                def turn(x, src, bank):
                    for b in range(2):
                        for i in range(BATCH):
                            ch = b * BATCH + i
                            for h in heads:
                                last = mm(bank[h, b, i * N:(i + 1) * N], src[h, ch * C1:(ch + 1) * C1],
                                          ident[h, h], start=True, stop=True, skip_group_check=True)
                        M.by(last, f"{x}t{b}")

                turn("v", v_, big2)
                need(V, "kt")
                for q in range(4):
                    for name, src, bank in (("LB", b_, q % 2), ("LK", k_, 2 + q % 2)):
                        if q >= 2:
                            need(V, f"{name}{q - 2}")
                        for i in range(4):
                            ch = 4 * q + i
                            for h in heads:
                                last = mm(w[h, bank, i * P:(i + 1) * P], src[h, ch * C1:(ch + 1) * C1],
                                          ar[h, ch, :, :], start=True, stop=True, skip_group_check=True)
                        M.by(last, f"{name}{q}")
                turn("b", b_, big)
                need(A, "vt1")
                turn("k", k_, big2)
                for b in range(2):
                    need(G, f"LM0{b}")
                    need(V, f"LB{2 + b}")
                    for i in range(BATCH):
                        last = per_head(w[:, b, i * C1:(i + 1) * C1], lm[:, b, i, :], masks["eye"])
                    M.by(last, f"T0{b}")
                need(V, "LK3")
                need(A, "bt1")
                for l in range(1, LEVELS):
                    for b in range(2):
                        need(G, f"LM{l}{b}")
                        need(V, f"X0{b}" if l == 1 else f"XT{l - 1}{b}")
                        for i in range(BATCH):
                            last = per_head(w[:, b, i * C1:(i + 1) * C1], lm[:, b, i, :], xx[:, b, i, :])
                        M.by(last, f"T{l}{b}")
                    for b in range(2):
                        need(A, f"T{l}{b}")
                        for i in range(BATCH):
                            cols_ = slice(i * C1, (i + 1) * C1)
                            if l < LEVELS - 1:
                                per_head(w[:, 2 + b, cols_], xt[:, b, i, :], tt[:, b, i, :])
                            last = per_head(big[:, b, cols_], tt[:, b, i, :], xt[:, b, i, :])
                        M.by(last, f"X{l}{b}")
                need(A, "kt1")
                for ch in range(NC1):
                    old = st[:, ch % 2, :]
                    x_t = xt[:, ch // BATCH, ch % BATCH, :]
                    if ch:
                        need(V, f"S{ch - 1}")
                        for h in heads:
                            mm(w[h, 0, 0:N], ar[h, ch, 0, :], old[h], start=True, stop=False, skip_group_check=True)
                            last = mm(w[h, 0, 0:N], lk[h, ch, 0, :], vt[h, ch, :], start=False, stop=True,
                                      skip_group_check=True)
                    else:
                        need(V, f"XT{LEVELS - 1}1")
                        last = per_head(w[:, 0, 0:N], lk[:, ch, 0, :], vt[:, ch, :])
                    M.by(last, f"G{ch}")
                    need(A, f"G{ch}")
                    M.by(per_head(w[:, 1, 0:N], x_t, gs), f"U{ch}")
                    need(V, f"U{ch}")
                    for h in heads:
                        mm(w[h, 2, 0:N], bt[h, ch, :], us[h], start=True, stop=False, skip_group_check=True)
                        last = mm(w[h, 2, 0:N], kt[h, ch, :], vt[h, ch, :], start=False, stop=True,
                                  skip_group_check=True)
                    M.by(last, f"S{ch}")
                    for h in heads:
                        y = big2[h, ch // BATCH, (ch % BATCH) * C1:(ch % BATCH + 1) * C1]
                        if ch:
                            mm(y, old[h], ar[h, ch, 1, :], start=True, stop=False, skip_group_check=True)
                        mm(y, us[h], lb[h, ch, 1, :], start=ch == 0, stop=False, skip_group_check=True)
                        last = mm(y, vt[h, ch, :], lk[h, ch, 1, :], start=False, stop=True, skip_group_check=True)
                    M.by(last, f"Y{ch}")
                need(A, "y")
                M.by(broad(big, masks["head_ones"][:], kk), "mean")
                need(A, "y_square")
                stats_bank = 3
                M.by(stats(), "y_stats")
                need(V, "y_wide")
                M.by(scales(a), "y_scale")
                M.by(broad(big2, masks["head_ones"][:], bon), "bonus")
                need(V, "yn")
                M.by(broad(big, ups[0:96, 2, :], low[:, 1, :], 0, 96), "gate")


def conv_norm_and_split(nc, consts, table, ident, conv, rwkv, hi, lo):
    with Scope(nc, "cln") as s:
        ones = s.sb("ones", [P, P])
        square = s.sb("square", [P, 4, T])
        std, inv = (s.sb(n, [P, NT]) for n in ("std", "inv"))
        wide = s.sb("wide", [P, NT, P])
        eps = s.sb("eps", [P, 1])
        mean = s.ps("mean", [P, 2, 512])
        stats = s.ps("stats", [P, 512])
        scale = s.ps("scale", [P, 2, 512])
        prepared = s.sem("prepared")
        mean_ready, centred, squared, stats_ready = (s.sem(n) for n in ("mean_ready", "centred", "squared", "stats_ready"))
        std_ready, inv_ready, wide_ready, scale_ready = (
            s.sem(n) for n in ("std_ready", "inv_ready", "wide_ready", "scale_ready"))
        scaled, active, hi_ready = (s.sem(n) for n in ("scaled", "active", "hi_ready"))
        block = s.block()
        scale_f, mean_f = (t[:].rearrange("p a b -> p (a b)") for t in (scale, mean))

        @block.tensor
        def _(pe):
            pe.wait_ge(prepared, 2)
            for h in range(2):
                for f in range(4):
                    mm = nc.tensor.matmul(mean[:, h, :], ones[:], conv[:, f, 512 * h:512 * h + 512],
                                          start=f == 0, stop=f == 3)
            mm.then_inc(mean_ready, 1)
            pe.wait_ge(squared, 4)
            for i in range(NT):
                for f in range(4):
                    mm = nc.tensor.matmul(stats[:, i:i + 1], square[:, f, i * P:(i + 1) * P], ones[:, 0:1],
                                          start=f == 0, stop=f == 3)
            mm.then_inc(stats_ready, 1)
            pe.wait_ge(wide_ready, 1)
            for i in range(NT):
                mm = nc.tensor.matmul(scale_f[:, i * P:(i + 1) * P], wide[:, i, :], ident[:], start=True, stop=True)
            mm.then_inc(scale_ready, 1)

        @block.vector
        def _(dve):
            vec = nc.vector
            vec.memset(ones[:], 1.0).then_inc(prepared, 1)
            vec.memset(eps[:], 1e-5).then_inc(prepared, 1)
            dve.wait_ge(mean_ready, 1)
            for f in range(4):
                vec.scalar_tensor_tensor(conv[:, f, :], mean_f, -1.0 / DR, conv[:, f, :], ALU.mult,
                                         ALU.add).then_inc(centred, 1)
            dve.wait_ge(std_ready, 1)
            vec.reciprocal(inv[:], std[:]).then_inc(inv_ready, 1)
            dve.wait_ge(inv_ready, 1)
            vec.tensor_copy(wide[:], inv[:].unsqueeze(2).broadcast_to((P, NT, P))).then_inc(wide_ready, 1)
            dve.wait_ge(scale_ready, 1)
            for f in range(4):
                vec.tensor_tensor(conv[:, f, :], scale_f, conv[:, f, :], ALU.mult).then_inc(scaled, 1)
            for f in range(4):
                dve.wait_ge(hi_ready, f + 1)
                vec.tensor_tensor(lo[:, f, :], rwkv[:, f, :], hi[:, f, :].bitcast(F32), ALU.subtract)
            for f in range(4):
                dve.wait_ge(hi_ready, f + 5)
                vec.tensor_tensor(lo[:, 4 + f, :], conv[:, f, :], hi[:, 4 + f, :].bitcast(F32), ALU.subtract)

        @block.scalar
        def _(act):
            for f in range(4):
                act.wait_ge(centred, f + 1)
                nc.scalar.activation(square[:, f, :], conv[:, f, :], ACT.Square).then_inc(squared, 1)
            act.wait_ge(stats_ready, 1)
            nc.scalar.activation(std[:], stats[:, 0:NT], ACT.Sqrt, scale=1.0 / DR, bias=eps[:]).then_inc(std_ready, 1)
            for f in range(4):
                nc.scalar.activation(hi[:, f, :], rwkv[:, f, :], ACT.Copy).then_inc(hi_ready, 1)
            for f in range(4):
                act.wait_ge(scaled, f + 1)
                nc.scalar.activation(conv[:, f, :], conv[:, f, :], ACT.Silu,
                                     scale=table[:, FIRST["cln_g"] + f:FIRST["cln_g"] + f + 1],
                                     bias=table[:, FIRST["cln_b"] + f:FIRST["cln_b"] + f + 1]).then_inc(active, 1)
            for f in range(4):
                act.wait_ge(active, f + 1)
                nc.scalar.activation(hi[:, 4 + f, :], conv[:, f, :], ACT.Copy).then_inc(hi_ready, 1)


def token_projection(nc, tag, w, hi, lo, x, x_src=None, gain=None, x_dst=None, meta=None):
    c0 = META if meta is not None else 0
    tiles = NT + (meta is not None)
    with Scope(nc, tag) as s:
        raw = s.sb("raw", [P, 2, D])
        w_hi = s.sb("w_hi", [P, KD, D], F32R)
        w_lo = s.sb("w_lo", [P, KD, D], F32R)
        squares = s.sb("squares", [P, D])
        sums, std, inv = (s.sb(n, [P, tiles]) for n in ("sums", "std", "inv"))
        gains = s.sb("gains", [P, D])
        normed = s.sb("normed", [P, 2, D])
        eps = s.sb("eps", [P, 1])
        out = [s.ps(f"out{e}", [P, 2, 512]) for e in range(2)]
        raw_landed = [s.sem(f"raw_landed{e}") for e in range(2)]
        x_landed, gains_landed, hi_ready, lo_ready, eps_ready = (
            s.sem(n) for n in ("x_landed", "gains_landed", "hi_ready", "lo_ready", "eps_ready"))
        product_ready, psum_free, sums_ready, std_ready, inv_ready, normed_ready, x_ready, stored = (
            s.sem(n) for n in ("product_ready", "psum_free", "sums_ready", "std_ready", "inv_ready",
                               "normed_ready", "x_ready", "stored"))
        block = s.block()

        @block.sync
        def _(sp):
            for k in range(KD):
                if k >= 2:
                    sp.wait_ge(lo_ready, k - 1)
                sp.dma_start(raw[:, k % 2, :], w[k * P:(k + 1) * P, :]).then_inc(raw_landed[k % 2], 16)
            if gain is not None:
                sp.dma_start(gains[:], gain.broadcast_to((P, D))).then_inc(gains_landed, 16)
            if x_src is not None:
                sp.dma_start(x[:], x_src).then_inc(x_landed, 16)
            if x_dst is not None:
                for i in range(NT):
                    sp.wait_ge(x_ready, i + 1)
                    sp.dma_start(x_dst[:, i, :], x[:, i, :]).then_inc(stored, 16)
                sp.wait_ge(stored, 16 * NT)

        @block.gpsimd
        def _(pool):
            for k in range(KD):
                pool.wait_ge(hi_ready, k + 1)
                nc.gpsimd.tensor_tensor(w_lo[:, k, :], raw[:, k % 2, :], w_hi[:, k, :], ALU.subtract).then_inc(
                    lo_ready, 1)

        @block.tensor
        def _(pe):
            for i in range(tiles):
                cols = slice(c0 + i * P, c0 + (i + 1) * P) if i < NT else slice(0, META)
                m = P if i < NT else META
                if i >= 2:
                    pe.wait_ge(psum_free, i - 1)
                for k in range(KD):
                    if i == 0:
                        pe.wait_ge(lo_ready, k + 1)
                    for part, (a, b) in enumerate(((hi, w_hi), (lo, w_hi), (hi, w_lo))):
                        for h in range(2):
                            mm = nc.tensor.matmul(out[i % 2][0:m, h, :], a[:, k, cols], b[:, k, 512 * h:512 * h + 512],
                                                  start=k == 0 and part == 0, stop=k == KD - 1 and part == 2)
                mm.then_inc(product_ready, 1)

        @block.scalar
        def _(act):
            for k in range(KD):
                act.wait_ge(raw_landed[k % 2], 16 * (k // 2 + 1))
                nc.scalar.activation(w_hi[:, k, :], raw[:, k % 2, :], ACT.Copy).then_inc(hi_ready, 1)
            if gain is None:
                return
            act.wait_ge(eps_ready, 1)
            for i in range(tiles):
                act.wait_ge(product_ready, i + 1)
                nc.scalar.activation(squares[:], out[i % 2][:].rearrange("p a b -> p (a b)"), ACT.Square,
                                     accum_out=sums[:, i:i + 1]).then_inc(sums_ready, 1)
                act.wait_ge(sums_ready, i + 1)
                nc.scalar.activation(std[:, i:i + 1], sums[:, i:i + 1], ACT.Sqrt, scale=1.0 / D,
                                     bias=eps[:]).then_inc(std_ready, 1)

        @block.vector
        def _(dve):
            vec = nc.vector
            vec.memset(eps[:], RMS_EPS).then_inc(eps_ready, 1)
            if x_src is not None:
                dve.wait_ge(x_landed, 16)
            if gain is not None:
                dve.wait_ge(gains_landed, 16)
            for i in range(tiles):
                flat = out[i % 2][:].rearrange("p a b -> p (a b)")
                if gain is None:
                    dve.wait_ge(product_ready, i + 1)
                    dst = x[:, i, :] if i < NT else meta[:, :]
                    m = P if i < NT else META
                    vec.tensor_tensor(dst, flat[0:m, :], dst, ALU.add).then_inc(psum_free, 1)
                    continue
                dve.wait_ge(std_ready, i + 1)
                vec.reciprocal(inv[:, i:i + 1], std[:, i:i + 1]).then_inc(inv_ready, 1)
                dve.wait_ge(inv_ready, i + 1)
                vec.scalar_tensor_tensor(normed[:, i % 2, :], flat, inv[:, i:i + 1], gains[:], ALU.mult,
                                         ALU.mult).then_inc(psum_free, 1)
                dve.wait_ge(psum_free, i + 1)
                vec.tensor_tensor(x[:, i, :], normed[:, i % 2, :], x[:, i, :], ALU.add).then_inc(x_ready, 1)


def feed_forward(nc, tag, ins, table, hi, lo, f, second):
    up = ins["w_up_2" if second else "ffn_up"][0]
    down = ins["w_down_2" if second else "ffn_down"][0]
    taps, bias = (FIRST["conv_w_2"], FIRST["conv_b_2"]) if second else (FIRST["ffn_conv_w"], FIRST["ffn_conv_b"])
    wide = F1 // P if second else 2 * F1 // P
    groups = F1 // P // 2
    c0 = META if second else 0
    func = ACT.Silu if second else ACT.Gelu_apprx_tanh
    DOWN = [f"down{t}" for t in range(2 * NT)]
    act_names = ["hi0", "hi1", "hi2", "y0", "hi3", "g0", "y1", "hid_hi0", "dhi", "y2", "g1", "y3", "hid_hi1"]
    if second:
        act_names = [n for n in act_names if n not in ("y1", "y3")]
    pool_names = ["lo0", "lo1", "lo2", "lo3", "dlo"]
    dve_names = []
    for q in range(2):
        for e in range(2):
            if not (second and e):
                dve_names += [f"tapa{2 * q + e}", f"tapb{2 * q + e}"]
                dve_names += [f"past1{q}", f"past0{q}"] if second else []
        dve_names += [f"hid{q}", f"hid_lo{q}"]
    dve_names += DOWN
    pe_names = [f"up{i}" for i in range(4)] + DOWN
    with Scope(nc, tag) as s:
        raw = s.sb("raw", [P, 2, KD, P])
        w_hi, w_lo = (s.sb(n, [P, 2, KD, P], F32R) for n in ("w_hi", "w_lo"))
        d_raw = s.sb("d_raw", [P, 2, D])
        d_hi, d_lo = (s.sb(n, [P, 2, D], F32R) for n in ("d_hi", "d_lo"))
        y = s.sb("y", [P, 2, T])
        hid_hi, hid_lo = (s.sb(n, [P, 2, 2, T], F32R) for n in ("hid_hi", "hid_lo"))
        out = [s.ps(f"out{e}", [P, 2, 512]) for e in range(2)]
        past = s.ps("past", [P, 512])
        acc = s.ps("acc", [P, 3, 512])
        flat = [o[:].rearrange("p a b -> p (a b)") for o in out]
        landed = [s.sem(f"landed{e}") for e in range(2)]
        d_landed, cleared = s.sem("d_landed"), s.sem("cleared")
        A = Made(s.sem("scalar_made"), act_names)
        V = Made(s.sem("vector_made"), dve_names)
        M = Made(s.sem("tensor_made"), pe_names)
        G = Made(s.sem("pool_made"), pool_names)
        block = s.block()

        def turns(eng, turn):
            turn(0, 0, True, False)
            with eng.Fori(0, (groups - 1) // 2) as h:
                turn(2 * h + 1, 1, True, True)
                turn(2 * h + 2, 0, True, True)
            turn(groups, groups % 2, False, True)

        @block.sync
        def _(sp):
            def turn(g, par, has_up, has_down):
                if has_up:
                    for i in range(4):
                        G.wait(sp, g, f"lo{(i - 2) % 4}", back=1 if i < 2 else 0)
                        sp.sem_inc(cleared, 1)
                        c = (2 * g + i // 2) * P + (i % 2) * F1
                        sp.dma_start(raw[:, i % 2], up[:, bass.ds(c, P)].rearrange("(k p) m -> p k m", p=P)).then_inc(
                            landed[i % 2], 16)
                if has_down:
                    G.wait(sp, g, "dlo", back=1)
                    sp.sem_inc(cleared, 1)
                    sp.dma_start(d_raw[:], down[bass.ds((g - 1) * 2 * P, 2 * P), :].rearrange(
                        "(k p) m -> p k m", p=P)).then_inc(d_landed, 16)

            turns(sp, turn)

        @block.gpsimd
        def _(pool):
            def turn(g, par, has_up, has_down):
                if has_up:
                    for i in range(4):
                        A.wait(pool, g, f"hi{i}")
                        G.by(nc.gpsimd.tensor_tensor(w_lo[:, i % 2], raw[:, i % 2], w_hi[:, i % 2], ALU.subtract),
                             f"lo{i}")
                else:
                    G.skip(pool, g, 4)
                if has_down:
                    A.wait(pool, g, "dhi")
                    G.by(nc.gpsimd.tensor_tensor(d_lo[:], d_raw[:], d_hi[:], ALU.subtract), "dlo")
                else:
                    G.skip(pool, g, 1)

            G.start(pool)
            turns(pool, turn)

        @block.tensor
        def _(pe):
            def turn(g, par, has_up, has_down):
                if has_up:
                    for i in range(4):
                        G.wait(pe, g, f"lo{i}")
                        last = f"tapb{(i - 2) % 4}" if not (second and i % 2) else f"hid{((i - 2) % 4) // 2}"
                        if second and i % 2 == 0:
                            last = f"past0{((i - 2) % 4) // 2}"
                        V.wait(pe, g, last, back=1 if i < 2 else 0)
                        A.wait(pe, g, f"y{(i - 2) % 4}" if not (second and i % 2) else "g0", back=1 if i < 2 else 0)
                        outs = [(out[i % 2][:, h, :], c0 + 512 * h, 512) for h in range(2)]
                        if second and i % 2 == 0:
                            outs.append((past[:, 0:2], META - 2, 2))
                        for k in range(KD):
                            for part, (a, b) in enumerate(((w_hi, hi), (w_hi, lo), (w_lo, hi))):
                                for o, first, n in outs:
                                    mm = nc.tensor.matmul(o, a[:, i % 2, k, :], b[:, k, first:first + n],
                                                          start=k == 0 and part == 0, stop=k == KD - 1 and part == 2)
                        M.by(mm, f"up{i}")
                else:
                    M.skip(pe, g, 4)
                if has_down:
                    G.wait(pe, g, "dlo")
                    V.wait(pe, g, DOWN[-1], back=1)
                    for t in range(2 * NT):
                        i, h = t // 2, t % 2
                        if t >= 3:
                            V.wait(pe, g, f"down{t - 3}")
                        for k in range(2):
                            for part, (a, b) in enumerate(((hid_hi, d_hi), (hid_lo, d_hi), (hid_hi, d_lo))):
                                mm = nc.tensor.matmul(acc[:, t % 3, :], a[:, 1 - par, k, i * P:(i + 1) * P],
                                                      b[:, k, 512 * h:512 * h + 512],
                                                      start=k == 0 and part == 0, stop=k == 1 and part == 2)
                        M.by(mm, f"down{t}")
                else:
                    M.skip(pe, g, 2 * NT)

            M.start(pe)
            turns(pe, turn)

        @block.scalar
        def _(act):
            def turn(g, par, has_up, has_down):
                def split(i):
                    act.wait_ge(landed[i % 2], (2 * g + i // 2 + 1) * 16)
                    M.wait(act, g, f"up{(i - 2) % 4}", back=1 if i < 2 else 0)
                    A.by(nc.scalar.activation(w_hi[:, i % 2], raw[:, i % 2], ACT.Copy), f"hi{i}")

                def column(at, i):
                    return table[:, bass.ds(2 * g + (at + i // 2 + (i % 2) * (F1 // P)), 1)]

                def conv_last(i):
                    M.wait(act, g, f"up{i}")
                    A.by(nc.scalar.activation(y[:, i % 2, :], flat[i % 2], ACT.Identity, scale=column(taps + 2 * wide, i),
                                              bias=column(bias, i)), f"y{i}")

                def activate(q):
                    V.wait(act, g, f"past0{q}" if second else f"tapb{2 * q}")
                    A.by(nc.scalar.activation(y[:, 0, :], y[:, 0, :], func), f"g{q}")

                def hidden_hi(q):
                    V.wait(act, g, f"hid{q}")
                    A.by(nc.scalar.activation(hid_hi[:, par, q, :], y[:, 1, :], ACT.Copy), f"hid_hi{q}")

                if has_up:
                    split(0)
                    split(1)
                    M.wait(act, g, "up0")
                    split(2)
                    conv_last(0)
                    split(3)
                    activate(0)
                    if not second:
                        conv_last(1)
                    hidden_hi(0)
                else:
                    A.skip(act, g, act_names.index("dhi"))
                if has_down:
                    act.wait_ge(d_landed, g * 16)
                    M.wait(act, g, DOWN[-1], back=1)
                    A.by(nc.scalar.activation(d_hi[:], d_raw[:], ACT.Copy), "dhi")
                else:
                    A.skip(act, g, 1)
                if has_up:
                    V.wait(act, g, "hid_lo0")
                    conv_last(2)
                    activate(1)
                    if not second:
                        conv_last(3)
                    hidden_hi(1)

            A.start(act)
            turns(act, turn)

        @block.vector
        def _(dve):
            vec = nc.vector

            def turn(g, par, has_up, has_down):
                def column(at, i):
                    return table[:, bass.ds(2 * g + (at + i // 2 + (i % 2) * (F1 // P)), 1)]

                def tap(i, back, at, name):
                    V.by(vec.scalar_tensor_tensor(y[:, i % 2, back:T], flat[i % 2][:, 0:T - back], column(at, i),
                                                  y[:, i % 2, back:T], ALU.mult, ALU.add), name)

                if has_up:
                    for q in range(2):
                        for e in range(2):
                            i = 2 * q + e
                            if second and e:
                                continue
                            A.wait(dve, g, f"y{i}")
                            tap(i, 1, taps + wide, f"tapa{i}")
                            V.wait(dve, g, f"tapa{i}")
                            tap(i, 2, taps, f"tapb{i}")
                            if second:
                                V.wait(dve, g, f"tapb{i}")
                                V.by(vec.scalar_tensor_tensor(y[:, 0, 0:1], past[:, 1:2], column(taps + wide, i),
                                                              y[:, 0, 0:1], ALU.mult, ALU.add), f"past1{q}")
                                V.wait(dve, g, f"past1{q}")
                                V.by(vec.scalar_tensor_tensor(y[:, 0, 0:2], past[:, 0:2], column(taps, i),
                                                              y[:, 0, 0:2], ALU.mult, ALU.add), f"past0{q}")
                        A.wait(dve, g, f"g{q}")
                        if second:
                            M.wait(dve, g, f"up{2 * q + 1}")
                            V.by(vec.tensor_tensor(y[:, 1, :], flat[1], y[:, 0, :], ALU.mult), f"hid{q}")
                        else:
                            V.wait(dve, g, f"tapb{2 * q + 1}")
                            V.by(vec.tensor_tensor(y[:, 1, :], y[:, 1, :], y[:, 0, :], ALU.mult), f"hid{q}")
                        A.wait(dve, g, f"hid_hi{q}")
                        V.by(vec.tensor_tensor(hid_lo[:, par, q, :], y[:, 1, :], hid_hi[:, par, q, :].bitcast(F32),
                                               ALU.subtract), f"hid_lo{q}")
                else:
                    V.skip(dve, g, len(dve_names) - len(DOWN))
                if has_down:
                    for t in range(2 * NT):
                        dst = f[:, t // 2, (t % 2) * 512:(t % 2) * 512 + 512]
                        M.wait(dve, g, f"down{t}")
                        V.by(vec.tensor_tensor(dst, acc[:, t % 3, :], dst, ALU.add), f"down{t}")
                else:
                    V.skip(dve, g, len(DOWN))

            V.start(dve)
            turns(dve, turn)


def post_norm(nc, tag, f, gain, x_src, out):
    with Scope(nc, tag) as s:
        gains = s.sb("gains", [P, D])
        xs = s.sb("xs", [P, NT, D]) if x_src is not None else None
        squares = s.sb("squares", [P, D])
        sums, std, inv = (s.sb(n, [P, NT]) for n in ("sums", "std", "inv"))
        eps = s.sb("eps", [P, 1])
        gains_landed, x_landed, eps_ready, sums_ready, std_ready, inv_ready, normed_ready, stored = (
            s.sem(n) for n in ("gains_landed", "x_landed", "eps_ready", "sums_ready", "std_ready", "inv_ready",
                               "normed_ready", "stored"))
        out_ready = s.sem("out_ready") if x_src is not None else normed_ready
        block = s.block()

        @block.sync
        def _(sp):
            sp.dma_start(gains[:], gain.broadcast_to((P, D))).then_inc(gains_landed, 16)
            if x_src is not None:
                sp.dma_start(xs[:], x_src).then_inc(x_landed, 16)
            for i in range(NT):
                sp.wait_ge(out_ready, i + 1)
                sp.dma_start(out[:, i, :], f[:, i, :]).then_inc(stored, 16)
            sp.wait_ge(stored, 16 * NT)

        @block.scalar
        def _(act):
            act.wait_ge(eps_ready, 1)
            for i in range(NT):
                if i:
                    act.wait_ge(sums_ready, i)
                nc.scalar.activation(squares[:], f[:, i, :], ACT.Square, accum_out=sums[:, i:i + 1]).then_inc(
                    sums_ready, 1)
            act.wait_ge(sums_ready, NT)
            nc.scalar.activation(std[:], sums[:], ACT.Sqrt, scale=1.0 / D, bias=eps[:]).then_inc(std_ready, 1)

        @block.vector
        def _(dve):
            nc.vector.memset(eps[:], RMS_EPS).then_inc(eps_ready, 1)
            dve.wait_ge(std_ready, 1)
            nc.vector.reciprocal(inv[:], std[:]).then_inc(inv_ready, 1)
            dve.wait_ge(inv_ready, 1)
            dve.wait_ge(gains_landed, 16)
            if x_src is not None:
                dve.wait_ge(x_landed, 16)
            for i in range(NT):
                nc.vector.scalar_tensor_tensor(f[:, i, :], f[:, i, :], inv[:, i:i + 1], gains[:], ALU.mult,
                                               ALU.mult).then_inc(normed_ready, 1)
                if x_src is not None:
                    dve.wait_ge(normed_ready, i + 1)
                    nc.vector.tensor_tensor(f[:, i, :], f[:, i, :], xs[:, i, :], ALU.add).then_inc(out_ready, 1)


LN_FLOOR = 2.0 ** -63
QS, FS, IS, OS, PS, GS = 0, 8, 16, 20, 24, 28
CHUNKS2 = 44


def second_projections(nc, ins, table, hi, lo, proj):
    w = ins["w_in_2"][0]
    kinds = [(QS, FS, ACT.Silu), (FS, IS, ACT.Sigmoid), (IS, OS, ACT.Copy), (OS, PS, ACT.Silu), (PS, GS, ACT.Copy),
             (GS, CHUNKS2, ACT.Sigmoid)]
    with Scope(nc, "proj2") as s:
        st = Stream(s)
        out = [s.ps(f"out{e}", [P, 2, 512]) for e in range(2)]
        first = [s.ps(f"first{e}", [P, 512]) for e in range(2)]
        ev = s.sb("ev", [P, 2, T2])
        stored = [s.sem(f"stored{e}") for e in range(2)]
        evacuated = s.sem("evacuated")
        block = s.block()

        @block.sync
        def _(sp):
            st.load(sp, 0, 0, w[:, 0:P], first=True)
            st.load(sp, 1, 1, w[:, P:2 * P], first=True)
            with sp.Fori(1, CHUNKS2 // 2) as i:
                for e in range(2):
                    st.load(sp, 2 * i + e, e, w[:, bass.ds((2 * i + e) * P, P)])

        @block.gpsimd
        def _(pool):
            with pool.Fori(0, CHUNKS2 // 2) as i:
                for e in range(2):
                    st.split_lo(nc, pool, 2 * i + e, e)

        @block.tensor
        def _(pe):
            def step(n, e, peeled=False):
                outs = [(out[e][:, h, :], META + 512 * h, 512) for h in range(2)] + [(first[e][:, 0:META], 0, META)]
                st.product(nc, pe, n, e, P, hi, lo, outs, peeled)

            step(0, 0, True)
            step(1, 1, True)
            with pe.Fori(1, CHUNKS2 // 2) as i:
                step(2 * i, 0)
                step(2 * i + 1, 1)

        @block.scalar
        def _(act):
            def evacuate(n, i, e, func, peeled=False):
                act.wait_ge(st.product_ready, n + 1)
                if not peeled:
                    act.wait_ge(stored[e], 16 * i)
                bias = {"bias": table[:, bass.ds(n + (FIRST["b_f_2"] - FS), 1)]} if (func, s0) == (ACT.Sigmoid, FS) else {}
                nc.scalar.activation(ev[:, e, META:], out[e][:].rearrange("p a b -> p (a b)"), func,
                                     **bias).then_inc(evacuated, 1)
                nc.scalar.activation(ev[:, e, 0:META], first[e][:, 0:META], func, **bias).then_inc(evacuated, 1)
                act.wait_ge(evacuated, 2 * n + 2)
                act.dma_start(proj[:, bass.ds(n, 1), :], ev[:, e, :]).then_inc(stored[e], 16)
                act.sem_inc(st.psum_free, 1)

            st.split_hi(nc, act, 0, 0, 0, first=True)
            st.split_hi(nc, act, 1, 0, 1, first=True)
            for s0, s1, func in kinds:
                start, end = s0 // 2, s1 // 2
                if s0 == 0:
                    for e in range(2):
                        act.wait_ge(st.product_ready, e + 1)
                        st.split_hi(nc, act, e + 2, 1, e)
                        evacuate(e, 0, e, func, peeled=True)
                    start = 1
                if s1 == CHUNKS2:
                    end -= 1
                with act.Fori(start, end) as i:
                    for e in range(2):
                        st.split_hi(nc, act, 2 * i + e + 2, i + 1, e)
                        evacuate(2 * i + e, i, e, func)
            for e in range(2):
                evacuate(CHUNKS2 - 2 + e, CHUNKS2 // 2 - 1, e, ACT.Sigmoid)
            for e in range(2):
                act.wait_ge(stored[e], 16 * (CHUNKS2 // 2))


def recurrence2(nc, ins, consts, table, ident, proj, oa_hi, oa_lo):
    TILES, LV = 9, 7
    tail = T2 - 8 * P
    act_names, dve_names, pe_names, pool_names = [], [], [], []
    for e in range(2):
        act_names += [f"{e}log", f"{e}ea"] + [f"{e}el{l}{x}" for l in range(LV) for x in "st"] + [f"{e}elast"]
        act_names += ([f"vt{b}" for b in range(3)] if e == 0 else []) + [f"{e}kt{b}" for b in range(2)]
        act_names += [f"{e}o{b}" for b in range(3)]
        dve_names += [f"{e}f", f"{e}k", f"{e}floor", f"{e}a", f"{e}qa"]
        dve_names += [f"{e}z{l}{x}" for l in range(LV) for x in "st"] + [f"{e}kl"]
        dve_names += [x for i in range(TILES) for x in ((f"{e}m{i}", f"{e}S{i}") if i < 8 else (f"{e}m{i}",))]
        pool_names += [f"{e}dlast"] + [f"{e}d{l}" for l in range(LV)]
        pe_names += ([f"vt{b}" for b in range(3)] if e == 0 else []) + [f"{e}kt{b}" for b in range(2)]
        pe_names += [f"{e}s0"]
        for i in range(TILES):
            pe_names += ([f"{e}s{i + 1}"] if i < 8 else []) + [f"{e}o{i}"] + ([f"{e}S{i}"] if i < 8 else [])
    act_names += ["square", "std", "std_tail", "hi"]
    dve_names += ["inv", "inv_tail", "wide", "wide_tail", "scaled", "scaled_tail", "gated", "lo"]
    pe_names += ["stats", "scale"]
    with Scope(nc, "rec2") as s:
        masks = s.sb("masks", [P, 8 * P])
        run = s.sb("run", [P, T2])
        head_sel = s.sb("head_sel", [P, 2])
        q, sf = (s.sb(n, [P, 2, T2]) for n in ("q", "sf"))
        iv, og = (s.sb(n, [P, T2]) for n in ("iv", "og"))
        k, a, ea, qa, kl = (s.sb(n, [P, T2]) for n in ("k", "a", "ea", "qa", "kl"))
        d = s.sb("d", [P, 2, T2])
        z = s.sb("z", [P, LV, T2])
        mk = s.sb("mk", [P, 2, 8, P])
        vt = s.sb("vt", [P, TILES, P])
        kt = s.sb("kt", [P, 8, P])
        S = s.sb("S", [P, 2, N])
        o = s.sb("o", [P, T2])
        std, inv = (s.sb(n, [P, 2 * TILES]) for n in ("std", "inv"))
        eps = s.sb("eps", [P, 1])
        lower = s.sb("lower", [P, 6, 8])
        lb, rest = s.sb("lb", [P, 8]), s.sb("rest", [P, 8])
        wide = z[:, 0:2, :].rearrange("p a b -> p (a b)")[:, 0:TILES * P].rearrange("p (i b) -> p i b", b=P)
        sc = [s.ps(f"sc{i}", [P, 2, 512]) for i in range(2)]
        ob = s.ps("ob", [P, 2, 512])
        upd = s.ps("upd", [P, 512])
        tr = s.ps("tr", [P, 512])
        consts_landed, landed, prepared, cleared, lb_ready, lb_exp = (
            s.sem(n) for n in ("consts_landed", "landed", "prepared", "cleared", "lb_ready", "lb_exp"))
        passed = s.sem("passed")
        A = Made(s.sem("scalar_made"), act_names)
        V = Made(s.sem("vector_made"), dve_names)
        M = Made(s.sem("tensor_made"), pe_names)
        G = Made(s.sem("pool_made"), pool_names)
        block = s.block()

        def halves(t, l, x):
            n = T2 if l < 4 else 8 * P
            return t[:, 0:n].rearrange("p (b h c) -> p b h c", h=2, c=2 ** l)[:, :, 1 if x == "t" else 0, :]

        def size(i):
            return P if i < 8 else tail

        @block.sync
        def _(sp):
            for t, name in ((masks, "levels2"), (run, "tile_run"), (head_sel, "head_sel")):
                sp.dma_start(t[:], const_of(consts, name)).then_inc(consts_landed, 16)
            with sp.Fori(0, PAIRS) as j:
                V.wait(sp, j, "lo", back=1)
                sp.sem_inc(cleared, 1)
                sp.dma_start(sf[:], proj[:, bass.ds(2 * j + FS, 2), :]).then_inc(landed, 16)
                sp.dma_start(q[:], proj[:, bass.ds(2 * j + QS, 2), :]).then_inc(landed, 16)
                sp.dma_start(iv[:], proj[:, bass.ds(j + IS, 1), :]).then_inc(landed, 16)
                sp.dma_start(og[:], proj[:, bass.ds(j + OS, 1), :]).then_inc(landed, 16)

        @block.gpsimd
        def _(pool):
            G.start(pool)
            with pool.Fori(0, PAIRS) as j:
                for e in range(2):
                    V.wait(pool, j, f"{e}a")
                    by_tile = lambda t: t[:, 0:8 * P].rearrange("p (i b) -> p i b", b=P)
                    at = by_tile(a)
                    G.by(nc.gpsimd.tensor_tensor(by_tile(kl), at[:, :, P - 1:P].broadcast_to((P, 8, P)), at,
                                                 ALU.subtract), f"{e}dlast")
                    for l in range(LV):
                        if l >= 2:
                            V.wait(pool, j, f"{e}z{l - 2}t")
                        n = T2 if l < 4 else 8 * P
                        blocks = a[:, 0:n].rearrange("p (b c) -> p b c", c=2 ** (l + 1))
                        ref = blocks[:, :, 2 ** l - 1:2 ** l].broadcast_to((P, n >> (l + 1), 2 ** (l + 1)))
                        G.by(nc.gpsimd.tensor_tensor(d[:, l % 2, 0:n].rearrange("p (b c) -> p b c", c=2 ** (l + 1)),
                                                     blocks, ref, ALU.subtract), f"{e}d{l}")

        @block.scalar
        def _(act):
            A.start(act)
            act.wait_ge(prepared, 4)
            for i in range(2):
                nc.scalar.activation(lower[:, 3 + i, :], lower[:, 1 + i, :], ACT.Exp).then_inc(lb_exp, 1)
            act.wait_ge(lb_ready, 4)
            with act.Fori(0, PAIRS) as j:
                for e in range(2):
                    V.wait(act, j, f"{e}floor")
                    A.by(nc.scalar.activation(ea[:], sf[:, e, :], ACT.Ln), f"{e}log")
                    V.wait(act, j, f"{e}a")
                    A.by(nc.scalar.activation(ea[:], a[:], ACT.Exp), f"{e}ea")
                    for l in range(LV):
                        G.wait(act, j, f"{e}d{l}")
                        for x in "st":
                            A.by(nc.scalar.activation(halves(d[:, l % 2, :], l, x), halves(d[:, l % 2, :], l, x), ACT.Exp,
                                                      scale=1.0 if x == "t" else -1.0), f"{e}el{l}{x}")
                    A.by(nc.scalar.activation(kl[:, 0:8 * P], kl[:, 0:8 * P], ACT.Exp), f"{e}elast")
                    if e == 0:
                        for b in range(3):
                            n = min(4, TILES - 4 * b)
                            m = P if n == 4 else tail
                            M.wait(act, j, f"vt{b}")
                            A.by(nc.scalar.activation(vt[0:m, 4 * b:4 * b + n, :], tr[0:m, 0:n * P].rearrange(
                                "p (i b) -> p i b", b=P), ACT.Copy), f"vt{b}")
                    for b in range(2):
                        M.wait(act, j, f"{e}kt{b}")
                        A.by(nc.scalar.activation(kt[:, 4 * b:4 * b + 4, :], tr[:].rearrange(
                            "p (i b) -> p i b", b=P), ACT.Copy), f"{e}kt{b}")
                    hp = slice(64 * e, 64 * e + 64)
                    for b in range(3):
                        c, n = (512 * b, 512) if b < 2 else (8 * P, tail)
                        M.wait(act, j, f"{e}o{min(4 * b + 3, TILES - 1)}")
                        A.by(nc.scalar.activation(o[hp, c:c + n], ob[hp, b % 2, 0:n], ACT.Copy), f"{e}o{b}")
                A.wait(act, j, "1o2")
                A.by(nc.scalar.activation(ea[:], o[:], ACT.Square), "square")
                M.wait(act, j, "stats")
                A.by(nc.scalar.activation(std[:, 0:16], tr[:, 0:16], ACT.Sqrt, scale=1.0 / N, bias=eps[:]), "std")
                A.by(nc.scalar.activation(std[0:tail, 16:18], tr[0:tail, 16:18], ACT.Sqrt, scale=1.0 / N,
                                          bias=eps[0:tail, :]), "std_tail")
                V.wait(act, j, "gated")
                A.by(nc.scalar.activation(oa_hi[:, bass.ds(j, 1), :], o[:], ACT.Copy), "hi")

        @block.vector
        def _(dve):
            vec = nc.vector
            V.start(dve)
            logits = table[:, FIRST["lb_logits_2"]:FIRST["lb_logits_2"] + 16].rearrange("p (r c) -> p r c", r=2)
            vec.tensor_tensor(lower[:, 0, :], logits[:, 0, :], logits[:, 1, :], ALU.max).then_inc(prepared, 1)
            vec.memset(eps[:], RMS_EPS).then_inc(prepared, 1)
            dve.wait_ge(prepared, 2)
            for i in range(2):
                vec.tensor_tensor(lower[:, 1 + i, :], logits[:, i, :], lower[:, 0, :], ALU.subtract).then_inc(prepared, 1)
            dve.wait_ge(lb_exp, 2)
            vec.tensor_tensor(lower[:, 5, :], lower[:, 3, :], lower[:, 4, :], ALU.add).then_inc(lb_ready, 1)
            dve.wait_ge(lb_ready, 1)
            vec.reciprocal(lower[:, 0, :], lower[:, 5, :]).then_inc(lb_ready, 1)
            dve.wait_ge(lb_ready, 2)
            vec.tensor_tensor(lb[:], lower[:, 3, :], lower[:, 0, :], ALU.mult).then_inc(lb_ready, 1)
            dve.wait_ge(lb_ready, 3)
            vec.tensor_scalar(rest[:], lb[:], -1.0, 1.0, ALU.mult, ALU.add).then_inc(lb_ready, 1)
            dve.wait_ge(lb_ready, 4)
            dve.wait_ge(consts_landed, 48)
            with dve.Fori(0, PAIRS) as j:
                dve.wait_ge(landed, 64 * (j + 1))
                for e in range(2):
                    col = lambda t: t[:, bass.ds(2 * j + e, 1)]
                    V.by(vec.tensor_scalar(sf[:, e, :], sf[:, e, :], col(rest), col(lb), ALU.mult, ALU.add), f"{e}f")
                    V.wait(dve, j, f"{e}f")
                    V.by(vec.tensor_scalar(k[:], sf[:, e, :], -1.0, 1.0, ALU.mult, ALU.add), f"{e}k")
                    V.by(vec.tensor_scalar(sf[:, e, :], sf[:, e, :], LN_FLOOR, None, ALU.max), f"{e}floor")
                    A.wait(dve, j, f"{e}log")
                    V.by(vec.tensor_tensor_scan(a[:], run[:], ea[:], 0.0, ALU.mult, ALU.add), f"{e}a")
                    A.wait(dve, j, f"{e}ea")
                    M.wait(dve, j, f"{1 - e}o8", back=1 - e)
                    V.by(vec.tensor_tensor(qa[:], q[:, e, :], ea[:], ALU.mult), f"{e}qa")
                    for l in range(LV):
                        for x, src in (("s", k), ("t", q[:, e, :])):
                            A.wait(dve, j, f"{e}el{l}{x}")
                            V.by(vec.tensor_tensor(halves(z[:, l, :], l, x), halves(src, l, x),
                                                   halves(d[:, l % 2, :], l, x), ALU.mult), f"{e}z{l}{x}")
                    A.wait(dve, j, f"{e}elast")
                    V.by(vec.tensor_tensor(kl[:, 0:8 * P], k[:, 0:8 * P], kl[:, 0:8 * P], ALU.mult), f"{e}kl")
                    for i in range(TILES):
                        M.wait(dve, j, f"{e}s{i}")
                        n, lv = size(i), 8 if i < 8 else 5
                        src = sc[i % 2][:].rearrange("p a (l b) -> p (a l) b", b=P)
                        mask = masks[:].rearrange("p (l b) -> p l b", b=P)
                        V.by(vec.tensor_tensor(mk[0:n, i % 2, 0:lv, 0:n], src[0:n, 0:lv, 0:n], mask[0:n, 0:lv, 0:n],
                                               ALU.mult), f"{e}m{i}")
                        if i < 8:
                            M.wait(dve, j, f"{e}S{i}")
                            if i:
                                last = ea[:, i * P + P - 1:i * P + P]
                                V.wait(dve, j, f"{e}S{i - 1}")
                                V.by(vec.scalar_tensor_tensor(S[:, (i + 1) % 2, :], S[:, i % 2, :], last, upd[:, 0:N],
                                                              ALU.mult, ALU.add), f"{e}S{i}")
                            else:
                                V.by(vec.tensor_copy(S[:, 1, :], upd[:, 0:N]), f"{e}S{i}")
                A.wait(dve, j, "std_tail")
                V.by(vec.reciprocal(inv[:, 0:16], std[:, 0:16]), "inv")
                V.by(vec.reciprocal(inv[0:tail, 16:18], std[0:tail, 16:18]), "inv_tail")
                V.wait(dve, j, "inv_tail")
                heads = wide.rearrange("p i (h n) -> p (i h) n", n=N)
                for m, c0, c1, name in ((P, 0, 16, "wide"), (tail, 16, 18, "wide_tail")):
                    V.by(vec.tensor_copy(heads[0:m, c0:c1, :],
                                         inv[0:m, c0:c1].unsqueeze(2).broadcast_to((m, c1 - c0, N))), name)
                M.wait(dve, j, "scale")
                hg = table[:, bass.ds(j + FIRST["head_norm_g_2"], 1)]
                V.by(vec.scalar_tensor_tensor(o[:, 0:8 * P], sc[0][:].rearrange("p a b -> p (a b)"), hg, o[:, 0:8 * P],
                                              ALU.mult, ALU.mult), "scaled")
                V.by(vec.scalar_tensor_tensor(o[:, 8 * P:T2], sc[1][:, 0, 0:tail], hg, o[:, 8 * P:T2],
                                              ALU.mult, ALU.mult), "scaled_tail")
                V.wait(dve, j, "scaled_tail")
                V.by(vec.tensor_tensor(o[:], o[:], og[:], ALU.mult), "gated")
                V.wait(dve, j, "gated")
                A.wait(dve, j, "hi")
                V.by(vec.tensor_tensor(oa_lo[:, bass.ds(j, 1), :], o[:], oa_hi[:, bass.ds(j, 1), :].bitcast(F32),
                                       ALU.subtract), "lo")

        @block.tensor
        def _(pe):
            mm = nc.tensor.matmul

            def need(made, name, back=0):
                made.wait(pe, j, name, back)
                pe.sem_inc(passed, 1)

            M.start(pe)
            with pe.Fori(0, PAIRS) as j:
                pe.wait_ge(landed, 64 * (j + 1))
                pe.sem_inc(passed, 1)
                for e in range(2):
                    hp = slice(64 * e, 64 * e + 64)
                    if e == 0:
                        for b in range(3):
                            if b:
                                need(A, f"vt{b - 1}")
                            for i in range(4 * b, min(4 * b + 4, TILES)):
                                last = nc.tensor.transpose(tr[0:size(i), (i % 4) * P:(i % 4) * P + P],
                                                           iv[:, i * P:i * P + size(i)], ident[:])
                            M.by(last, f"vt{b}")
                        need(A, "vt2")
                    need(V, f"{e}kl")
                    for b in range(2):
                        if b:
                            need(A, f"{e}kt0")
                        for i in range(4 * b, 4 * b + 4):
                            last = nc.tensor.transpose(tr[:, (i % 4) * P:(i % 4) * P + P], kl[:, i * P:(i + 1) * P],
                                                       ident[:])
                        M.by(last, f"{e}kt{b}")

                    def scores(i):
                        n = size(i)
                        cols = slice(i * P, i * P + n)
                        if i >= 2:
                            need(V, f"{e}m{i - 2}")
                        for l in range(8 if i < 8 else 5):
                            lhs = k[:, cols] if l == 0 else z[:, l - 1, cols]
                            rhs = q[:, e, cols] if l == 0 else z[:, l - 1, cols]
                            last = mm(sc[i % 2][0:n, l // 4, (l % 4) * P:(l % 4) * P + n], lhs, rhs, start=True, stop=True)
                        M.by(last, f"{e}s{i}")

                    scores(0)
                    for i in range(TILES):
                        n = size(i)
                        cols = slice(i * P, i * P + n)
                        if i < 8:
                            scores(i + 1)
                        need(V, f"{e}m{i}")
                        if i == 8:
                            need(A, f"{e}o0")
                        if i == 0 and e == 1:
                            need(A, "0o2")
                        dst = ob[hp, (i // 4) % 2, (i % 4) * P:(i % 4) * P + n]
                        levels = 8 if i < 8 else 5
                        for l in range(levels):
                            last = mm(dst, vt[0:n, i, hp], mk[0:n, i % 2, l, 0:n], start=l == 0,
                                      stop=l == levels - 1 and i == 0, skip_group_check=True)
                        if i:
                            need(V, f"{e}S{i - 1}")
                            last = mm(dst, S[:, i % 2, :], qa[:, cols], start=False, stop=True, skip_group_check=True)
                        M.by(last, f"{e}o{i}")
                        if i < 8:
                            if i == 0:
                                need(A, f"{e}kt1")
                            M.by(mm(upd[:, 0:N], kt[:, i, :], vt[:, i, hp], start=True, stop=True), f"{e}S{i}")
                need(A, "square")
                for i in range(TILES):
                    n = size(i)
                    last = mm(tr[0:n, 2 * i:2 * i + 2], ea[:, i * P:i * P + n], head_sel[:], start=True, stop=True)
                M.by(last, "stats")
                need(V, "wide_tail")
                for i in range(TILES):
                    n = size(i)
                    dst = sc[i // 8][:].rearrange("p a b -> p (a b)")[:, (i % 8) * P:(i % 8) * P + n]
                    last = mm(dst, wide[0:n, i, :], ident[0:n, 0:n], start=True, stop=True)
                M.by(last, "scale")


def pool_mixer(nc, ins, consts, table, proj, ob_hi, ob_lo):
    with Scope(nc, "pool") as s:
        rate = s.sb("rate", [P, 64])
        w = s.sb("w", [P, 4, P])
        pin = s.sb("pin", [P, 4, T2])
        sums = s.sb("sums", [P, 4, T2])
        part = s.sb("part", [P, 4, T2])
        out = [s.ps(f"out{e}", [P, 3, 512]) for e in range(2)]
        y = s.sb("y", [P, 4, T2])
        landed, made, product_ready, y_ready, hi_ready, psum_free = (
            s.sem(n) for n in ("landed", "made", "product_ready", "y_ready", "hi_ready", "psum_free"))
        d_ready = s.sem("d_ready")
        block = s.block()
        pieces = [(0, META, 2)] + [(META + 512 * h, 512, h) for h in range(2)]

        @block.sync
        def _(sp):
            sp.dma_start(rate[:], const_of(consts, "pool_rate")).then_inc(landed, 16)
            sp.dma_start(w[:], ins["w_pool_2"][0].rearrange("g c d -> c g d")).then_inc(landed, 16)
            sp.dma_start(pin[:], proj[:, PS:PS + 4, :]).then_inc(landed, 16)

        @block.vector
        def _(dve):
            vec = nc.vector
            count = [0]

            def step(ins_):
                ins_.then_inc(made, 1)
                count[0] += 1
                dve.wait_ge(made, count[0])

            dve.wait_ge(landed, 48)
            for g in range(4):
                src, dst, other = pin[:, g, :], sums[:, g, :], part[:, g, :]
                for r in range(g + 1):
                    back = 2 ** r
                    step(vec.tensor_tensor(dst[:, back:T2], src[:, back:T2], src[:, 0:T2 - back], ALU.add))
                    step(vec.tensor_copy(dst[:, 0:back], src[:, 0:back]))
                    src, dst, other = dst, other, dst
                total = src
                step(vec.tensor_tensor(total[:, 0:16], total[:, 0:16], rate[:, 16 * g:16 * g + 16], ALU.mult))
                vec.scalar_tensor_tensor(dst, total, 1.0 / 2 ** (g + 1), pin[:, g, :], ALU.mult,
                                         ALU.subtract).then_inc(d_ready, 1)
            for g in range(4):
                dve.wait_ge(hi_ready, g + 1)
                vec.tensor_tensor(ob_lo[:, g, :], y[:, g, :], ob_hi[:, g, :].bitcast(F32), ALU.subtract)

        @block.tensor
        def _(pe):
            for g in range(4):
                pe.wait_ge(d_ready, g + 1)
                if g >= 2:
                    pe.wait_ge(psum_free, 2 * (g - 1))
                d = (part if g % 2 == 0 else sums)[:, g, :]
                for c, n, bank in pieces:
                    mm = nc.tensor.matmul(out[g % 2][:, bank, 0:n], w[:, g, :], d[:, c:c + n], start=True, stop=True)
                mm.then_inc(product_ready, 1)

        @block.scalar
        def _(act):
            for g in range(4):
                act.wait_ge(product_ready, g + 1)
                scale = table[:, FIRST["pool_scale_2"] + g:FIRST["pool_scale_2"] + g + 1]
                nc.scalar.activation(y[:, g, META:], out[g % 2][:, 0:2, :].rearrange("p a b -> p (a b)"), ACT.Copy,
                                     scale=scale).then_inc(psum_free, 1)
                nc.scalar.activation(y[:, g, 0:META], out[g % 2][:, 2, 0:META], ACT.Copy,
                                     scale=scale).then_inc(psum_free, 1)
                act.wait_ge(psum_free, 2 * g + 2)
                nc.scalar.activation(ob_hi[:, g, :], y[:, g, :], ACT.Copy).then_inc(hi_ready, 1)


def branches(nc, ins, proj, oa, ob, mix_hi, mix_lo):
    w = [ins["w_branch_a_2"][0], ins["w_branch_b_2"][0]]
    act_names = ["whi", "hi"]
    dve_names = ["a0", "a1", "b0", "b1", "mix", "lo"]
    with Scope(nc, "branch") as s:
        raw = s.sb("raw", [P, KD, P])
        w_hi, w_lo = (s.sb(n, [P, 2, KD, P], F32R) for n in ("w_hi", "w_lo"))
        gates = s.sb("gates", [P, 2, 2, T2])
        out = [s.ps(f"out{e}", [P, 3, 512]) for e in range(2)]
        landed = [s.sem(f"landed{e}") for e in range(2)]
        cleared = s.sem("cleared")
        A = Made(s.sem("scalar_made"), [f"{n}{e}" for e in range(2) for n in act_names])
        V = Made(s.sem("vector_made"), [f"{n}{e}" for e in range(2) for n in dve_names])
        M = Made(s.sem("tensor_made"), [f"{n}{e}" for e in range(2) for n in "ab"])
        G = Made(s.sem("pool_made"), ["wlo0", "wlo1"])
        block = s.block()
        pieces = [(0, META, 2)] + [(META + 512 * h, 512, h) for h in range(2)]

        @block.sync
        def _(sp):
            with sp.Fori(0, KD // 2) as i:
                for e in range(2):
                    G.wait(sp, i, f"wlo{1 - e}", back=1 - e)
                    sp.sem_inc(cleared, 1)
                    for b in range(2):
                        sp.dma_start(raw[:, 4 * b:4 * b + 4, :], w[b][:, bass.ds((2 * i + e) * P, P)].rearrange(
                            "(k p) m -> p k m", p=P)).then_inc(landed[e], 16)
                    V.wait(sp, i, f"lo{e}", back=1)
                    sp.sem_inc(cleared, 1)
                    for b in range(2):
                        sp.dma_start(gates[:, e, b, :], proj[:, bass.ds(2 * i + e + GS + 8 * b, 1), :]).then_inc(
                            landed[e], 16)

        @block.gpsimd
        def _(pool):
            G.start(pool)
            with pool.Fori(0, KD // 2) as i:
                for e in range(2):
                    A.wait(pool, i, f"whi{e}")
                    G.by(nc.gpsimd.tensor_tensor(w_lo[:, e], raw[:], w_hi[:, e], ALU.subtract), f"wlo{e}")

        @block.tensor
        def _(pe):
            M.start(pe)
            with pe.Fori(0, KD // 2) as i:
                for e in range(2):
                    G.wait(pe, i, f"wlo{e}")
                    for b, (hi, lo) in enumerate((oa, ob)):
                        V.wait(pe, i, f"{'ab'[b]}1{1 - e}", back=1 - e)
                        for k in range(4):
                            for part, (x, y) in enumerate(((w_hi, hi), (w_hi, lo), (w_lo, hi))):
                                for c, n, bank in pieces:
                                    mm = nc.tensor.matmul(out[b][:, bank, 0:n], x[:, e, 4 * b + k, :], y[:, k, c:c + n],
                                                          start=k == 0 and part == 0, stop=k == 3 and part == 2)
                        M.by(mm, f"{'ab'[b]}{e}")

        @block.scalar
        def _(act):
            A.start(act)
            with act.Fori(0, KD // 2) as i:
                for e in range(2):
                    act.wait_ge(landed[e], 64 * (i + 1))
                    M.wait(act, i, f"b{e}", back=1)
                    A.by(nc.scalar.activation(w_hi[:, e], raw[:], ACT.Copy), f"whi{e}")
                    V.wait(act, i, f"mix{e}")
                    A.by(nc.scalar.activation(mix_hi[:, bass.ds(2 * i + e, 1), :], gates[:, e, 0, :], ACT.Copy), f"hi{e}")

        @block.vector
        def _(dve):
            vec = nc.vector
            V.start(dve)
            with dve.Fori(0, KD // 2) as i:
                for e in range(2):
                    for b in range(2):
                        M.wait(dve, i, f"{'ab'[b]}{e}")
                        g = gates[:, e, b, :]
                        V.by(vec.tensor_tensor(g[:, 0:META], out[b][:, 2, 0:META], g[:, 0:META], ALU.mult),
                             f"{'ab'[b]}0{e}")
                        V.by(vec.tensor_tensor(g[:, META:], out[b][:, 0:2, :].rearrange("p a b -> p (a b)"),
                                               g[:, META:], ALU.mult), f"{'ab'[b]}1{e}")
                    V.wait(dve, i, f"b1{e}")
                    V.by(vec.tensor_tensor(gates[:, e, 0, :], gates[:, e, 0, :], gates[:, e, 1, :], ALU.add), f"mix{e}")
                    A.wait(dve, i, f"hi{e}")
                    V.by(vec.tensor_tensor(mix_lo[:, bass.ds(2 * i + e, 1), :], gates[:, e, 0, :],
                                           mix_hi[:, bass.ds(2 * i + e, 1), :].bitcast(F32), ALU.subtract), f"lo{e}")

SCRATCH = [("proj2", (P, CHUNKS2, T2)), ("x_mid", (P, NT, D)), ("conv", (P, 4, T)), ("mix", (P, 2, KD, T2)), ("x3", (P, NT, D)), ("rwkv", (P, 4, T))]


def program(nc, ins, consts, out, scratch):
    x_src = ins["x"].rearrange("b (i p) d -> p (b i) d", p=P)
    x_mid = scratch["x_mid"]
    Scope.used = []
    with Scope(nc, "top") as s:
        ident = s.sb("ident", [P, P])
        table = s.sb("table", [P, ROWS])
        load_parameters(nc, ins, consts, table, ident)
        first_block(nc, ins, consts, table, ident, x_src, x_mid, scratch)
        clear_semaphores(nc)
        second_block(nc, ins, consts, table, ident, scratch["x3"], scratch, out)


def first_block(nc, ins, consts, table, ident, x_src, x_mid, scratch):
    with Scope(nc, "mix1") as m:
        col_mu = m.sb("col_mu", [P, 2])
        rkv = m.sb("rkv", [P, 12, T])
        c = m.sb("c", [P, 4, CONVW - 1 + T])
        low = m.sb("low", [P, 2, T])
        with Scope(nc, "in1") as g:
            x = g.sb("x", [P, NT, D])
            hi = g.sb("hi", [P, KD, T], F32R)
            lo = g.sb("lo", [P, KD, T], F32R)
            load_tokens(nc, ins, x, x_src, col_mu)
            norm_to_features(nc, "norm1", x, ins["norm_pre_mix"], hi, lo, ident)
            first_projections(nc, ins, table, col_mu, hi, lo, c, rkv, low)
        conv = m.sb("conv", [P, 4, T])
        recurrence1(nc, ins, consts, table, ident, c, rkv, low, conv)
        park(nc, "park1", [(scratch["conv"], conv[:]), (scratch["rwkv"], rkv[:, 0:4, :])])
    with Scope(nc, "blk1") as m:
        x = m.sb("x", [P, NT, D])
        hi = m.sb("hi", [P, KD, T], F32R)
        lo = m.sb("lo", [P, KD, T], F32R)
        with Scope(nc, "cn") as n:
            conv = n.sb("conv", [P, 4, T])
            rwkv = n.sb("rwkv", [P, 4, T])
            park(nc, "unpark1", [(conv[:], scratch["conv"]), (rwkv[:], scratch["rwkv"])])
            conv_norm_and_split(nc, consts, table, ident, conv, rwkv, hi, lo)
        token_projection(nc, "wout1", ins["w_out"][0], hi, lo, x, x_src, ins["norm_post_mix"], x_mid)
        norm_to_features(nc, "norm2", x, ins["norm_pre_ffn"], hi, lo, ident)
        clear(nc, x)
        feed_forward(nc, "ffn1", ins, table, hi, lo, x, False)
        with Scope(nc, "post") as g:
            post_norm(nc, "post1", x, ins["norm_post_ffn"], x_mid, scratch["x3"])


def second_block(nc, ins, consts, table, ident, x3, scratch, out):
    proj = scratch["proj2"]
    with Scope(nc, "blk2") as m:
        x = m.sb("x", [P, NT, D])
        meta = m.sb("meta", [META, D])
        park(nc, "load2", [(x[:], x3), (meta[:], ins["meta_tokens_2"])])
        with Scope(nc, "in2") as g:
            hi = g.sb("hi", [P, KD, T2], F32R)
            lo = g.sb("lo", [P, KD, T2], F32R)
            norm_to_features(nc, "norm3", x, ins["norm1_g_2"], hi, lo, ident, meta)
            second_projections(nc, ins, table, hi, lo, proj)
        with Scope(nc, "mix2") as g:
            oa = [g.sb(f"oa{i}", [P, 4, T2], F32R) for i in range(2)]
            recurrence2(nc, ins, consts, table, ident, proj, *oa)
            ob = [g.sb(f"ob{i}", [P, 4, T2], F32R) for i in range(2)]
            pool_mixer(nc, ins, consts, table, proj, *ob)
            mix = [g.sb(f"mix{i}", [P, KD, T2], F32R) for i in range(2)]
            branches(nc, ins, proj, oa, ob, *mix)
            park(nc, "parkmix", [(scratch["mix"][:, i], mix[i][:].bitcast(F32)) for i in range(2)])
        hi = m.sb("hi", [P, KD, T2], F32R)
        lo = m.sb("lo", [P, KD, T2], F32R)
        park(nc, "unparkmix", [(t[:].bitcast(F32), scratch["mix"][:, i]) for i, t in enumerate((hi, lo))])
        token_projection(nc, "wout2", ins["w_out_2"][0], hi, lo, x, meta=meta)
        norm_to_features(nc, "norm4", x, ins["norm2_g_2"], hi, lo, ident, meta)
        feed_forward(nc, "ffn2", ins, table, hi, lo, x, True)
        post_norm(nc, "post2", x, ins["final_norm_g_2"].rearrange("(a d) -> a d", a=1), None, out)


def load_tokens(nc, ins, x, x_src, col_mu):
    with Scope(nc, "load") as l:
        landed, zeroed = l.sem("landed"), l.sem("zeroed")
        block = l.block()

        @block.vector
        def _(dve):
            nc.vector.memset(col_mu[:], 0.0).then_inc(zeroed, 1)

        @block.sync
        def _(sp):
            sp.dma_start(x[:], x_src).then_inc(landed, 16)
            mu = ins["mu_first"].rearrange("(p a) -> p a", a=1)
            sp.wait_ge(zeroed, 1)
            sp.dma_start(col_mu[0:64, 0:1], mu[3 * DR:3 * DR + 64, :]).then_inc(landed, 16)
            sp.dma_start(col_mu[0:96, 1:2], mu[3 * DR + 64:3 * DR + 160, :]).then_inc(landed, 16)
            sp.wait_ge(landed, 48)


def clear(nc, x):
    with Scope(nc, "clear") as l:
        block = l.block()

        @block.vector
        def _(dve):
            nc.vector.memset(x[:], 0.0)


def park(nc, tag, pairs):
    with Scope(nc, tag) as l:
        landed = l.sem("landed")
        block = l.block()

        @block.sync
        def _(sp):
            for dst, src in pairs:
                sp.dma_start(dst, src).then_inc(landed, 16)
            sp.wait_ge(landed, 16 * len(pairs))


def kernel(**inputs):
    import concourse.bacc as bacc
    from concourse.bass_utils import run_bass_kernel_spmd

    nc = bacc.Bacc("TRN2", target_bir_lowering=False, num_devices=1)
    arrays, ins = {}, {}
    for name, a in inputs.items():
        if 0 in a.shape:
            continue
        arrays[name] = np.ascontiguousarray(a)
        ins[name] = nc.dram_tensor(name, a.shape, F32, kind="ExternalInput").ap()
    arrays["shape_constants"] = CONSTS
    consts = nc.dram_tensor("shape_constants", CONSTS.shape, F32, kind="ExternalInput").ap()
    out_t = nc.dram_tensor("out", (1, T, D), F32, kind="ExternalOutput").ap()
    out = out_t.rearrange("b (i p) d -> p (b i) d", p=P)
    scratch = {n: nc.dram_tensor(n, sh, F32).ap() for n, sh in SCRATCH}
    program(nc, ins, consts, out, scratch)
    r = run_bass_kernel_spmd(nc, [arrays], core_ids=[0])
    return r.results[0]["out"]
```

```python
from contextlib import ExitStack

import concourse.bass as bass
from concourse import mybir
import numpy as np

ALU = mybir.AluOpType
ACT = mybir.ActivationFunctionType
AX = mybir.AxisListType
F32 = mybir.dt.float32
F32R = mybir.dt.float32r

P = 128
T = 1024
D = 1024
KD = D // P
NT = T // P
META = 16
T2 = T + META
H = 8
N = 64
C1 = 64
NC1 = T // C1
PAIRS = H // 2
DR = H * N
F1 = 2816
CONVW = 31
RMS_EPS = 1e-6

PARAMS = [("mu_first", 12), ("decay_w0", 4), ("iclr_a0", 4), ("k_k", 4), ("k_a", 4), ("r_k", 4),
          ("lnx_g", 4), ("lnx_b", 4), ("cconv_b", 4), ("cln_g", 4), ("cln_b", 4),
          ("lb_logits_2", 16), ("b_f_2", 8), ("head_norm_g_2", 4), ("pool_scale_2", 4), ("ffn_conv_b", 44),
          ("cconv_w", 124),
          ("ffn_conv_w", 132),
          ("conv_w_2", 66), ("conv_b_2", 22)]


def param_rows():
    pieces, first, row = [], {}, 0
    for name, rows in PARAMS:
        first[name] = row
        done = 0
        while done < rows:
            k = min(rows - done, P - row % P)
            pieces.append((name, done, k, row // P, row % P))
            row += k
            done += k
    return pieces, first, row


PIECES, FIRST, ROWS = param_rows()
ROW_TILES = -(-ROWS // P)


def shape_constants():
    p, out = np.arange(P), {}
    out["ident"] = np.eye(P)
    out["head_ones"] = (p[:, None] // N == p[None, :] // N).astype(float)
    out["head_sel"] = (p[:, None] // N == np.arange(2)[None, :]).astype(float)
    s, t = (p % C1)[:, None], np.arange(C1)[None, :]
    out["eye"] = (s == t).astype(float)
    out["before"] = (s < t).astype(float)
    out["upto"] = (s <= t).astype(float)
    out["levels"] = np.concatenate(
        [((s >> l) + 1 == (t >> l)) & ((s >> l) % 2 == 0) for l in range(6)], axis=1).astype(float)
    s, t = p[:, None], p[None, :]
    out["levels2"] = np.concatenate(
        [s == t] + [((s >> l) + 1 == (t >> l)) & ((s >> l) % 2 == 0) for l in range(7)], axis=1).astype(float)
    out["chunk_run"] = np.broadcast_to((np.arange(T) % C1 != 0).astype(float), (P, T))
    out["tile_run"] = np.broadcast_to((np.arange(T2) % P != 0).astype(float), (P, T2))
    windows = np.array([2, 4, 8, 16])[:, None]
    rate = windows / np.minimum(np.arange(1, 17)[None, :], windows)
    out["pool_rate"] = np.broadcast_to(rate.reshape(1, 64), (P, 64))
    at, first = 0, {}
    for name, a in out.items():
        first[name] = (at, a.shape[1])
        at += a.shape[1]
    return np.ascontiguousarray(np.concatenate(list(out.values()), axis=1).astype(np.float32)), first


CONSTS, CONST_AT = shape_constants()


class Made:

    def __init__(self, sem, names):
        self.sem, self.names, self.turn, self.next = sem, list(names), len(names), 0

    def start(self, eng):
        eng.sem_inc(self.sem, self.turn)

    def skip(self, eng, j, n):
        eng.wait_ge(self.sem, (j + 1) * self.turn + self.next)
        eng.sem_inc(self.sem, n)
        self.next = (self.next + n) % self.turn

    def by(self, instruction, name):
        assert self.names[self.next] == name, (self.names[self.next], name)
        self.next = (self.next + 1) % self.turn
        instruction.then_inc(self.sem, 1)

    def wait(self, eng, j, name, back=0):
        eng.wait_ge(self.sem, (j + 1 - back) * self.turn + self.names.index(name) + 1)


class Scope:

    used = []

    def __init__(self, nc, tag, side="left"):
        self.nc, self.tag, self.side, self.ctx = nc, tag, side, ExitStack()

    def __enter__(self):
        return self

    def __exit__(self, *a):
        return self.ctx.__exit__(*a)

    def sb(self, name, shape, dt=F32):
        return self.ctx.enter_context(self.nc.sbuf_tensor(f"{self.tag}_{name}", shape, dt, side=self.side))

    def ps(self, name, shape, dt=F32):
        return self.ctx.enter_context(self.nc.psum_tensor(f"{self.tag}_{name}", shape, dt))

    def sem(self, name):
        handle = self.nc.alloc_semaphore(f"{self.tag}_{name}")
        self.used.append(handle)
        return handle

    def block(self):
        return self.ctx.enter_context(self.nc.Block())


def clear_semaphores(nc):
    nc.clear_and_free_semaphores(Scope.used)
    Scope.used = []
    nc.all_engine_barrier()


def const_of(consts, name):
    at, n = CONST_AT[name]
    return consts[:, at:at + n]


def load_parameters(nc, ins, consts, table, ident):
    with Scope(nc, "par") as s:
        rows = s.sb("rows", [P, ROW_TILES, P])
        turned = s.ps("turned", [P, ROW_TILES, P])
        landed = s.sem("landed")
        ident_landed = s.sem("ident_landed")
        turned_ready = s.sem("turned_ready")
        block = s.block()

        @block.sync
        def _(sp):
            sp.dma_start(ident[:], const_of(consts, "ident")).then_inc(ident_landed, 16)
            for name, r0, k, tile, at in PIECES:
                v = ins[name]
                letters = "abcd"[:len(v.shape)]
                flat = v.rearrange(f"{' '.join(letters)} -> ({' '.join(letters)})").rearrange("(r p) -> r p", p=P) \
                    if len(v.shape) > 1 else v[0:(v.shape[0] // P) * P].rearrange("(r p) -> r p", p=P)
                sp.dma_start(rows[at:at + k, tile, :], flat[r0:r0 + k, :]).then_inc(landed, 16)

        @block.tensor
        def _(pe):
            pe.wait_ge(ident_landed, 16)
            pe.wait_ge(landed, 16 * len(PIECES))
            for tile in range(ROW_TILES):
                k = min(P, ROWS - tile * P)
                mm = nc.tensor.transpose(turned[:, tile, 0:k], rows[0:k, tile, :], ident[0:k, 0:k])
            mm.then_inc(turned_ready, 1)

        @block.vector
        def _(dve):
            dve.wait_ge(turned_ready, 1)
            nc.vector.tensor_copy(table[:, 0:ROWS], turned[:].rearrange("p a b -> p (a b)")[:, 0:ROWS])


def norm_to_features(nc, tag, x, gain, hi, lo, ident, meta=None, clear=False):
    first_col = META if meta is not None else 0
    with Scope(nc, tag) as s:
        gains = s.sb("gains", [P, D])
        squares = s.sb("squares", [P, D])
        sums = s.sb("sums", [P, NT + 1])
        stds = s.sb("stds", [P, NT + 1])
        rstds = s.sb("rstds", [P, NT + 1])
        eps = s.sb("eps", [P, 1])
        normed = s.sb("normed", [P, 2, D])
        turned = [s.ps(f"turned{i}", [P, KD, P]) for i in range(2)]
        gains_landed = s.sem("gains_landed")
        eps_ready = s.sem("eps_ready")
        sums_ready = s.sem("sums_ready")
        std_ready = s.sem("std_ready")
        rstd_ready = s.sem("rstd_ready")
        normed_ready = s.sem("normed_ready")
        turned_ready = s.sem("turned_ready")
        hi_ready = s.sem("hi_ready")
        lo_ready = s.sem("lo_ready")
        block = s.block()

        @block.sync
        def _(sp):
            sp.dma_start(gains[:], gain.broadcast_to((P, D))).then_inc(gains_landed, 16)

        @block.gpsimd
        def _(pool):
            for i in range(NT if clear else 0):
                pool.wait_ge(normed_ready, i + 1)
                nc.gpsimd.memset(x[:, i, :], 0.0)

        @block.scalar
        def _(act):
            def statistics(n, src, p, col):
                nc.scalar.activation(squares[0:p, :], src, ACT.Square,
                                     accum_out=sums[0:p, col]).then_inc(sums_ready, 1)
                act.wait_ge(sums_ready, n + 1)
                nc.scalar.activation(stds[0:p, col], sums[0:p, col], ACT.Sqrt, scale=1.0 / D,
                                     bias=eps[0:p, :]).then_inc(std_ready, 1)

            def split(n, slot, p, cols):
                act.wait_ge(turned_ready, n + 1)
                nc.scalar.activation(hi[:, :, cols], turned[slot][:, :, 0:p], ACT.Copy).then_inc(hi_ready, 1)

            act.wait_ge(eps_ready, 1)
            statistics(0, x[:, 0, :], P, slice(0, 1))
            statistics(1, x[:, 1, :], P, slice(1, 2))
            with act.Fori(0, NT // 2 - 1) as i:
                for e in range(2):
                    n = 2 * i + e
                    statistics(n + 2, x[:, bass.ds(n + 2, 1), :], P, bass.ds(n + 2, 1))
                    split(n, e, P, bass.ds(n * P + first_col, P))
            if meta is not None:
                statistics(NT, meta[:, :], META, slice(NT, NT + 1))
            split(NT - 2, 0, P, slice((NT - 2) * P + first_col, (NT - 1) * P + first_col))
            split(NT - 1, 1, P, slice((NT - 1) * P + first_col, NT * P + first_col))
            if meta is not None:
                split(NT, 0, META, slice(0, META))

        @block.vector
        def _(dve):
            def normalise(n, src, slot, p, col):
                dve.wait_ge(std_ready, n + 1)
                nc.vector.reciprocal(rstds[0:p, col], stds[0:p, col]).then_inc(rstd_ready, 1)
                dve.wait_ge(rstd_ready, n + 1)
                nc.vector.scalar_tensor_tensor(normed[0:p, slot, :], src, rstds[0:p, col], gains[0:p, :],
                                               ALU.mult, ALU.mult).then_inc(normed_ready, 1)

            def split(n, slot, p, cols):
                dve.wait_ge(hi_ready, n + 1)
                nc.vector.tensor_tensor(lo[:, :, cols], turned[slot][:, :, 0:p], hi[:, :, cols].bitcast(F32),
                                        ALU.subtract).then_inc(lo_ready, 1)

            nc.vector.memset(eps[:], RMS_EPS).then_inc(eps_ready, 1)
            dve.wait_ge(gains_landed, 16)
            normalise(0, x[:, 0, :], 0, P, slice(0, 1))
            normalise(1, x[:, 1, :], 1, P, slice(1, 2))
            with dve.Fori(0, NT // 2 - 1) as i:
                for e in range(2):
                    split(2 * i + e, e, P, bass.ds((2 * i + e) * P + first_col, P))
                    normalise(2 * i + e + 2, x[:, bass.ds(2 * i + e + 2, 1), :], e, P, bass.ds(2 * i + e + 2, 1))
            split(NT - 2, 0, P, slice((NT - 2) * P + first_col, (NT - 1) * P + first_col))
            if meta is not None:
                normalise(NT, meta[:, :], 0, META, slice(NT, NT + 1))
            split(NT - 1, 1, P, slice((NT - 1) * P + first_col, NT * P + first_col))
            if meta is not None:
                split(NT, 0, META, slice(0, META))

        @block.tensor
        def _(pe):
            def turn(n, slot, p):
                pe.wait_ge(normed_ready, n + 1)
                for f in range(KD):
                    mm = nc.tensor.transpose(turned[slot][:, f, 0:p], normed[0:p, slot, f * P:(f + 1) * P],
                                             ident[0:p, 0:p])
                mm.then_inc(turned_ready, 1)

            turn(0, 0, P)
            turn(1, 1, P)
            with pe.Fori(0, NT // 2 - 1) as i:
                for e in range(2):
                    pe.wait_ge(lo_ready, 2 * i + e + 1)
                    turn(2 * i + e + 2, e, P)
            if meta is not None:
                pe.wait_ge(lo_ready, NT - 1)
                turn(NT, 0, META)


class Stream:

    def __init__(self, s):
        self.raw = s.sb("w_raw", [P, 2, KD, P])
        self.hi = s.sb("w_hi", [P, 2, KD, P], F32R)
        self.lo = s.sb("w_lo", [P, 2, KD, P], F32R)
        self.landed = [s.sem(f"w_landed{e}") for e in range(2)]
        self.hi_ready = s.sem("w_hi_ready")
        self.lo_ready = s.sem("w_lo_ready")
        self.product_ready = s.sem("product_ready")
        self.psum_free = s.sem("psum_free")
        self.cleared = s.sem("cleared")

    def load(self, sp, n, slot, src, first=False):
        if not first:
            sp.wait_ge(self.lo_ready, n - 1)
            sp.sem_inc(self.cleared, 1)
        m = src.shape[1]
        sp.dma_start(self.raw[:, slot, :, 0:m], src.rearrange("(k p) m -> p k m", p=P)).then_inc(
            self.landed[slot], 16)

    def split_hi(self, nc, act, n, turn, slot, m=P, first=False):
        act.wait_ge(self.landed[slot], 16 * (turn + 1))
        if not first:
            act.wait_ge(self.product_ready, n - 1)
        nc.scalar.activation(self.hi[:, slot, :, 0:m], self.raw[:, slot, :, 0:m], ACT.Copy).then_inc(
            self.hi_ready, 1)

    def split_lo(self, nc, pool, n, slot, m=P):
        pool.wait_ge(self.hi_ready, n + 1)
        nc.gpsimd.tensor_tensor(self.lo[:, slot, :, 0:m], self.raw[:, slot, :, 0:m],
                                self.hi[:, slot, :, 0:m], ALU.subtract).then_inc(self.lo_ready, 1)

    def product(self, nc, pe, n, slot, m, hi, lo, outs, first=False):
        pe.wait_ge(self.lo_ready, n + 1)
        if not first:
            pe.wait_ge(self.psum_free, n - 1)
        for k in range(KD):
            for part, (w, a) in enumerate(((self.hi, hi), (self.hi, lo), (self.lo, hi))):
                for out, c0, c in outs:
                    mm = nc.tensor.matmul(out, w[:, slot, k, 0:m], a[:, k, c0:c0 + c],
                                          start=k == 0 and part == 0, stop=k == KD - 1 and part == 2)
        mm.then_inc(self.product_ready, 1)


def first_projections(nc, ins, table, col_mu, hi, lo, c, rkv, low):
    w = ins["w_in_first"]
    U = 2 * DR
    GLU = 8
    RKV = 12
    steps = GLU + RKV + 2
    with Scope(nc, "proj1") as s:
        st = Stream(s)
        out = [s.ps(f"out{e}", [P, 2, 512]) for e in range(2)]
        gate = s.sb("gate", [P, T])
        shifted = s.sb("shifted", [P, 2, 1 + T])
        keep = s.sb("keep", [P, 14])
        gate_ready = s.sem("gate_ready")
        shifted_ready = s.sem("shifted_ready")
        prepared = s.sem("prepared")
        block = s.block()
        flat = [o[:].rearrange("p a b -> p (a b)") for o in out]

        def cols(c0, n=P):
            return w[:, bass.ds(c0, n)]

        @block.sync
        def _(sp):
            st.load(sp, 0, 0, w[:, DR:DR + P], first=True)
            st.load(sp, 1, 1, w[:, 0:P], first=True)
            with sp.Fori(1, 4) as i:
                st.load(sp, 2 * i, 0, cols(i * P + DR))
                st.load(sp, 2 * i + 1, 1, cols(i * P))
            with sp.Fori(0, RKV // 2) as i:
                for e in range(2):
                    st.load(sp, 2 * i + e + GLU, e, cols((2 * i + e) * P + U))
            st.load(sp, GLU + RKV, 0, w[:, U + 3 * DR:U + 3 * DR + 64])
            st.load(sp, GLU + RKV + 1, 1, w[:, U + 3 * DR + 64:U + 3 * DR + 160])

        @block.gpsimd
        def _(pool):
            with pool.Fori(0, (steps - 2) // 2) as i:
                for e in range(2):
                    st.split_lo(nc, pool, 2 * i + e, e)
            st.split_lo(nc, pool, steps - 2, 0, 64)
            st.split_lo(nc, pool, steps - 1, 1, 96)

        @block.tensor
        def _(pe):
            def step(n, e, m=P, first=False):
                st.product(nc, pe, n, e, m, hi, lo,
                           [(out[e][0:m, h, :], 512 * h, 512) for h in range(2)], first)

            step(0, 0, first=True)
            step(1, 1, first=True)
            with pe.Fori(1, (steps - 2) // 2) as i:
                step(2 * i, 0)
                step(2 * i + 1, 1)
            step(steps - 2, 0, 64)
            step(steps - 1, 1, 96)

        @block.scalar
        def _(act):
            def shift(n, e, mu, m=P):
                act.wait_ge(st.product_ready, n + 1)
                act.wait_ge(st.psum_free, n - 1)
                nc.scalar.activation(shifted[0:m, e, 1:1 + T], flat[e][0:m, :], ACT.Copy,
                                     scale=mu).then_inc(shifted_ready, 1)

            def glu(i, peeled=False):
                act.wait_ge(st.product_ready, 2 * i + 1)
                if not peeled:
                    act.wait_ge(st.psum_free, 2 * i)
                nc.scalar.activation(gate[:], flat[0][:], ACT.Sigmoid).then_inc(gate_ready, 1)

            st.split_hi(nc, act, 0, 0, 0, first=True)
            st.split_hi(nc, act, 1, 0, 1, first=True)
            glu(0, peeled=True)
            st.split_hi(nc, act, 2, 1, 0)
            st.split_hi(nc, act, 3, 1, 1)
            with act.Fori(1, 4) as i:
                glu(i)
                st.split_hi(nc, act, 2 * i + 2, i + 1, 0)
                st.split_hi(nc, act, 2 * i + 3, i + 1, 1)
            act.wait_ge(prepared, 3)
            with act.Fori(0, RKV // 2 - 1) as i:
                for e in range(2):
                    n = 2 * i + e + GLU
                    shift(n, e, table[:, bass.ds(2 * i + e + FIRST["mu_first"], 1)])
                    st.split_hi(nc, act, n + 2, i + GLU // 2 + 1, e)
            n = GLU + RKV - 2
            for e, m in ((0, 64), (1, 96)):
                mu = FIRST["mu_first"] + RKV - 2 + e
                shift(n + e, e, table[:, mu:mu + 1])
                st.split_hi(nc, act, n + e + 2, n // 2 + 1, e, m)
            shift(n + 2, 0, col_mu[0:64, 0:1], 64)
            shift(n + 3, 1, col_mu[0:96, 1:2], 96)

        @block.vector
        def _(dve):
            def shift(n, e, dst, keep_col, m=P):
                dve.wait_ge(shifted_ready, n - GLU + 1)
                nc.vector.scalar_tensor_tensor(dst, flat[e][0:m, :], keep_col, shifted[0:m, e, 0:T],
                                               ALU.mult, ALU.add).then_inc(st.psum_free, 1)

            nc.vector.tensor_scalar(keep[:, 0:12], table[:, FIRST["mu_first"]:FIRST["mu_first"] + 12],
                                    -1.0, 1.0, ALU.mult, ALU.add).then_inc(prepared, 1)
            nc.vector.tensor_scalar(keep[:, 12:14], col_mu[:, :], -1.0, 1.0, ALU.mult,
                                    ALU.add).then_inc(prepared, 1)
            nc.vector.memset(shifted[:, :, 0:1], 0.0).then_inc(prepared, 1)
            nc.vector.memset(c[:, :, 0:CONVW - 1], 0.0)
            dve.wait_ge(prepared, 3)
            with dve.Fori(0, 4) as i:
                dve.wait_ge(gate_ready, i + 1)
                dve.wait_ge(st.product_ready, 2 * i + 2)
                nc.vector.tensor_tensor(c[:, bass.ds(i, 1), CONVW - 1:CONVW - 1 + T], flat[1][:], gate[:],
                                        ALU.mult).then_inc(st.psum_free, 2)
            with dve.Fori(0, RKV // 2) as i:
                for e in range(2):
                    shift(2 * i + e + GLU, e, rkv[:, bass.ds(2 * i + e, 1), :], keep[:, bass.ds(2 * i + e, 1)])
            shift(GLU + RKV, 0, low[0:64, 0, :], keep[0:64, 12:13], 64)
            shift(GLU + RKV + 1, 1, low[0:96, 1, :], keep[0:96, 13:14], 96)


GN_EPS = 64e-5
HALF_E = float(np.exp(-0.5))
BATCH = 8
LEVELS = 6


def recurrence1(nc, ins, consts, table, ident, c, rkv, low, conv):
    act_names = (["sg", "a", "square", "p", "pinv", "pprev", "kk_std", "v"]
                 + [f"{x}t{b}" for x in "vbk" for b in range(2)]
                 + [f"T{l}{b}" for l in range(1, LEVELS) for b in range(2)]
                 + [x for ch in range(NC1) for x in ((f"G{ch}", f"SP{ch}") if ch else (f"G{ch}",))]
                 + ["y", "y_square", "y_std"])
    taps = iter(range(1, CONVW))
    plan = {}

    def tap_names(at, n):
        plan[at] = [t for _, t in zip(range(n), taps)]
        return [f"tap{t}" for t in plan[at]]

    dve_names = ["kkr", "sg_sum", "before_sum", "kk_floor", "kat", "kf", "bon", "kk_inv",
                 "kk_wide", "tap0"] + tap_names("stats", 2)
    dve_names += ["kk", "at", "rt", "b1", "bt", "kt"]
    for q in range(4):
        dve_names += [f"LB{q}", f"LK{q}"]
    for b in range(2):
        dve_names += [f"XT0{b}"]
    for b in range(2):
        dve_names += [f"X0{b}"]
    for l in range(1, LEVELS):
        for b in range(2):
            dve_names += tap_names(f"level{l}{b}", 2 - b)
            dve_names += ([f"X{l}{b}"] if l < LEVELS - 1 else []) + [f"XT{l}{b}"]
    for ch in range(NC1):
        dve_names += [f"U{ch}", f"S{ch}"] + tap_names(f"chunk{ch}", 1)
    dve_names += ["yc", "y_inv", "y_wide", "yn", "ynorm", "bonus", "ysum", "gated"]
    assert not list(taps)
    pe_names = ["decay", "iclr", "kk_stats", "kk_scale"]
    pe_names += ["vt0", "vt1"]
    for q in range(4):
        pe_names += [f"LB{q}", f"LK{q}"]
    pe_names += ["bt0", "bt1", "kt0", "kt1", "T00", "T01"]
    for l in range(1, LEVELS):
        for b in range(2):
            pe_names += [f"T{l}{b}"]
        for b in range(2):
            pe_names += [f"X{l}{b}"]
    for ch in range(NC1):
        pe_names += [f"G{ch}", f"U{ch}", f"S{ch}", f"Y{ch}"]
    pe_names += ["mean", "y_stats", "y_scale", "bonus", "gate"]
    pool_names = [f"LM{l}{b}" for l in range(LEVELS) for b in range(2)]

    with Scope(nc, "rec1") as s:
        masks = {}
        for name in ("head_ones", "head_sel", "before", "upto", "levels", "eye", "chunk_run"):
            masks[name] = s.sb(name, [P, CONST_AT[name][1]])
        both = s.sb("both", [P, 2, C1])
        ups = s.sb("ups", [P, 3, P])
        cols = s.sb("cols", [P, 4])
        gn_eps = s.sb("gn_eps", [P, 1])

        def wide(name):
            return s.sb(name, [P, T])

        sg, a, p, pinv, kkr, kk, kf, bon, sq, cumt = map(
            wide, ("sg", "a", "p", "pinv", "kkr", "kk", "kf", "bon", "sq", "cumt"))
        ar = s.sb("ar", [P, NC1, 2, C1])
        b_, k_, v_ = map(wide, ("b", "k", "v"))
        vt, bt, kt = (s.sb(n, [P, NC1, C1]) for n in ("vt", "bt", "kt"))
        lb, lk = (s.sb(n, [P, NC1, 2, C1]) for n in ("lb", "lk"))
        lm, tt, xx, xt = (s.sb(n, [P, 2, BATCH, C1]) for n in ("lm", "tt", "xx", "xt"))
        floor, std, inv = (s.sb(n, [P, 2 * NT]) for n in ("floor", "std", "inv"))
        gs, us = (s.sb(n, [P, N]) for n in ("gs", "us"))
        st = s.sb("st", [P, 2, N])
        sp_ = s.sb("sp", [P, N])

        big = s.ps("big", [P, 2, 512])
        big2 = s.ps("big2", [P, 2, 512])
        w = s.ps("w", [P, 4, 512])
        bigf, big2f = (t[:].rearrange("p a b -> p (a b)") for t in (big, big2))
        consts_landed = s.sem("consts_landed")
        ups_landed = s.sem("ups_landed")
        gate_landed = s.sem("gate_landed")
        prepared = s.sem("prepared")
        low_ready = s.sem("low_ready")
        passed = s.sem("passed")
        cleared = s.sem("cleared")
        A = Made(s.sem("scalar_made"), act_names)
        V = Made(s.sem("vector_made"), dve_names)
        M = Made(s.sem("tensor_made"), pe_names)
        G = Made(s.sem("pool_made"), pool_names)
        block = s.block()
        col = lambda name, j: table[:, bass.ds(j + FIRST[name], 1)]
        heads = [slice(0, N), slice(N, P)]

        @block.sync
        def _(sp):
            for name, tile in masks.items():
                sp.dma_start(tile[:], const_of(consts, name)).then_inc(consts_landed, 16)
            with sp.Fori(0, PAIRS) as j:
                for n, (name, p0, k, user, landed) in enumerate((
                        ("decay_up", 0, 32, "decay", ups_landed), ("iclr_up", 32, 32, "iclr", ups_landed),
                        ("gate_up", 0, 96, "gate", gate_landed))):
                    M.wait(sp, j, user, back=1)
                    sp.sem_inc(cleared, 1)
                    sp.dma_start(ups[p0:p0 + k, n, :], ins[name][0, :, bass.ds(j * P, P)]).then_inc(landed, 16)

        @block.gpsimd
        def _(pool):
            G.start(pool)
            pool.wait_ge(consts_landed, 16 * len(masks))
            with pool.Fori(0, PAIRS) as j:
                for l in range(LEVELS):
                    for b in range(2):
                        if l == 0:
                            V.wait(pool, j, f"LB{2 * b + 1}")
                        else:
                            M.wait(pool, j, f"T{l - 1}{b}")
                            if l == 1:
                                V.wait(pool, j, f"XT0{b}")
                        mask = masks["levels"][:, l * C1:(l + 1) * C1].unsqueeze(1).broadcast_to((P, BATCH, C1))
                        G.by(nc.gpsimd.tensor_tensor(lm[:, b], lb[:, b * BATCH:(b + 1) * BATCH, 0, :], mask,
                                                     ALU.mult), f"LM{l}{b}")

        @block.scalar
        def _(act):
            A.start(act)
            act.wait_ge(consts_landed, 16 * len(masks))
            nc.scalar.activation(low[0:32, 0, :], low[0:32, 0, :], ACT.Tanh).then_inc(low_ready, 1)
            nc.scalar.activation(low[0:96, 1, :], low[0:96, 1, :], ACT.Sigmoid).then_inc(low_ready, 1)
            act.wait_ge(prepared, 4)
            with act.Fori(0, PAIRS) as j:
                M.wait(act, j, "decay")
                A.by(nc.scalar.activation(sg[:], bigf, ACT.Sigmoid, bias=col("decay_w0", j)), "sg")
                M.wait(act, j, "iclr")
                A.by(nc.scalar.activation(a[:], big2f, ACT.Sigmoid, bias=col("iclr_a0", j)), "a")
                V.wait(act, j, "kkr")
                A.by(nc.scalar.activation(sq[:], kkr[:], ACT.Square), "square")
                V.wait(act, j, "before_sum")
                A.by(nc.scalar.activation(p[:], cumt[:], ACT.Exp, scale=-HALF_E), "p")
                A.by(nc.scalar.activation(pinv[:], cumt[:], ACT.Exp, scale=HALF_E), "pinv")
                A.by(nc.scalar.activation(sg[:], sg[:], ACT.Exp, scale=-HALF_E), "pprev")
                V.wait(act, j, "kk_floor")
                A.by(nc.scalar.activation(std[:], floor[:], ACT.Sqrt), "kk_std")
                A.by(nc.scalar.activation(v_[:], rkv[:, bass.ds(j + 8, 1), :], ACT.Copy), "v")
                for x, dst, bank in (("v", vt, big2), ("b", bt, big), ("k", kt, big2)):
                    for b in range(2):
                        M.wait(act, j, f"{x}t{b}")
                        A.by(nc.scalar.activation(dst[:, b * BATCH:(b + 1) * BATCH, :],
                                                  bank[:, b, :].rearrange("p (c n) -> p c n", n=N), ACT.Copy), f"{x}t{b}")
                for l in range(1, LEVELS):
                    for b in range(2):
                        M.wait(act, j, f"T{l}{b}")
                        A.by(nc.scalar.activation(tt[:, b], w[:, b, :].rearrange("p (c n) -> p c n", n=C1), ACT.Copy),
                             f"T{l}{b}")
                for ch in range(NC1):
                    M.wait(act, j, f"G{ch}")
                    A.by(nc.scalar.activation(gs[:], w[:, 0, 0:N], ACT.Copy), f"G{ch}")
                    if ch:
                        V.wait(act, j, f"S{ch - 1}")
                        A.by(nc.scalar.activation(sp_[:], st[:, ch % 2, :], ACT.Copy,
                                                  scale=p[:, ch * C1 + C1 - 1:ch * C1 + C1]), f"SP{ch}")
                M.wait(act, j, f"Y{NC1 - 1}")
                A.by(nc.scalar.activation(kk[:], big2f, ACT.Copy), "y")
                V.wait(act, j, "yc")
                A.by(nc.scalar.activation(sq[:], kk[:], ACT.Square), "y_square")
                M.wait(act, j, "y_stats")
                A.by(nc.scalar.activation(std[:], w[:, 3, 0:2 * NT], ACT.Sqrt, scale=1.0 / N,
                                          bias=gn_eps[:]), "y_std")

        @block.vector
        def _(dve):
            vec = nc.vector

            def conv_taps(j, at):
                for t in plan[at]:
                    V.wait(dve, j, f"tap{t - 1}")
                    V.by(vec.scalar_tensor_tensor(conv[:, bass.ds(j, 1), :], c[:, bass.ds(j, 1), t:t + T],
                                                  table[:, bass.ds(j + (FIRST["cconv_w"] + 4 * t), 1)],
                                                  conv[:, bass.ds(j, 1), :], ALU.mult, ALU.add), f"tap{t}")

            V.start(dve)
            dve.wait_ge(consts_landed, 16 * len(masks))
            vec.memset(gn_eps[:], GN_EPS).then_inc(prepared, 1)
            vec.tensor_scalar(cols[:], table[:, FIRST["k_a"]:FIRST["k_a"] + 4], -1.0, 1.0, ALU.mult,
                              ALU.add).then_inc(prepared, 1)
            vec.tensor_copy(both[:, 0, :], masks["before"][:]).then_inc(prepared, 1)
            vec.tensor_copy(both[:, 1, :], masks["upto"][:]).then_inc(prepared, 1)
            dve.wait_ge(prepared, 4)
            with dve.Fori(0, PAIRS) as j:
                r, k, v = (rkv[:, bass.ds(j + 4 * n, 1), :] for n in range(3))
                V.by(vec.tensor_scalar(kkr[:], k, col("k_k", j), None, ALU.mult), "kkr")
                A.wait(dve, j, "sg")
                V.by(vec.tensor_tensor_scan(cumt[:], masks["chunk_run"][:], sg[:], 0.0, ALU.mult, ALU.add), "sg_sum")
                V.wait(dve, j, "sg_sum")
                V.by(vec.tensor_tensor(sg[:], cumt[:], sg[:], ALU.subtract), "before_sum")
                M.wait(dve, j, "kk_stats")
                V.by(vec.tensor_scalar(floor[:], w[:, 0, 0:2 * NT], 1e-24, None, ALU.max), "kk_floor")
                A.wait(dve, j, "a")
                V.by(vec.tensor_scalar(kf[:], a[:], col("k_a", j), cols[:, bass.ds(j, 1)], ALU.mult, ALU.add), "kat")
                V.wait(dve, j, "kat")
                V.by(vec.tensor_tensor(kf[:], k, kf[:], ALU.mult), "kf")
                V.wait(dve, j, "kf")
                V.by(vec.scalar_tensor_tensor(bon[:], r, col("r_k", j), kf[:], ALU.mult, ALU.mult), "bon")
                A.wait(dve, j, "kk_std")
                V.by(vec.reciprocal(inv[:], std[:]), "kk_inv")
                V.wait(dve, j, "kk_inv")
                wide_inv = inv[:].unsqueeze(2).broadcast_to((P, 2 * NT, N))
                V.by(vec.tensor_copy(kk[:].rearrange("p (a n) -> p a n", n=N), wide_inv), "kk_wide")
                V.by(vec.tensor_scalar(conv[:, bass.ds(j, 1), :], c[:, bass.ds(j, 1), 0:T],
                                       table[:, bass.ds(j + FIRST["cconv_w"], 1)], col("cconv_b", j),
                                       ALU.mult, ALU.add), "tap0")
                conv_taps(j, "stats")
                M.wait(dve, j, "kk_scale")
                V.by(vec.tensor_tensor(kk[:], bigf, kkr[:], ALU.mult), "kk")
                A.wait(dve, j, "pprev")
                V.wait(dve, j, "kk")
                chunks = lambda t: t.rearrange("p (c n) -> p c n", n=C1)
                V.by(vec.scalar_tensor_tensor(ar[:, :, 0, :], chunks(kk[:]), -1.0, chunks(sg[:]),
                                              ALU.mult, ALU.mult), "at")
                V.by(vec.tensor_tensor(ar[:, :, 1, :], r.rearrange("p a (c n) -> p (a c) n", n=C1), chunks(p[:]),
                                       ALU.mult), "rt")
                V.by(vec.tensor_tensor(kk[:], kk[:], a[:], ALU.mult), "b1")
                V.wait(dve, j, "b1")
                V.by(vec.tensor_tensor(b_[:], kk[:], pinv[:], ALU.mult), "bt")
                V.by(vec.tensor_tensor(k_[:], kf[:], pinv[:], ALU.mult), "kt")
                mask = both[:].unsqueeze(1).broadcast_to((P, 4, 2, C1))
                for q in range(4):
                    for name, dst, bank in (("LB", lb, q % 2), ("LK", lk, 2 + q % 2)):
                        M.wait(dve, j, f"{name}{q}")
                        V.by(vec.tensor_tensor(dst[:, 4 * q:4 * q + 4], w[:, bank, :].rearrange(
                            "p (c x n) -> p c x n", x=2, n=C1), mask, ALU.mult), f"{name}{q}")
                eye = masks["eye"][:].unsqueeze(1).broadcast_to((P, BATCH, C1))
                for b in range(2):
                    G.wait(dve, j, f"LM0{b}")
                    V.by(vec.tensor_tensor(xt[:, b], lm[:, b], eye, ALU.add), f"XT0{b}")
                bank = lambda t: t.rearrange("p (c n) -> p c n", n=C1)
                for b in range(2):
                    M.wait(dve, j, f"T0{b}")
                    V.by(vec.tensor_tensor(xx[:, b], bank(w[:, b, :]), eye, ALU.add), f"X0{b}")
                for l in range(1, LEVELS):
                    for b in range(2):
                        conv_taps(j, f"level{l}{b}")
                        M.wait(dve, j, f"X{l}{b}")
                        if l < LEVELS - 1:
                            V.by(vec.tensor_tensor(xx[:, b], bank(w[:, 2 + b, :]), xx[:, b], ALU.add), f"X{l}{b}")
                        V.by(vec.tensor_tensor(xt[:, b], bank(big[:, b, :]), xt[:, b], ALU.add), f"XT{l}{b}")
                for ch in range(NC1):
                    M.wait(dve, j, f"U{ch}")
                    V.by(vec.tensor_copy(us[:], w[:, 1, 0:N]), f"U{ch}")
                    M.wait(dve, j, f"S{ch}")
                    decay = p[:, ch * C1 + C1 - 1:ch * C1 + C1]
                    if ch:
                        A.wait(dve, j, f"SP{ch}")
                        V.by(vec.scalar_tensor_tensor(st[:, (ch + 1) % 2, :], w[:, 2, 0:N], decay, sp_[:],
                                                      ALU.mult, ALU.add), f"S{ch}")
                    else:
                        V.by(vec.tensor_scalar(st[:, 1, :], w[:, 2, 0:N], decay, None, ALU.mult), f"S{ch}")
                    conv_taps(j, f"chunk{ch}")
                M.wait(dve, j, "mean")
                V.by(vec.scalar_tensor_tensor(kk[:], bigf, -1.0 / N, kk[:], ALU.mult, ALU.add), "yc")
                A.wait(dve, j, "y_std")
                V.by(vec.reciprocal(inv[:], std[:]), "y_inv")
                V.wait(dve, j, "y_inv")
                V.by(vec.tensor_copy(a[:].rearrange("p (a n) -> p a n", n=N), wide_inv), "y_wide")
                M.wait(dve, j, "y_scale")
                V.by(vec.tensor_tensor(kk[:], bigf, kk[:], ALU.mult), "yn")
                V.wait(dve, j, "yn")
                V.by(vec.tensor_scalar(kk[:], kk[:], col("lnx_g", j), col("lnx_b", j), ALU.mult, ALU.add), "ynorm")
                M.wait(dve, j, "bonus")
                V.by(vec.tensor_tensor(kf[:], big2f, v_[:], ALU.mult), "bonus")
                V.wait(dve, j, "bonus")
                V.by(vec.tensor_tensor(kk[:], kk[:], kf[:], ALU.add), "ysum")
                M.wait(dve, j, "gate")
                V.wait(dve, j, "ysum")
                V.by(vec.tensor_tensor(r, w[:, 0:2, :].rearrange("p a b -> p (a b)").unsqueeze(1), kk[:].unsqueeze(1), ALU.mult), "gated")

        @block.tensor
        def _(pe):
            mm = nc.tensor.matmul

            def broad(out, lhs, rhs, p0=0, k=P):
                for h in range(2):
                    last = mm(out[:, h, :], lhs, rhs[p0:p0 + k, 512 * h:512 * h + 512], start=True, stop=True)
                return last

            def per_head(out, lhs, rhs, start=True, stop=True):
                for h in heads:
                    last = mm(out[h], lhs[h], rhs[h], start=start, stop=stop, skip_group_check=True)
                return last

            def stats():
                for i in range(NT):
                    last = mm(w[:, stats_bank, 2 * i:2 * i + 2], sq[:, i * P:(i + 1) * P], masks["head_sel"][:],
                              start=True, stop=True)
                return last

            def scales(src):
                for i in range(NT):
                    last = mm(bigf[:, i * P:(i + 1) * P], src[:, i * P:(i + 1) * P], ident[:], start=True, stop=True)
                return last

            def at(t, ch):
                return t[:, ch * C1:(ch + 1) * C1]

            def need(made, name, back=0):
                made.wait(pe, j, name, back)
                pe.sem_inc(passed, 1)

            M.start(pe)
            pe.wait_ge(consts_landed, 16 * len(masks))
            pe.wait_ge(low_ready, 2)
            with pe.Fori(0, PAIRS) as j:
                pe.wait_ge(ups_landed, 32 * (j + 1))
                need(V, "yn", back=1)
                M.by(broad(big, ups[0:32, 0, :], low[:, 0, :], 0, 32), "decay")
                need(V, "bonus", back=1)
                M.by(broad(big2, ups[32:64, 1, :], low[:, 0, :], 32, 32), "iclr")
                need(V, "gated", back=1)
                need(A, "square")
                stats_bank = 0
                M.by(stats(), "kk_stats")
                need(V, "kk_wide")
                M.by(scales(kk), "kk_scale")
                need(A, "v")

                def turn(x, src, bank):
                    for b in range(2):
                        for i in range(BATCH):
                            ch = b * BATCH + i
                            for h in heads:
                                last = mm(bank[h, b, i * N:(i + 1) * N], src[h, ch * C1:(ch + 1) * C1],
                                          ident[h, h], start=True, stop=True, skip_group_check=True)
                        M.by(last, f"{x}t{b}")

                turn("v", v_, big2)
                need(V, "kt")
                for q in range(4):
                    for name, src, bank in (("LB", b_, q % 2), ("LK", k_, 2 + q % 2)):
                        if q >= 2:
                            need(V, f"{name}{q - 2}")
                        for i in range(4):
                            ch = 4 * q + i
                            for h in heads:
                                last = mm(w[h, bank, i * P:(i + 1) * P], src[h, ch * C1:(ch + 1) * C1],
                                          ar[h, ch, :, :], start=True, stop=True, skip_group_check=True)
                        M.by(last, f"{name}{q}")
                turn("b", b_, big)
                need(A, "vt1")
                turn("k", k_, big2)
                for b in range(2):
                    need(G, f"LM0{b}")
                    need(V, f"LB{2 + b}")
                    for i in range(BATCH):
                        last = per_head(w[:, b, i * C1:(i + 1) * C1], lm[:, b, i, :], masks["eye"])
                    M.by(last, f"T0{b}")
                need(V, "LK3")
                need(A, "bt1")
                for l in range(1, LEVELS):
                    for b in range(2):
                        need(G, f"LM{l}{b}")
                        need(V, f"X0{b}" if l == 1 else f"XT{l - 1}{b}")
                        for i in range(BATCH):
                            last = per_head(w[:, b, i * C1:(i + 1) * C1], lm[:, b, i, :], xx[:, b, i, :])
                        M.by(last, f"T{l}{b}")
                    for b in range(2):
                        need(A, f"T{l}{b}")
                        for i in range(BATCH):
                            cols_ = slice(i * C1, (i + 1) * C1)
                            if l < LEVELS - 1:
                                per_head(w[:, 2 + b, cols_], xt[:, b, i, :], tt[:, b, i, :])
                            last = per_head(big[:, b, cols_], tt[:, b, i, :], xt[:, b, i, :])
                        M.by(last, f"X{l}{b}")
                need(A, "kt1")
                for ch in range(NC1):
                    old = st[:, ch % 2, :]
                    x_t = xt[:, ch // BATCH, ch % BATCH, :]
                    if ch:
                        need(V, f"S{ch - 1}")
                        for h in heads:
                            mm(w[h, 0, 0:N], ar[h, ch, 0, :], old[h], start=True, stop=False, skip_group_check=True)
                            last = mm(w[h, 0, 0:N], lk[h, ch, 0, :], vt[h, ch, :], start=False, stop=True,
                                      skip_group_check=True)
                    else:
                        need(V, f"XT{LEVELS - 1}1")
                        last = per_head(w[:, 0, 0:N], lk[:, ch, 0, :], vt[:, ch, :])
                    M.by(last, f"G{ch}")
                    need(A, f"G{ch}")
                    M.by(per_head(w[:, 1, 0:N], x_t, gs), f"U{ch}")
                    need(V, f"U{ch}")
                    for h in heads:
                        mm(w[h, 2, 0:N], bt[h, ch, :], us[h], start=True, stop=False, skip_group_check=True)
                        last = mm(w[h, 2, 0:N], kt[h, ch, :], vt[h, ch, :], start=False, stop=True,
                                  skip_group_check=True)
                    M.by(last, f"S{ch}")
                    for h in heads:
                        y = big2[h, ch // BATCH, (ch % BATCH) * C1:(ch % BATCH + 1) * C1]
                        if ch:
                            mm(y, old[h], ar[h, ch, 1, :], start=True, stop=False, skip_group_check=True)
                        mm(y, us[h], lb[h, ch, 1, :], start=ch == 0, stop=False, skip_group_check=True)
                        last = mm(y, vt[h, ch, :], lk[h, ch, 1, :], start=False, stop=True, skip_group_check=True)
                    M.by(last, f"Y{ch}")
                need(A, "y")
                M.by(broad(big, masks["head_ones"][:], kk), "mean")
                need(A, "y_square")
                stats_bank = 3
                M.by(stats(), "y_stats")
                need(V, "y_wide")
                M.by(scales(a), "y_scale")
                M.by(broad(big2, masks["head_ones"][:], bon), "bonus")
                pe.wait_ge(gate_landed, 16 * (j + 1))
                pe.sem_inc(passed, 1)
                M.by(broad(w, ups[0:96, 2, :], low[:, 1, :], 0, 96), "gate")


def conv_norm_and_split(nc, consts, table, ident, conv, rwkv, hi, lo):
    with Scope(nc, "cln") as s:
        ones = s.sb("ones", [P, P])
        square = s.sb("square", [P, 4, T])
        std, inv = (s.sb(n, [P, NT]) for n in ("std", "inv"))
        wide = s.sb("wide", [P, NT, P])
        eps = s.sb("eps", [P, 1])
        mean = s.ps("mean", [P, 2, 512])
        stats = s.ps("stats", [P, 512])
        scale = s.ps("scale", [P, 2, 512])
        prepared = s.sem("prepared")
        mean_ready, centred, squared, stats_ready = (s.sem(n) for n in ("mean_ready", "centred", "squared", "stats_ready"))
        std_ready, inv_ready, wide_ready, scale_ready = (
            s.sem(n) for n in ("std_ready", "inv_ready", "wide_ready", "scale_ready"))
        scaled, active, hi_ready = (s.sem(n) for n in ("scaled", "active", "hi_ready"))
        block = s.block()
        scale_f, mean_f = (t[:].rearrange("p a b -> p (a b)") for t in (scale, mean))

        @block.tensor
        def _(pe):
            pe.wait_ge(prepared, 2)
            for h in range(2):
                for f in range(4):
                    mm = nc.tensor.matmul(mean[:, h, :], ones[:], conv[:, f, 512 * h:512 * h + 512],
                                          start=f == 0, stop=f == 3)
            mm.then_inc(mean_ready, 1)
            pe.wait_ge(squared, 4)
            for i in range(NT):
                for f in range(4):
                    mm = nc.tensor.matmul(stats[:, i:i + 1], square[:, f, i * P:(i + 1) * P], ones[:, 0:1],
                                          start=f == 0, stop=f == 3)
            mm.then_inc(stats_ready, 1)
            pe.wait_ge(wide_ready, 1)
            for i in range(NT):
                mm = nc.tensor.matmul(scale_f[:, i * P:(i + 1) * P], wide[:, i, :], ident[:], start=True, stop=True)
            mm.then_inc(scale_ready, 1)

        @block.vector
        def _(dve):
            vec = nc.vector
            vec.memset(ones[:], 1.0).then_inc(prepared, 1)
            vec.memset(eps[:], 1e-5).then_inc(prepared, 1)
            dve.wait_ge(mean_ready, 1)
            for f in range(4):
                vec.scalar_tensor_tensor(conv[:, f, :], mean_f, -1.0 / DR, conv[:, f, :], ALU.mult,
                                         ALU.add).then_inc(centred, 1)
            dve.wait_ge(std_ready, 1)
            vec.reciprocal(inv[:], std[:]).then_inc(inv_ready, 1)
            dve.wait_ge(inv_ready, 1)
            vec.tensor_copy(wide[:], inv[:].unsqueeze(2).broadcast_to((P, NT, P))).then_inc(wide_ready, 1)
            dve.wait_ge(scale_ready, 1)
            for f in range(4):
                vec.tensor_tensor(conv[:, f, :], scale_f, conv[:, f, :], ALU.mult).then_inc(scaled, 1)
            for f in range(4):
                dve.wait_ge(hi_ready, f + 1)
                vec.tensor_tensor(lo[:, f, :], rwkv[:, f, :], hi[:, f, :].bitcast(F32), ALU.subtract)
            for f in range(4):
                dve.wait_ge(hi_ready, f + 5)
                vec.tensor_tensor(lo[:, 4 + f, :], conv[:, f, :], hi[:, 4 + f, :].bitcast(F32), ALU.subtract)

        @block.scalar
        def _(act):
            for f in range(4):
                act.wait_ge(centred, f + 1)
                nc.scalar.activation(square[:, f, :], conv[:, f, :], ACT.Square).then_inc(squared, 1)
            act.wait_ge(stats_ready, 1)
            nc.scalar.activation(std[:], stats[:, 0:NT], ACT.Sqrt, scale=1.0 / DR, bias=eps[:]).then_inc(std_ready, 1)
            for f in range(4):
                nc.scalar.activation(hi[:, f, :], rwkv[:, f, :], ACT.Copy).then_inc(hi_ready, 1)
            for f in range(4):
                act.wait_ge(scaled, f + 1)
                nc.scalar.activation(conv[:, f, :], conv[:, f, :], ACT.Silu,
                                     scale=table[:, FIRST["cln_g"] + f:FIRST["cln_g"] + f + 1],
                                     bias=table[:, FIRST["cln_b"] + f:FIRST["cln_b"] + f + 1]).then_inc(active, 1)
            for f in range(4):
                act.wait_ge(active, f + 1)
                nc.scalar.activation(hi[:, 4 + f, :], conv[:, f, :], ACT.Copy).then_inc(hi_ready, 1)


def token_projection(nc, tag, w, hi, lo, x, x_src=None, gain=None, x_dst=None, meta=None, meta_src=None):
    c0 = META if meta is not None else 0
    tiles = NT + (meta is not None)
    with Scope(nc, tag) as s:
        raw = s.sb("raw", [P, 2, D])
        w_hi = s.sb("w_hi", [P, KD, D], F32R)
        w_lo = s.sb("w_lo", [P, KD, D], F32R)
        squares = s.sb("squares", [P, D])
        sums, std, inv = (s.sb(n, [P, tiles]) for n in ("sums", "std", "inv"))
        gains = s.sb("gains", [P, D])
        normed = s.sb("normed", [P, 2, D])
        eps = s.sb("eps", [P, 1])
        out = [s.ps(f"out{e}", [P, 2, 512]) for e in range(2)]
        raw_landed = [s.sem(f"raw_landed{e}") for e in range(2)]
        x_landed, gains_landed, hi_ready, lo_ready, eps_ready = (
            s.sem(n) for n in ("x_landed", "gains_landed", "hi_ready", "lo_ready", "eps_ready"))
        product_ready, psum_free, sums_ready, std_ready, inv_ready, normed_ready, x_ready, stored = (
            s.sem(n) for n in ("product_ready", "psum_free", "sums_ready", "std_ready", "inv_ready",
                               "normed_ready", "x_ready", "stored"))
        block = s.block()

        @block.sync
        def _(sp):
            for k in range(KD):
                if k >= 2:
                    sp.wait_ge(lo_ready, k - 1)
                sp.dma_start(raw[:, k % 2, :], w[k * P:(k + 1) * P, :]).then_inc(raw_landed[k % 2], 16)
            if gain is not None:
                sp.dma_start(gains[:], gain.broadcast_to((P, D))).then_inc(gains_landed, 16)
            if x_src is not None:
                sp.dma_start(x[:], x_src).then_inc(x_landed, 16)
            if meta is not None:
                sp.dma_start(meta[:], meta_src).then_inc(x_landed, 16)
            if x_dst is not None:
                for i in range(NT):
                    sp.wait_ge(x_ready, i + 1)
                    sp.dma_start(x_dst[:, i, :], x[:, i, :]).then_inc(stored, 16)
                sp.wait_ge(stored, 16 * NT)

        @block.gpsimd
        def _(pool):
            for k in range(KD):
                pool.wait_ge(hi_ready, k + 1)
                nc.gpsimd.tensor_tensor(w_lo[:, k, :], raw[:, k % 2, :], w_hi[:, k, :], ALU.subtract).then_inc(
                    lo_ready, 1)

        @block.tensor
        def _(pe):
            for i in range(tiles):
                cols = slice(c0 + i * P, c0 + (i + 1) * P) if i < NT else slice(0, META)
                m = P if i < NT else META
                if i >= 2:
                    pe.wait_ge(psum_free, i - 1)
                for k in range(KD):
                    if i == 0:
                        pe.wait_ge(lo_ready, k + 1)
                    for part, (a, b) in enumerate(((hi, w_hi), (lo, w_hi), (hi, w_lo))):
                        for h in range(2):
                            mm = nc.tensor.matmul(out[i % 2][0:m, h, :], a[:, k, cols], b[:, k, 512 * h:512 * h + 512],
                                                  start=k == 0 and part == 0, stop=k == KD - 1 and part == 2)
                mm.then_inc(product_ready, 1)

        @block.scalar
        def _(act):
            for k in range(KD):
                act.wait_ge(raw_landed[k % 2], 16 * (k // 2 + 1))
                nc.scalar.activation(w_hi[:, k, :], raw[:, k % 2, :], ACT.Copy).then_inc(hi_ready, 1)
            if gain is None:
                return
            act.wait_ge(eps_ready, 1)
            for i in range(tiles):
                act.wait_ge(product_ready, i + 1)
                nc.scalar.activation(squares[:], out[i % 2][:].rearrange("p a b -> p (a b)"), ACT.Square,
                                     accum_out=sums[:, i:i + 1]).then_inc(sums_ready, 1)
                act.wait_ge(sums_ready, i + 1)
                nc.scalar.activation(std[:, i:i + 1], sums[:, i:i + 1], ACT.Sqrt, scale=1.0 / D,
                                     bias=eps[:]).then_inc(std_ready, 1)

        @block.vector
        def _(dve):
            vec = nc.vector
            vec.memset(eps[:], RMS_EPS).then_inc(eps_ready, 1)
            if x_src is not None:
                dve.wait_ge(x_landed, 32 if meta is not None else 16)
            if gain is not None:
                dve.wait_ge(gains_landed, 16)
            for i in range(tiles):
                flat = out[i % 2][:].rearrange("p a b -> p (a b)")
                if gain is None:
                    dve.wait_ge(product_ready, i + 1)
                    dst = x[:, i, :] if i < NT else meta[:, :]
                    m = P if i < NT else META
                    vec.tensor_tensor(dst, flat[0:m, :], dst, ALU.add).then_inc(psum_free, 1)
                    continue
                dve.wait_ge(std_ready, i + 1)
                vec.reciprocal(inv[:, i:i + 1], std[:, i:i + 1]).then_inc(inv_ready, 1)
                dve.wait_ge(inv_ready, i + 1)
                vec.scalar_tensor_tensor(normed[:, i % 2, :], flat, inv[:, i:i + 1], gains[:], ALU.mult,
                                         ALU.mult).then_inc(psum_free, 1)
                dve.wait_ge(psum_free, i + 1)
                vec.tensor_tensor(x[:, i, :], normed[:, i % 2, :], x[:, i, :], ALU.add).then_inc(x_ready, 1)


def feed_forward(nc, tag, ins, table, hi, lo, f, second):
    up = ins["w_up_2" if second else "ffn_up"][0]
    down = ins["w_down_2" if second else "ffn_down"][0]
    taps, bias = (FIRST["conv_w_2"], FIRST["conv_b_2"]) if second else (FIRST["ffn_conv_w"], FIRST["ffn_conv_b"])
    wide = F1 // P if second else 2 * F1 // P
    groups = F1 // P // 2
    c0 = META if second else 0
    func = ACT.Silu if second else ACT.Gelu_apprx_tanh
    DOWN = [f"down{t}" for t in range(2 * NT)]
    act_names = ["hi0", "hi1", "hi2", "y0", "hi3", "g0", "y1", "hid_hi0", "dhi", "y2", "g1", "y3", "hid_hi1"]
    if second:
        act_names = [n for n in act_names if n not in ("y1", "y3")]
    pool_names = ["lo0", "lo1", "lo2", "lo3", "dlo"]
    dve_names = []
    for q in range(2):
        for e in range(2):
            if not (second and e):
                dve_names += [f"tapa{2 * q + e}", f"tapb{2 * q + e}"]
                dve_names += [f"past1{q}", f"past0{q}"] if second else []
        dve_names += [f"hid{q}", f"hid_lo{q}"]
    dve_names += DOWN
    pe_names = [f"up{i}" for i in range(4)] + DOWN
    with Scope(nc, tag) as s:
        raw = s.sb("raw", [P, 2, KD, P])
        w_hi, w_lo = (s.sb(n, [P, 2, KD, P], F32R) for n in ("w_hi", "w_lo"))
        d_raw = s.sb("d_raw", [P, 2, D])
        d_hi, d_lo = (s.sb(n, [P, 2, D], F32R) for n in ("d_hi", "d_lo"))
        y = s.sb("y", [P, 2, T])
        hid_hi, hid_lo = (s.sb(n, [P, 2, 2, T], F32R) for n in ("hid_hi", "hid_lo"))
        out = [s.ps(f"out{e}", [P, 2, 512]) for e in range(2)]
        past = s.ps("past", [P, 512])
        acc = s.ps("acc", [P, 3, 512])
        flat = [o[:].rearrange("p a b -> p (a b)") for o in out]
        landed = [s.sem(f"landed{e}") for e in range(2)]
        d_landed, cleared = s.sem("d_landed"), s.sem("cleared")
        A = Made(s.sem("scalar_made"), act_names)
        V = Made(s.sem("vector_made"), dve_names)
        M = Made(s.sem("tensor_made"), pe_names)
        G = Made(s.sem("pool_made"), pool_names)
        block = s.block()

        def turns(eng, turn):
            turn(0, 0, True, False)
            with eng.Fori(0, (groups - 1) // 2) as h:
                turn(2 * h + 1, 1, True, True)
                turn(2 * h + 2, 0, True, True)
            turn(groups, groups % 2, False, True)

        @block.sync
        def _(sp):
            def turn(g, par, has_up, has_down):
                if has_up:
                    for i in range(4):
                        G.wait(sp, g, f"lo{(i - 2) % 4}", back=1 if i < 2 else 0)
                        sp.sem_inc(cleared, 1)
                        c = (2 * g + i // 2) * P + (i % 2) * F1
                        sp.dma_start(raw[:, i % 2], up[:, bass.ds(c, P)].rearrange("(k p) m -> p k m", p=P)).then_inc(
                            landed[i % 2], 16)
                if has_down:
                    G.wait(sp, g, "dlo", back=1)
                    sp.sem_inc(cleared, 1)
                    sp.dma_start(d_raw[:], down[bass.ds((g - 1) * 2 * P, 2 * P), :].rearrange(
                        "(k p) m -> p k m", p=P)).then_inc(d_landed, 16)

            turns(sp, turn)

        @block.gpsimd
        def _(pool):
            def turn(g, par, has_up, has_down):
                if has_up:
                    for i in range(4):
                        A.wait(pool, g, f"hi{i}")
                        G.by(nc.gpsimd.tensor_tensor(w_lo[:, i % 2], raw[:, i % 2], w_hi[:, i % 2], ALU.subtract),
                             f"lo{i}")
                else:
                    G.skip(pool, g, 4)
                if has_down:
                    A.wait(pool, g, "dhi")
                    G.by(nc.gpsimd.tensor_tensor(d_lo[:], d_raw[:], d_hi[:], ALU.subtract), "dlo")
                else:
                    G.skip(pool, g, 1)

            G.start(pool)
            turns(pool, turn)

        @block.tensor
        def _(pe):
            def turn(g, par, has_up, has_down):
                if has_up:
                    for i in range(4):
                        G.wait(pe, g, f"lo{i}")
                        last = f"tapb{(i - 2) % 4}" if not (second and i % 2) else f"hid{((i - 2) % 4) // 2}"
                        if second and i % 2 == 0:
                            last = f"past0{((i - 2) % 4) // 2}"
                        V.wait(pe, g, last, back=1 if i < 2 else 0)
                        A.wait(pe, g, f"y{(i - 2) % 4}" if not (second and i % 2) else "g0", back=1 if i < 2 else 0)
                        outs = [(out[i % 2][:, h, :], c0 + 512 * h, 512) for h in range(2)]
                        if second and i % 2 == 0:
                            outs.append((past[:, 0:2], META - 2, 2))
                        for k in range(KD):
                            for part, (a, b) in enumerate(((w_hi, hi), (w_hi, lo), (w_lo, hi))):
                                for o, first, n in outs:
                                    mm = nc.tensor.matmul(o, a[:, i % 2, k, :], b[:, k, first:first + n],
                                                          start=k == 0 and part == 0, stop=k == KD - 1 and part == 2)
                        M.by(mm, f"up{i}")
                else:
                    M.skip(pe, g, 4)
                if has_down:
                    G.wait(pe, g, "dlo")
                    V.wait(pe, g, DOWN[-1], back=1)
                    for t in range(2 * NT):
                        i, h = t // 2, t % 2
                        if t >= 3:
                            V.wait(pe, g, f"down{t - 3}")
                        for k in range(2):
                            for part, (a, b) in enumerate(((hid_hi, d_hi), (hid_lo, d_hi), (hid_hi, d_lo))):
                                mm = nc.tensor.matmul(acc[:, t % 3, :], a[:, 1 - par, k, i * P:(i + 1) * P],
                                                      b[:, k, 512 * h:512 * h + 512],
                                                      start=k == 0 and part == 0, stop=k == 1 and part == 2)
                        M.by(mm, f"down{t}")
                else:
                    M.skip(pe, g, 2 * NT)

            M.start(pe)
            turns(pe, turn)

        @block.scalar
        def _(act):
            def turn(g, par, has_up, has_down):
                def split(i):
                    act.wait_ge(landed[i % 2], (2 * g + i // 2 + 1) * 16)
                    M.wait(act, g, f"up{(i - 2) % 4}", back=1 if i < 2 else 0)
                    A.by(nc.scalar.activation(w_hi[:, i % 2], raw[:, i % 2], ACT.Copy), f"hi{i}")

                def column(at, i):
                    return table[:, bass.ds(2 * g + (at + i // 2 + (i % 2) * (F1 // P)), 1)]

                def conv_last(i):
                    M.wait(act, g, f"up{i}")
                    A.by(nc.scalar.activation(y[:, i % 2, :], flat[i % 2], ACT.Identity, scale=column(taps + 2 * wide, i),
                                              bias=column(bias, i)), f"y{i}")

                def activate(q):
                    V.wait(act, g, f"past0{q}" if second else f"tapb{2 * q}")
                    A.by(nc.scalar.activation(y[:, 0, :], y[:, 0, :], func), f"g{q}")

                def hidden_hi(q):
                    V.wait(act, g, f"hid{q}")
                    A.by(nc.scalar.activation(hid_hi[:, par, q, :], y[:, 1, :], ACT.Copy), f"hid_hi{q}")

                if has_up:
                    split(0)
                    split(1)
                    M.wait(act, g, "up0")
                    split(2)
                    conv_last(0)
                    split(3)
                    activate(0)
                    if not second:
                        conv_last(1)
                    hidden_hi(0)
                else:
                    A.skip(act, g, act_names.index("dhi"))
                if has_down:
                    act.wait_ge(d_landed, g * 16)
                    M.wait(act, g, DOWN[-1], back=1)
                    A.by(nc.scalar.activation(d_hi[:], d_raw[:], ACT.Copy), "dhi")
                else:
                    A.skip(act, g, 1)
                if has_up:
                    V.wait(act, g, "hid_lo0")
                    conv_last(2)
                    activate(1)
                    if not second:
                        conv_last(3)
                    hidden_hi(1)

            A.start(act)
            turns(act, turn)

        @block.vector
        def _(dve):
            vec = nc.vector

            def turn(g, par, has_up, has_down):
                def column(at, i):
                    return table[:, bass.ds(2 * g + (at + i // 2 + (i % 2) * (F1 // P)), 1)]

                def tap(i, back, at, name):
                    V.by(vec.scalar_tensor_tensor(y[:, i % 2, back:T], flat[i % 2][:, 0:T - back], column(at, i),
                                                  y[:, i % 2, back:T], ALU.mult, ALU.add), name)

                if has_up:
                    for q in range(2):
                        for e in range(2):
                            i = 2 * q + e
                            if second and e:
                                continue
                            A.wait(dve, g, f"y{i}")
                            tap(i, 1, taps + wide, f"tapa{i}")
                            V.wait(dve, g, f"tapa{i}")
                            tap(i, 2, taps, f"tapb{i}")
                            if second:
                                V.wait(dve, g, f"tapb{i}")
                                V.by(vec.scalar_tensor_tensor(y[:, 0, 0:1], past[:, 1:2], column(taps + wide, i),
                                                              y[:, 0, 0:1], ALU.mult, ALU.add), f"past1{q}")
                                V.wait(dve, g, f"past1{q}")
                                V.by(vec.scalar_tensor_tensor(y[:, 0, 0:2], past[:, 0:2], column(taps, i),
                                                              y[:, 0, 0:2], ALU.mult, ALU.add), f"past0{q}")
                        A.wait(dve, g, f"g{q}")
                        if second:
                            M.wait(dve, g, f"up{2 * q + 1}")
                            V.by(vec.tensor_tensor(y[:, 1, :], flat[1], y[:, 0, :], ALU.mult), f"hid{q}")
                        else:
                            V.wait(dve, g, f"tapb{2 * q + 1}")
                            V.by(vec.tensor_tensor(y[:, 1, :], y[:, 1, :], y[:, 0, :], ALU.mult), f"hid{q}")
                        A.wait(dve, g, f"hid_hi{q}")
                        V.by(vec.tensor_tensor(hid_lo[:, par, q, :], y[:, 1, :], hid_hi[:, par, q, :].bitcast(F32),
                                               ALU.subtract), f"hid_lo{q}")
                else:
                    V.skip(dve, g, len(dve_names) - len(DOWN))
                if has_down:
                    for t in range(2 * NT):
                        dst = f[:, t // 2, (t % 2) * 512:(t % 2) * 512 + 512]
                        M.wait(dve, g, f"down{t}")
                        V.by(vec.tensor_tensor(dst, acc[:, t % 3, :], dst, ALU.add), f"down{t}")
                else:
                    V.skip(dve, g, len(DOWN))

            V.start(dve)
            turns(dve, turn)


def post_norm(nc, tag, f, gain, x_src, out):
    with Scope(nc, tag) as s:
        gains = s.sb("gains", [P, D])
        xs = s.sb("xs", [P, NT, D]) if x_src is not None else None
        squares = s.sb("squares", [P, D])
        sums, std, inv = (s.sb(n, [P, NT]) for n in ("sums", "std", "inv"))
        eps = s.sb("eps", [P, 1])
        gains_landed, x_landed, eps_ready, sums_ready, std_ready, inv_ready, normed_ready, stored = (
            s.sem(n) for n in ("gains_landed", "x_landed", "eps_ready", "sums_ready", "std_ready", "inv_ready",
                               "normed_ready", "stored"))
        out_ready = s.sem("out_ready") if x_src is not None else normed_ready
        block = s.block()

        @block.sync
        def _(sp):
            sp.dma_start(gains[:], gain.broadcast_to((P, D))).then_inc(gains_landed, 16)
            if x_src is not None:
                sp.dma_start(xs[:], x_src).then_inc(x_landed, 16)
            for i in range(NT):
                sp.wait_ge(out_ready, i + 1)
                sp.dma_start(out[:, i, :], f[:, i, :]).then_inc(stored, 16)
            sp.wait_ge(stored, 16 * NT)

        @block.scalar
        def _(act):
            act.wait_ge(eps_ready, 1)
            for i in range(NT):
                nc.scalar.activation(squares[:], f[:, i, :], ACT.Square, accum_out=sums[:, i:i + 1]).then_inc(
                    sums_ready, 1)
                act.wait_ge(sums_ready, i + 1)
                nc.scalar.activation(std[:, i:i + 1], sums[:, i:i + 1], ACT.Sqrt, scale=1.0 / D,
                                     bias=eps[:]).then_inc(std_ready, 1)

        @block.gpsimd
        def _(pool):
            if x_src is not None:
                pool.wait_ge(x_landed, 16)
                for i in range(NT):
                    pool.wait_ge(normed_ready, i + 1)
                    nc.gpsimd.tensor_tensor(f[:, i, :], f[:, i, :], xs[:, i, :], ALU.add).then_inc(out_ready, 1)

        @block.vector
        def _(dve):
            nc.vector.memset(eps[:], RMS_EPS).then_inc(eps_ready, 1)
            dve.wait_ge(gains_landed, 16)
            for i in range(NT):
                dve.wait_ge(std_ready, i + 1)
                nc.vector.reciprocal(inv[:, i:i + 1], std[:, i:i + 1]).then_inc(inv_ready, 1)
                dve.wait_ge(inv_ready, i + 1)
                nc.vector.scalar_tensor_tensor(f[:, i, :], f[:, i, :], inv[:, i:i + 1], gains[:], ALU.mult,
                                               ALU.mult).then_inc(normed_ready, 1)


LN_FLOOR = 2.0 ** -63
QS, FS, IS, OS, PS, GS = 0, 8, 16, 20, 24, 28
CHUNKS2 = 44


def second_projections(nc, ins, consts, table, hi, lo, proj, ob):
    w = ins["w_in_2"][0]
    kinds = [(QS, FS, ACT.Silu), (FS, IS, ACT.Sigmoid), (IS, OS, ACT.Copy), (OS, PS, ACT.Silu), (PS, GS, ACT.Copy),
             (GS, CHUNKS2, ACT.Sigmoid)]
    with Scope(nc, "proj2") as s:
        st = Stream(s)
        out = [s.ps(f"out{e}", [P, 2, 512]) for e in range(2)]
        first = [s.ps(f"first{e}", [P, 512]) for e in range(2)]
        ev = s.sb("ev", [P, 2, T2])
        rate = s.sb("rate", [P, 64])
        w_pool = s.sb("w_pool", [P, 4, P])
        pin = s.sb("pin", [P, 4, T2])
        sums = s.sb("sums", [P, T2])
        part = s.sb("part", [P, T2])
        diff = s.sb("diff", [P, 2, T2])
        mapped = s.ps("mapped", [P, 2, 512])
        third = T2 // 3 // 8 * 8 + 8
        pieces = [(0, third, 0), (third, third, 1), (2 * third, T2 - 2 * third, 0)]
        pool_landed, pin_taken, pool_step, diff_ready, mapped_ready, mapped_used = (
            s.sem(n) for n in ("pool_landed", "pin_taken", "pool_step", "diff_ready", "mapped_ready", "mapped_used"))
        stored = [s.sem(f"stored{e}") for e in range(2)]
        evacuated = s.sem("evacuated")
        block = s.block()

        @block.sync
        def _(sp):
            st.load(sp, 0, 0, w[:, 0:P], first=True)
            st.load(sp, 1, 1, w[:, P:2 * P], first=True)
            sp.dma_start(rate[:], const_of(consts, "pool_rate")).then_inc(pool_landed, 16)
            sp.dma_start(w_pool[:], ins["w_pool_2"][0].rearrange("g c d -> c g d")).then_inc(pool_landed, 16)
            with sp.Fori(1, CHUNKS2 // 2) as i:
                for e in range(2):
                    st.load(sp, 2 * i + e, e, w[:, bass.ds((2 * i + e) * P, P)])

        @block.gpsimd
        def _(pool):
            with pool.Fori(0, CHUNKS2 // 2) as i:
                for e in range(2):
                    st.split_lo(nc, pool, 2 * i + e, e)

        @block.tensor
        def _(pe):
            def step(n, e, peeled=False):
                outs = [(out[e][:, h, :], META + 512 * h, 512) for h in range(2)] + [(first[e][:, 0:META], 0, META)]
                st.product(nc, pe, n, e, P, hi, lo, outs, peeled)

            step(0, 0, True)
            step(1, 1, True)
            with pe.Fori(1, GS // 2) as i:
                step(2 * i, 0)
                step(2 * i + 1, 1)
            for g in range(4):
                step(GS + 2 * g, 0)
                step(GS + 2 * g + 1, 1)
                pe.wait_ge(diff_ready, g + 1)
                for n, (c, size, bank) in enumerate(pieces):
                    if g or n == 2:
                        pe.wait_ge(mapped_used, 3 * g + (1 if n == 2 else 0))
                    nc.tensor.matmul(mapped[:, bank, 0:size], w_pool[:, g, :], diff[:, g % 2, c:c + size],
                                     start=True, stop=True).then_inc(mapped_ready, 1)
            with pe.Fori(GS // 2 + 4, CHUNKS2 // 2) as i:
                step(2 * i, 0)
                step(2 * i + 1, 1)

        @block.vector
        def _(dve):
            vec = nc.vector
            count = [0]

            def step(ins_):
                ins_.then_inc(pool_step, 1)
                count[0] += 1
                dve.wait_ge(pool_step, count[0])

            def windows(g):
                p = pin[:, g, :]
                if g:
                    dve.wait_ge(diff_ready, g)
                src, dst, other = p, sums[:], part[:]
                for r in range(g + 1):
                    back = 2 ** r
                    step(vec.tensor_tensor(dst[:, back:T2], src[:, back:T2], src[:, 0:T2 - back], ALU.add))
                    step(vec.tensor_copy(dst[:, 0:back], src[:, 0:back]))
                    src, dst, other = dst, other, dst
                step(vec.tensor_tensor(src[:, 0:16], src[:, 0:16], rate[:, 16 * g:16 * g + 16], ALU.mult))
                if g >= 2:
                    dve.wait_ge(mapped_ready, 3 * (g - 1))
                vec.scalar_tensor_tensor(diff[:, g % 2, :], src, 1.0 / 2 ** (g + 1), p, ALU.mult,
                                         ALU.subtract).then_inc(diff_ready, 1)

            def scaled(g):
                col = FIRST["pool_scale_2"] + g
                for n, (c, size, bank) in enumerate(pieces):
                    dve.wait_ge(mapped_ready, 3 * g + n + 1)
                    vec.tensor_scalar(ob[:, g, c:c + size], mapped[:, bank, 0:size], table[:, col:col + 1], None,
                                      ALU.mult).then_inc(mapped_used, 1)

            dve.wait_ge(pool_landed, 32)
            for g in range(4):
                dve.wait_ge(evacuated, 2 * (PS + g) + 2)
                vec.tensor_copy(pin[:, g, :], ev[:, g % 2, :]).then_inc(pin_taken, 1)
            dve.wait_ge(pin_taken, 4)
            for g in range(4):
                windows(g)
                if g >= 1:
                    scaled(g - 1)
            scaled(3)

        @block.scalar
        def _(act):
            def evacuate(n, i, e, func, peeled=False):
                act.wait_ge(st.product_ready, n + 1)
                if not peeled:
                    act.wait_ge(stored[e], 16 * i)
                bias = {"bias": table[:, bass.ds(n + (FIRST["b_f_2"] - FS), 1)]} if (func, s0) == (ACT.Sigmoid, FS) else {}
                nc.scalar.activation(ev[:, e, META:], out[e][:].rearrange("p a b -> p (a b)"), func,
                                     **bias).then_inc(evacuated, 1)
                nc.scalar.activation(ev[:, e, 0:META], first[e][:, 0:META], func, **bias).then_inc(evacuated, 1)
                act.wait_ge(evacuated, 2 * n + 2)
                act.dma_start(proj[:, bass.ds(n, 1), :], ev[:, e, :]).then_inc(stored[e], 16)
                act.sem_inc(st.psum_free, 1)

            st.split_hi(nc, act, 0, 0, 0, first=True)
            st.split_hi(nc, act, 1, 0, 1, first=True)
            for s0, s1, func in kinds:
                start, end = s0 // 2, s1 // 2
                if s0 == 0:
                    for e in range(2):
                        act.wait_ge(st.product_ready, e + 1)
                        st.split_hi(nc, act, e + 2, 1, e)
                        evacuate(e, 0, e, func, peeled=True)
                    start = 1
                if s1 == CHUNKS2:
                    end -= 1
                    act.wait_ge(pin_taken, 4)
                if s0 == PS:
                    for n in range(PS, GS):
                        st.split_hi(nc, act, n + 2, n // 2 + 1, n % 2)
                        if n >= PS + 2:
                            act.wait_ge(pin_taken, n - PS - 1)
                        evacuate(n, n // 2, n % 2, func)
                    continue
                with act.Fori(start, end) as i:
                    for e in range(2):
                        st.split_hi(nc, act, 2 * i + e + 2, i + 1, e)
                        evacuate(2 * i + e, i, e, func)
            for e in range(2):
                evacuate(CHUNKS2 - 2 + e, CHUNKS2 // 2 - 1, e, ACT.Sigmoid)
            for e in range(2):
                act.wait_ge(stored[e], 16 * (CHUNKS2 // 2))


def recurrence2(nc, ins, consts, table, ident, proj, oa):
    TILES, LV = 9, 7
    FULL = TILES - 1
    tail = T2 - FULL * P
    dve_beside = {0: ["f", "k", "floor"], 1: ["a"], 2: ["qa", "z0s", "z0t"], 8: ["z6s", "z6t", "kl"]}
    dve_beside |= {i: [f"z{i - 2}s", f"z{i - 2}t"] for i in range(3, 8)}
    pool_beside = {1: ["dlast", "d0"]} | {i: [f"d{i - 1}"] for i in range(2, 8)}
    levels = [f"el{l}{x}" for l in range(LV) for x in "st"]
    act_before, act_after = ["log", "ea"] + levels[:6], levels[6:] + ["elast"]
    act_names, dve_names, pe_names, pool_names = [], [], [], []
    for e in range(2):
        nx = 1 - e
        act_names += ([f"vt{b}" for b in range(3)] if e == 0 else []) + [f"{e}kt{b}" for b in range(2)]
        act_names += [f"{nx}{n}" for n in act_before] + [f"{e}o0"] + [f"{nx}{n}" for n in act_after] + [
            f"{e}o1", f"{e}o2"]
        for i in range(TILES):
            dve_names += [f"{e}m{i}"] + ([f"{e}S{i}"] if i < FULL else []) + [f"{nx}{n}" for n in dve_beside[i]]
            pool_names += [f"{e}add{i}"] + [f"{nx}{n}" for n in pool_beside.get(i, [])]
        pe_names += ([f"vt{b}" for b in range(3)] if e == 0 else []) + [f"{e}kt{b}" for b in range(2)] + [f"{e}s0"]
        for i in range(TILES + 1):
            pe_names += ([f"{e}s{i + 1}"] if i < FULL else []) + ([f"{e}o{i - 1}"] if i else []) + (
                [f"{e}S{i}"] if i < FULL else [])
    act_names += ["square", "std", "std_tail"]
    dve_names += ["inv", "inv_tail", "wide", "wide_tail", "scaled", "scaled_tail", "gated"]
    pe_names += ["stats", "scale"]
    with Scope(nc, "rec2") as s:
        masks = s.sb("masks", [P, 8 * P])
        run = s.sb("run", [P, T2])
        head_sel = s.sb("head_sel", [P, 2])
        q, sf, k, ea, qa, kl, d = (s.sb(n, [P, 2, T2]) for n in ("q", "sf", "k", "ea", "qa", "kl", "d"))
        iv, og, a, o = (s.sb(n, [P, T2]) for n in ("iv", "og", "a", "o"))
        z = [s.sb(f"z{e}", [P, LV, T2]) for e in range(2)]
        mk = s.sb("mk", [P, 3, 8, P])
        vt = s.sb("vt", [P, TILES, P])
        kt = s.sb("kt", [P, FULL, P])
        S = s.sb("S", [P, 2, N])
        sq = s.sb("sq", [P, T2])
        std, inv = (s.sb(n, [P, 2 * TILES]) for n in ("std", "inv"))
        eps = s.sb("eps", [P, 1])
        lower = s.sb("lower", [P, 6, 8])
        lb, rest = s.sb("lb", [P, 8]), s.sb("rest", [P, 8])
        wide = s.sb("wide", [P, TILES, P])
        sc = [s.ps(f"sc{i}", [P, 2, 512]) for i in range(2)]
        ob = s.ps("ob", [P, 2, 512])
        upd = s.ps("upd", [P, 512])
        tr = s.ps("tr", [P, 512])
        consts_landed, prepared, cleared, lb_ready, lb_exp, iv_landed, og_landed = (
            s.sem(n) for n in ("consts_landed", "prepared", "cleared", "lb_ready", "lb_exp", "iv_landed", "og_landed"))
        head_landed = [s.sem(f"head_landed{e}") for e in range(2)]
        passed = s.sem("passed")
        A = Made(s.sem("scalar_made"), act_names)
        V = Made(s.sem("vector_made"), dve_names)
        M = Made(s.sem("tensor_made"), pe_names)
        G = Made(s.sem("pool_made"), pool_names)
        block = s.block()

        def halves(t, l, x):
            n = T2 if l < 4 else FULL * P
            return t[:, 0:n].rearrange("p (b h c) -> p b h c", h=2, c=2 ** l)[:, :, 1 if x == "t" else 0, :]

        def size(i):
            return P if i < FULL else tail

        def turns(eng, made, turn):
            if made is not None:
                made.start(eng)
            turn(0, False, True)
            with eng.Fori(1, PAIRS) as t:
                turn(t, True, True)
            turn(PAIRS, True, False)

        @block.sync
        def _(sp):
            for t, name in ((masks, "levels2"), (run, "tile_run"), (head_sel, "head_sel")):
                sp.dma_start(t[:], const_of(consts, name)).then_inc(consts_landed, 16)

            def turn(t, tiles, more):
                def load(e, h):
                    sp.dma_start(sf[:, e, :], proj[:, bass.ds(h + FS, 1), :]).then_inc(head_landed[e], 16)
                    sp.dma_start(q[:, e, :], proj[:, bass.ds(h + QS, 1), :]).then_inc(head_landed[e], 16)

                if tiles:
                    M.wait(sp, t, "vt2", back=1)
                    sp.sem_inc(cleared, 1)
                    sp.dma_start(iv[:], proj[:, bass.ds(t - 1 + IS, 1), :]).then_inc(iv_landed, 16)
                    M.wait(sp, t, "1o8", back=1)
                    sp.sem_inc(cleared, 1)
                    load(1, 2 * t - 1)
                    V.wait(sp, t, "gated", back=1)
                    sp.sem_inc(cleared, 1)
                    sp.dma_start(og[:], proj[:, bass.ds(t - 1 + OS, 1), :]).then_inc(og_landed, 16)
                if more:
                    if tiles:
                        M.wait(sp, t, "0o8")
                        sp.sem_inc(cleared, 1)
                    load(0, 2 * t)

            turns(sp, None, turn)

        @block.gpsimd
        def _(pool):
            def turn(t, tiles, more):
                for e in range(2):
                    nx = 1 - e
                    for i in range(TILES):
                        if tiles:
                            V.wait(pool, t, f"{e}m{i}")
                            n, lv = size(i), 4 if i < FULL else 1
                            m = mk[0:n, i % 3]
                            G.by(nc.gpsimd.tensor_tensor(m[:, 0:lv, 0:n], m[:, 0:lv, 0:n], m[:, 4:4 + lv, 0:n],
                                                         ALU.add), f"{e}add{i}")
                        else:
                            G.skip(pool, t, 1)
                        for name in pool_beside.get(i, []):
                            if (e == 0 and not tiles) or (e == 1 and not more):
                                G.skip(pool, t, 1)
                            elif name == "dlast":
                                V.wait(pool, t, f"{nx}a")
                                at = a[:, 0:FULL * P].rearrange("p (i b) -> p i b", b=P)
                                G.by(nc.gpsimd.tensor_tensor(
                                    kl[:, nx, 0:FULL * P].rearrange("p (i b) -> p i b", b=P),
                                    at[:, :, P - 1:P].broadcast_to((P, FULL, P)), at, ALU.subtract), f"{nx}dlast")
                            else:
                                l = int(name[1:])
                                if l >= 2:
                                    V.wait(pool, t, f"{nx}z{l - 2}t")
                                n = T2 if l < 4 else FULL * P
                                blocks = a[:, 0:n].rearrange("p (b c) -> p b c", c=2 ** (l + 1))
                                ref = blocks[:, :, 2 ** l - 1:2 ** l].broadcast_to((P, n >> (l + 1), 2 ** (l + 1)))
                                G.by(nc.gpsimd.tensor_tensor(
                                    d[:, l % 2, 0:n].rearrange("p (b c) -> p b c", c=2 ** (l + 1)), blocks, ref,
                                    ALU.subtract), f"{nx}d{l}")

            turns(pool, G, turn)

        @block.scalar
        def _(act):
            act.wait_ge(prepared, 4)
            for i in range(2):
                nc.scalar.activation(lower[:, 3 + i, :], lower[:, 1 + i, :], ACT.Exp).then_inc(lb_exp, 1)
            act.wait_ge(lb_ready, 4)

            def turn(t, tiles, more):
                def beside(nx, names, run_):
                    if not run_:
                        A.skip(act, t, len(names))
                        return
                    for name in names:
                        if name == "log":
                            V.wait(act, t, f"{nx}floor")
                            A.by(nc.scalar.activation(ea[:, nx, :], sf[:, nx, :], ACT.Ln), f"{nx}log")
                        elif name == "ea":
                            V.wait(act, t, f"{nx}a")
                            A.by(nc.scalar.activation(ea[:, nx, :], a[:], ACT.Exp), f"{nx}ea")
                        elif name == "elast":
                            last = kl[:, nx, 0:FULL * P]
                            A.by(nc.scalar.activation(last, last, ACT.Exp), f"{nx}elast")
                        else:
                            l, x = int(name[2]), name[3]
                            if x == "s":
                                G.wait(act, t, f"{nx}d{l}")
                            half = halves(d[:, l % 2, :], l, x)
                            A.by(nc.scalar.activation(half, half, ACT.Exp, scale=1.0 if x == "t" else -1.0), f"{nx}{name}")

                for e in range(2):
                    nx = 1 - e
                    run_ = tiles if e == 0 else more
                    if tiles:
                        if e == 0:
                            for b in range(3):
                                n = min(4, TILES - 4 * b)
                                m = P if n == 4 else tail
                                M.wait(act, t, f"vt{b}")
                                A.by(nc.scalar.activation(vt[0:m, 4 * b:4 * b + n, :], tr[0:m, 0:n * P].rearrange(
                                    "p (i b) -> p i b", b=P), ACT.Copy), f"vt{b}")
                        for b in range(2):
                            M.wait(act, t, f"{e}kt{b}")
                            A.by(nc.scalar.activation(kt[:, 4 * b:4 * b + 4, :], tr[:].rearrange(
                                "p (i b) -> p i b", b=P), ACT.Copy), f"{e}kt{b}")
                    else:
                        A.skip(act, t, 5 if e == 0 else 2)

                    def result(b):
                        hp = slice(64 * e, 64 * e + 64)
                        c, n = (512 * b, 512) if b < 2 else (FULL * P, tail)
                        M.wait(act, t, f"{e}o{min(4 * b + 3, FULL)}")
                        A.by(nc.scalar.activation(o[hp, c:c + n], ob[hp, b % 2, 0:n], ACT.Copy), f"{e}o{b}")

                    beside(nx, act_before, run_)
                    result(0) if tiles else A.skip(act, t, 1)
                    beside(nx, act_after, run_)
                    if tiles:
                        result(1)
                        result(2)
                    else:
                        A.skip(act, t, 2)
                if tiles:
                    A.wait(act, t, "1o2")
                    A.by(nc.scalar.activation(sq[:], o[:], ACT.Square), "square")
                    M.wait(act, t, "stats")
                    A.by(nc.scalar.activation(std[:, 0:16], tr[:, 0:16], ACT.Sqrt, scale=1.0 / N, bias=eps[:]), "std")
                    A.by(nc.scalar.activation(std[0:tail, 16:18], tr[0:tail, 16:18], ACT.Sqrt, scale=1.0 / N,
                                              bias=eps[0:tail, :]), "std_tail")
                else:
                    A.skip(act, t, 3)

            turns(act, A, turn)

        @block.vector
        def _(dve):
            vec = nc.vector
            logits = table[:, FIRST["lb_logits_2"]:FIRST["lb_logits_2"] + 16].rearrange("p (r c) -> p r c", r=2)
            vec.tensor_tensor(lower[:, 0, :], logits[:, 0, :], logits[:, 1, :], ALU.max).then_inc(prepared, 1)
            vec.memset(eps[:], RMS_EPS).then_inc(prepared, 1)
            dve.wait_ge(prepared, 2)
            for i in range(2):
                vec.tensor_tensor(lower[:, 1 + i, :], logits[:, i, :], lower[:, 0, :], ALU.subtract).then_inc(prepared, 1)
            dve.wait_ge(lb_exp, 2)
            vec.tensor_tensor(lower[:, 5, :], lower[:, 3, :], lower[:, 4, :], ALU.add).then_inc(lb_ready, 1)
            dve.wait_ge(lb_ready, 1)
            vec.reciprocal(lower[:, 0, :], lower[:, 5, :]).then_inc(lb_ready, 1)
            dve.wait_ge(lb_ready, 2)
            vec.tensor_tensor(lb[:], lower[:, 3, :], lower[:, 0, :], ALU.mult).then_inc(lb_ready, 1)
            dve.wait_ge(lb_ready, 3)
            vec.tensor_scalar(rest[:], lb[:], -1.0, 1.0, ALU.mult, ALU.add).then_inc(lb_ready, 1)
            dve.wait_ge(lb_ready, 4)
            dve.wait_ge(consts_landed, 48)

            def turn(t, tiles, more):
                def beside(e, h, name):
                    col = lambda c: c[:, bass.ds(h, 1)]
                    f = sf[:, e, :]
                    if name == "f":
                        dve.wait_ge(head_landed[e], 32 * (t + 1 - e))
                        ins_ = vec.tensor_scalar(f, f, col(rest), col(lb), ALU.mult, ALU.add)
                    elif name == "k":
                        V.wait(dve, t, f"{e}f")
                        ins_ = vec.tensor_scalar(k[:, e, :], f, -1.0, 1.0, ALU.mult, ALU.add)
                    elif name == "floor":
                        ins_ = vec.tensor_scalar(f, f, LN_FLOOR, None, ALU.max)
                    elif name == "a":
                        A.wait(dve, t, f"{e}log")
                        ins_ = vec.tensor_tensor_scan(a[:], run[:], ea[:, e, :], 0.0, ALU.mult, ALU.add)
                    elif name == "qa":
                        A.wait(dve, t, f"{e}ea")
                        ins_ = vec.tensor_tensor(qa[:, e, :], q[:, e, :], ea[:, e, :], ALU.mult)
                    elif name == "kl":
                        A.wait(dve, t, f"{e}elast")
                        last = kl[:, e, 0:FULL * P]
                        ins_ = vec.tensor_tensor(last, k[:, e, 0:FULL * P], last, ALU.mult)
                    else:
                        l, x = int(name[1]), name[2]
                        src = k if x == "s" else q
                        A.wait(dve, t, f"{e}el{l}{x}")
                        ins_ = vec.tensor_tensor(halves(z[e][:, l, :], l, x), halves(src[:, e, :], l, x),
                                                 halves(d[:, l % 2, :], l, x), ALU.mult)
                    V.by(ins_, f"{e}{name}")

                for e in range(2):
                    nx = 1 - e
                    run_ = tiles if e == 0 else more
                    for i in range(TILES):
                        if tiles:
                            M.wait(dve, t, f"{e}s{i}")
                            if i == 0:
                                M.wait(dve, t, f"{nx}o8", back=1 - e)
                            n, lv = size(i), 8 if i < FULL else 5
                            src = sc[i % 2][:].rearrange("p a (l b) -> p (a l) b", b=P)
                            mask = masks[:].rearrange("p (l b) -> p l b", b=P)
                            V.by(vec.tensor_tensor(mk[0:n, i % 3, 0:lv, 0:n], src[0:n, 0:lv, 0:n], mask[0:n, 0:lv, 0:n],
                                                   ALU.mult), f"{e}m{i}")
                            if i < FULL:
                                M.wait(dve, t, f"{e}S{i}")
                                if i:
                                    last = ea[:, e, i * P + P - 1:i * P + P]
                                    V.wait(dve, t, f"{e}S{i - 1}")
                                    V.by(vec.scalar_tensor_tensor(S[:, (i + 1) % 2, :], S[:, i % 2, :], last,
                                                                  upd[:, 0:N], ALU.mult, ALU.add), f"{e}S{i}")
                                else:
                                    V.by(vec.tensor_copy(S[:, 1, :], upd[:, 0:N]), f"{e}S{i}")
                        else:
                            V.skip(dve, t, 2 if i < FULL else 1)
                        if run_:
                            for name in dve_beside[i]:
                                beside(nx, 2 * t - 1 if nx else 2 * t, name)
                        else:
                            V.skip(dve, t, len(dve_beside[i]))
                if not tiles:
                    V.skip(dve, t, 7)
                    return
                A.wait(dve, t, "std_tail")
                V.by(vec.reciprocal(inv[:, 0:16], std[:, 0:16]), "inv")
                V.by(vec.reciprocal(inv[0:tail, 16:18], std[0:tail, 16:18]), "inv_tail")
                V.wait(dve, t, "inv_tail")
                heads = wide[:].rearrange("p i (h n) -> p (i h) n", n=N)
                for m, c0, c1, name in ((P, 0, 16, "wide"), (tail, 16, 18, "wide_tail")):
                    V.by(vec.tensor_copy(heads[0:m, c0:c1, :],
                                         inv[0:m, c0:c1].unsqueeze(2).broadcast_to((m, c1 - c0, N))), name)
                M.wait(dve, t, "scale")
                hg = table[:, bass.ds(t - 1 + FIRST["head_norm_g_2"], 1)]
                V.by(vec.scalar_tensor_tensor(o[:, 0:FULL * P], sc[0][:].rearrange("p a b -> p (a b)"), hg,
                                              o[:, 0:FULL * P], ALU.mult, ALU.mult), "scaled")
                V.by(vec.scalar_tensor_tensor(o[:, FULL * P:T2], sc[1][:, 0, 0:tail], hg, o[:, FULL * P:T2],
                                              ALU.mult, ALU.mult), "scaled_tail")
                V.wait(dve, t, "scaled_tail")
                dve.wait_ge(og_landed, 16 * t)
                V.by(vec.tensor_tensor(oa[:, bass.ds(t - 1, 1), :], o[:], og[:], ALU.mult), "gated")

            turns(dve, V, turn)

        @block.tensor
        def _(pe):
            mm = nc.tensor.matmul

            def turn(t, tiles, more):
                def need(made, name, back=0):
                    made.wait(pe, t, name, back)
                    pe.sem_inc(passed, 1)

                if not tiles:
                    M.skip(pe, t, len(pe_names))
                    return
                for e in range(2):
                    hp = slice(64 * e, 64 * e + 64)
                    if e == 0:
                        pe.wait_ge(iv_landed, 16 * t)
                        pe.sem_inc(passed, 1)
                        for b in range(3):
                            if b:
                                need(A, f"vt{b - 1}")
                            for i in range(4 * b, min(4 * b + 4, TILES)):
                                last = nc.tensor.transpose(tr[0:size(i), (i % 4) * P:(i % 4) * P + P],
                                                           iv[:, i * P:i * P + size(i)], ident[:])
                            M.by(last, f"vt{b}")
                        need(A, "vt2")
                    need(V, f"{e}kl", back=1 - e)
                    for b in range(2):
                        if b:
                            need(A, f"{e}kt0")
                        for i in range(4 * b, 4 * b + 4):
                            last = nc.tensor.transpose(tr[:, (i % 4) * P:(i % 4) * P + P],
                                                       kl[:, e, i * P:(i + 1) * P], ident[:])
                        M.by(last, f"{e}kt{b}")

                    def scores(i):
                        n = size(i)
                        cols = slice(i * P, i * P + n)
                        if i >= 2:
                            need(V, f"{e}m{i - 2}")
                        elif i == 0 and e == 0:
                            need(V, "scaled_tail", back=1)
                        elif i == 0:
                            need(V, f"0m{FULL}")
                        for l in range(8 if i < FULL else 5):
                            lhs = k[:, e, cols] if l == 0 else z[e][:, l - 1, cols]
                            rhs = q[:, e, cols] if l == 0 else z[e][:, l - 1, cols]
                            last = mm(sc[i % 2][0:n, l // 4, (l % 4) * P:(l % 4) * P + n], lhs, rhs, start=True, stop=True)
                        M.by(last, f"{e}s{i}")

                    def outputs(i):
                        n = size(i)
                        need(G, f"{e}add{i}")
                        if i == FULL:
                            need(A, f"{e}o0")
                        if i == 0 and e == 1:
                            need(A, "0o2")
                        dst = ob[hp, (i // 4) % 2, (i % 4) * P:(i % 4) * P + n]
                        for l in range(4):
                            last = mm(dst, vt[0:n, i, hp], mk[0:n, i % 3, l, 0:n], start=l == 0,
                                      stop=l == 3 and i == 0, skip_group_check=True)
                        if i:
                            need(V, f"{e}S{i - 1}")
                            last = mm(dst, S[:, i % 2, :], qa[:, e, i * P:i * P + n], start=False, stop=True,
                                      skip_group_check=True)
                        M.by(last, f"{e}o{i}")

                    scores(0)
                    for i in range(TILES + 1):
                        if i < FULL:
                            scores(i + 1)
                        if i:
                            outputs(i - 1)
                        if i < FULL:
                            if i == 0:
                                need(A, f"{e}kt1")
                            else:
                                need(V, f"{e}S{i - 1}")
                            M.by(mm(upd[:, 0:N], kt[:, i, :], vt[:, i, hp], start=True, stop=True), f"{e}S{i}")
                need(A, "square")
                for i in range(TILES):
                    n = size(i)
                    last = mm(tr[0:n, 2 * i:2 * i + 2], sq[:, i * P:i * P + n], head_sel[:], start=True, stop=True)
                M.by(last, "stats")
                need(V, "wide_tail")
                for i in range(TILES):
                    n = size(i)
                    dst = sc[i // 8][:].rearrange("p a b -> p (a b)")[:, (i % 8) * P:(i % 8) * P + n]
                    last = mm(dst, wide[0:n, i, :], ident[0:n, 0:n], start=True, stop=True)
                M.by(last, "scale")

            turns(pe, M, turn)


def branches(nc, ins, proj, oa_full, ob_full, mix_hi, mix_lo):
    w = [ins["w_branch_a_2"][0], ins["w_branch_b_2"][0]]
    act_names = ["whi", "hi"]
    dve_names = ["a0", "a1", "b0", "b1", "mix", "lo"]
    with Scope(nc, "branch") as s:
        raw = s.sb("raw", [P, KD, P])
        w_hi, w_lo = (s.sb(n, [P, 2, KD, P], F32R) for n in ("w_hi", "w_lo"))
        gates = s.sb("gates", [P, 2, 2, T2])
        out = [s.ps(f"out{e}", [P, 3, 512]) for e in range(2)]
        landed = [s.sem(f"landed{e}") for e in range(2)]
        cleared, o_hi_ready, o_lo_ready = (s.sem(n) for n in ("cleared", "o_hi_ready", "o_lo_ready"))
        oa, ob = ([s.sb(f"{n}{part}", [P, 4, T2], F32R) for part in ("hi", "lo")] for n in ("oa", "ob"))
        split = [(o[0][:, k, :], o[1][:, k, :], full[:, k, :]) for o, full in ((oa, oa_full), (ob, ob_full))
                 for k in range(4)]
        A = Made(s.sem("scalar_made"), [f"{n}{e}" for e in range(2) for n in act_names])
        V = Made(s.sem("vector_made"), [f"{n}{e}" for e in range(2) for n in dve_names])
        M = Made(s.sem("tensor_made"), [f"{n}{e}" for e in range(2) for n in "ab"])
        G = Made(s.sem("pool_made"), ["wlo0", "wlo1"])
        block = s.block()
        pieces = [(0, META, 2)] + [(META + 512 * h, 512, h) for h in range(2)]

        @block.sync
        def _(sp):
            with sp.Fori(0, KD // 2) as i:
                for e in range(2):
                    G.wait(sp, i, f"wlo{1 - e}", back=1 - e)
                    sp.sem_inc(cleared, 1)
                    for b in range(2):
                        sp.dma_start(raw[:, 4 * b:4 * b + 4, :], w[b][:, bass.ds((2 * i + e) * P, P)].rearrange(
                            "(k p) m -> p k m", p=P)).then_inc(landed[e], 16)
                    V.wait(sp, i, f"lo{e}", back=1)
                    sp.sem_inc(cleared, 1)
                    for b in range(2):
                        sp.dma_start(gates[:, e, b, :], proj[:, bass.ds(2 * i + e + GS + 8 * b, 1), :]).then_inc(
                            landed[e], 16)

        @block.gpsimd
        def _(pool):
            G.start(pool)
            with pool.Fori(0, KD // 2) as i:
                for e in range(2):
                    A.wait(pool, i, f"whi{e}")
                    G.by(nc.gpsimd.tensor_tensor(w_lo[:, e], raw[:], w_hi[:, e], ALU.subtract), f"wlo{e}")

        @block.tensor
        def _(pe):
            M.start(pe)
            pe.wait_ge(o_lo_ready, len(split))
            with pe.Fori(0, KD // 2) as i:
                for e in range(2):
                    G.wait(pe, i, f"wlo{e}")
                    for b, (hi, lo) in enumerate((oa, ob)):
                        V.wait(pe, i, f"{'ab'[b]}1{1 - e}", back=1 - e)
                        for k in range(4):
                            for part, (x, y) in enumerate(((w_hi, hi), (w_hi, lo), (w_lo, hi))):
                                for c, n, bank in pieces:
                                    mm = nc.tensor.matmul(out[b][:, bank, 0:n], x[:, e, 4 * b + k, :], y[:, k, c:c + n],
                                                          start=k == 0 and part == 0, stop=k == 3 and part == 2)
                        M.by(mm, f"{'ab'[b]}{e}")

        @block.scalar
        def _(act):
            A.start(act)
            for hi, _, full in split:
                nc.scalar.activation(hi, full, ACT.Copy).then_inc(o_hi_ready, 1)
            with act.Fori(0, KD // 2) as i:
                for e in range(2):
                    act.wait_ge(landed[e], 64 * (i + 1))
                    M.wait(act, i, f"b{e}", back=1)
                    A.by(nc.scalar.activation(w_hi[:, e], raw[:], ACT.Copy), f"whi{e}")
                    V.wait(act, i, f"mix{e}")
                    A.by(nc.scalar.activation(mix_hi[:, bass.ds(2 * i + e, 1), :], gates[:, e, 0, :], ACT.Copy), f"hi{e}")

        @block.vector
        def _(dve):
            vec = nc.vector
            V.start(dve)
            for n, (hi, lo, full) in enumerate(split):
                dve.wait_ge(o_hi_ready, n + 1)
                vec.tensor_tensor(lo, full, hi.bitcast(F32), ALU.subtract).then_inc(o_lo_ready, 1)
            with dve.Fori(0, KD // 2) as i:
                for e in range(2):
                    for b in range(2):
                        M.wait(dve, i, f"{'ab'[b]}{e}")
                        g = gates[:, e, b, :]
                        V.by(vec.tensor_tensor(g[:, 0:META], out[b][:, 2, 0:META], g[:, 0:META], ALU.mult),
                             f"{'ab'[b]}0{e}")
                        V.by(vec.tensor_tensor(g[:, META:], out[b][:, 0:2, :].rearrange("p a b -> p (a b)"),
                                               g[:, META:], ALU.mult), f"{'ab'[b]}1{e}")
                    V.wait(dve, i, f"b1{e}")
                    V.by(vec.tensor_tensor(gates[:, e, 0, :], gates[:, e, 0, :], gates[:, e, 1, :], ALU.add), f"mix{e}")
                    A.wait(dve, i, f"hi{e}")
                    V.by(vec.tensor_tensor(mix_lo[:, bass.ds(2 * i + e, 1), :], gates[:, e, 0, :],
                                           mix_hi[:, bass.ds(2 * i + e, 1), :].bitcast(F32), ALU.subtract), f"lo{e}")

SCRATCH = [("proj2", (P, CHUNKS2, T2)), ("x_mid", (P, NT, D)), ("x3", (P, NT, D)), ]


def program(nc, ins, consts, out, scratch):
    x_src = ins["x"].rearrange("b (i p) d -> p (b i) d", p=P)
    x_mid = scratch["x_mid"]
    Scope.used = []
    with Scope(nc, "top") as s:
        ident = s.sb("ident", [P, P])
        table = s.sb("table", [P, ROWS])
        load_parameters(nc, ins, consts, table, ident)
        tokens = Scope(nc, "tokens")
        x = first_block(nc, ins, consts, table, ident, x_src, x_mid, scratch, tokens)
        clear_semaphores(nc)
        second_block(nc, ins, consts, table, ident, x, tokens, scratch, out)


def first_block(nc, ins, consts, table, ident, x_src, x_mid, scratch, tokens):
    with Scope(nc, "mixed1", side="right") as r:
        rkv = r.sb("rkv", [P, 12, T])
        with Scope(nc, "mix1") as m:
            col_mu = m.sb("col_mu", [P, 2])
            c = m.sb("c", [P, 4, CONVW - 1 + T])
            low = m.sb("low", [P, 2, T])
            with Scope(nc, "in1") as g:
                x = g.sb("x", [P, NT, D])
                hi = g.sb("hi", [P, KD, T], F32R)
                lo = g.sb("lo", [P, KD, T], F32R)
                load_tokens(nc, ins, x, x_src, col_mu)
                norm_to_features(nc, "norm1", x, ins["norm_pre_mix"], hi, lo, ident)
                first_projections(nc, ins, table, col_mu, hi, lo, c, rkv, low)
            conv = r.sb("conv", [P, 4, T])
            recurrence1(nc, ins, consts, table, ident, c, rkv, low, conv)
        x = tokens.sb("x", [P, NT, D])
        m = Scope(nc, "blk1")
        hi = m.sb("hi", [P, KD, T], F32R)
        lo = m.sb("lo", [P, KD, T], F32R)
        conv_norm_and_split(nc, consts, table, ident, conv, rkv, hi, lo)
    with m:
        token_projection(nc, "wout1", ins["w_out"][0], hi, lo, x, x_src, ins["norm_post_mix"], x_mid)
        norm_to_features(nc, "norm2", x, ins["norm_pre_ffn"], hi, lo, ident, clear=True)
        feed_forward(nc, "ffn1", ins, table, hi, lo, x, False)
        post_norm(nc, "post1", x, ins["norm_post_ffn"], x_mid, scratch["x3"])
    return x


def second_block(nc, ins, consts, table, ident, x, tokens, scratch, out):
    x3 = scratch["x3"]
    proj = scratch["proj2"]
    with Scope(nc, "mixed2", side="right") as r:
        ob = r.sb("ob", [P, 4, T2])
        oa = r.sb("oa", [P, 4, T2])
        with tokens, Scope(nc, "in2") as g:
            meta = g.sb("meta", [META, D])
            copy(nc, "load2", [(meta[:], ins["meta_tokens_2"])])
            hi = g.sb("hi", [P, KD, T2], F32R)
            lo = g.sb("lo", [P, KD, T2], F32R)
            norm_to_features(nc, "norm3", x, ins["norm1_g_2"], hi, lo, ident, meta)
            second_projections(nc, ins, consts, table, hi, lo, proj, ob)
        recurrence2(nc, ins, consts, table, ident, proj, oa)
        m = Scope(nc, "blk2")
        hi = m.sb("hi", [P, KD, T2], F32R)
        lo = m.sb("lo", [P, KD, T2], F32R)
        branches(nc, ins, proj, oa, ob, hi, lo)
    with m:
        x = m.sb("x", [P, NT, D])
        meta = m.sb("meta", [META, D])
        token_projection(nc, "wout2", ins["w_out_2"][0], hi, lo, x, x3, meta=meta, meta_src=ins["meta_tokens_2"])
        norm_to_features(nc, "norm4", x, ins["norm2_g_2"], hi, lo, ident, meta)
        feed_forward(nc, "ffn2", ins, table, hi, lo, x, True)
        post_norm(nc, "post2", x, ins["final_norm_g_2"].rearrange("(a d) -> a d", a=1), None, out)


def load_tokens(nc, ins, x, x_src, col_mu):
    with Scope(nc, "load") as l:
        landed, zeroed = l.sem("landed"), l.sem("zeroed")
        block = l.block()

        @block.vector
        def _(dve):
            nc.vector.memset(col_mu[:], 0.0).then_inc(zeroed, 1)

        @block.sync
        def _(sp):
            sp.dma_start(x[:], x_src).then_inc(landed, 16)
            mu = ins["mu_first"].rearrange("(p a) -> p a", a=1)
            sp.wait_ge(zeroed, 1)
            sp.dma_start(col_mu[0:64, 0:1], mu[3 * DR:3 * DR + 64, :]).then_inc(landed, 16)
            sp.dma_start(col_mu[0:96, 1:2], mu[3 * DR + 64:3 * DR + 160, :]).then_inc(landed, 16)
            sp.wait_ge(landed, 48)


def copy(nc, tag, pairs):
    with Scope(nc, tag) as l:
        landed = l.sem("landed")
        block = l.block()

        @block.sync
        def _(sp):
            for dst, src in pairs:
                sp.dma_start(dst, src).then_inc(landed, 16)
            sp.wait_ge(landed, 16 * len(pairs))


def kernel(**inputs):
    import concourse.bacc as bacc
    from concourse.bass_utils import run_bass_kernel_spmd

    nc = bacc.Bacc("TRN2", target_bir_lowering=False, num_devices=1)
    arrays, ins = {}, {}
    for name, a in inputs.items():
        if 0 in a.shape:
            continue
        arrays[name] = np.ascontiguousarray(a)
        ins[name] = nc.dram_tensor(name, a.shape, F32, kind="ExternalInput").ap()
    arrays["shape_constants"] = CONSTS
    consts = nc.dram_tensor("shape_constants", CONSTS.shape, F32, kind="ExternalInput").ap()
    out_t = nc.dram_tensor("out", (1, T, D), F32, kind="ExternalOutput").ap()
    out = out_t.rearrange("b (i p) d -> p (b i) d", p=P)
    scratch = {n: nc.dram_tensor(n, sh, F32).ap() for n, sh in SCRATCH}
    program(nc, ins, consts, out, scratch)
    r = run_bass_kernel_spmd(nc, [arrays], core_ids=[0])
    return r.results[0]["out"]
```
